# Optimizing a Trainium2 kernel written in Bass

```python
import math
import jax, jax.numpy as jnp
from jax import lax
import numpy as np

D_MODEL = 1024
BATCH = 1
SEQ = 512
DEPTH = 2

HEAD_DIM = 64
N_HEADS = D_MODEL // HEAD_DIM
A_GROUPS = ((128, 1), (512, 4), (2048, 16))
A_HEADS_PER_GROUP = N_HEADS // 4
A_HEADS = A_HEADS_PER_GROUP * len(A_GROUPS)
B_HEADS = N_HEADS - A_HEADS
GRID_W = 64
NA_ROWS_MAX = 8
NA_COLS = 16
NA_QCOLS = 16
T5_BUCKETS = 32
T5_MAX_DIST = 1024
CONV_WIDTH = 31
N_EXPERTS = 16
N_GROUPS = 4
TOP_K = 2
D_EXPERT = 512
ALPHA = (2 * DEPTH) ** 0.25
BETA = (8 * DEPTH) ** -0.25
LN_EPS = 1e-5
NEG = -1e30

kernel_name = "hybrid_dilated_natten_conformer_moe_encoder"

def layer_norm(x, g, b):
    xf = x.astype(jnp.float32)
    mu = xf.mean(-1, keepdims=True)
    var = jnp.square(xf - mu).mean(-1, keepdims=True)
    return ((xf - mu) * lax.rsqrt(var + LN_EPS) * g + b).astype(x.dtype)

def t5_bucket(rel):
    nb = T5_BUCKETS // 2
    max_exact = nb // 2
    ret = jnp.where(rel > 0, nb, 0)
    n = jnp.abs(rel)
    nf = jnp.maximum(n, 1).astype(jnp.float32)
    large = max_exact + (jnp.log(nf / max_exact) / math.log(T5_MAX_DIST / max_exact)
                         * (nb - max_exact)).astype(jnp.int32)
    large = jnp.minimum(large, nb - 1)
    return ret + jnp.where(n < max_exact, n, large)

def dilated_attention(q, k, v, bias_tab, window, dil):
    b, h, s, dh = q.shape
    n_side = window // (2 * dil)
    qb = n_side
    L = s // dil
    nblk = -(-L // qb)
    Lp = nblk * qb

    def strided(t):
        return t.reshape(b, h, L, dil, dh).transpose(0, 1, 3, 2, 4)

    qs = jnp.pad(strided(q), ((0, 0),) * 3 + ((0, Lp - L), (0, 0)))
    qs = qs.reshape(b, h, dil, nblk, qb, dh)
    pad_kv = ((0, 0),) * 3 + ((qb, Lp - L + qb), (0, 0))

    def band(t):
        t = jnp.pad(strided(t), pad_kv).reshape(b, h, dil, nblk + 2, qb, dh)
        return jnp.concatenate([t[:, :, :, :-2], t[:, :, :, 1:-1], t[:, :, :, 2:]], axis=4)

    kb, vb = band(k), band(v)
    rel = jnp.arange(3 * qb)[None, :] - qb - jnp.arange(qb)[:, None]
    band_ok = jnp.abs(rel) <= n_side
    bias = jnp.moveaxis(bias_tab[t5_bucket(rel * dil)], -1, 0)
    kpos = jnp.arange(nblk)[:, None] * qb - qb + jnp.arange(3 * qb)[None, :]
    in_range = (kpos >= 0) & (kpos < L)
    valid = band_ok[None] & in_range[:, None, :]
    logits = jnp.einsum('bhrnqd,bhrnkd->bhrnqk', qs, kb).astype(jnp.float32)
    logits = jnp.where(valid, logits + bias[None, :, None, None], NEG)
    lse = jax.nn.logsumexp(logits, axis=-1)
    p = jnp.exp(logits - lse[..., None]).astype(v.dtype)
    out = jnp.einsum('bhrnqk,bhrnkd->bhrnqd', p, vb)
    out = out.reshape(b, h, dil, Lp, dh)[:, :, :, :L].transpose(0, 1, 3, 2, 4).reshape(b, h, s, dh)
    lse = lse.reshape(b, h, dil, Lp)[:, :, :, :L].transpose(0, 1, 3, 2).reshape(b, h, s)
    return out, lse

def neighborhood_attention(q, k, v, rpb):
    b, h, s, dh = q.shape
    rows = s // GRID_W
    kh = min(NA_ROWS_MAX, rows)
    n_cb = GRID_W // NA_QCOLS
    kspan = NA_QCOLS + NA_COLS
    r = jnp.arange(rows)
    row_idx = jnp.clip(r - kh // 2, 0, rows - kh)[:, None] + jnp.arange(kh)[None, :]
    cb = jnp.arange(n_cb)
    col_idx = (jnp.clip(cb * NA_QCOLS - NA_COLS // 2, 0, GRID_W - kspan)[:, None]
               + jnp.arange(kspan)[None, :])
    qcol = cb[:, None] * NA_QCOLS + jnp.arange(NA_QCOLS)[None, :]
    win0 = jnp.clip(qcol - NA_COLS // 2, 0, GRID_W - NA_COLS)[..., None]
    kc = col_idx[:, None, :]
    col_ok = (kc >= win0) & (kc < win0 + NA_COLS)
    dc = kc - qcol[..., None]
    dr = row_idx - r[:, None]

    def gather(t):
        g = t.reshape(b, h, rows, GRID_W, dh)[:, :, row_idx]
        g = g[:, :, :, :, col_idx]
        return g.transpose(0, 1, 2, 4, 3, 5, 6).reshape(b, h, rows, n_cb, kh * kspan, dh)

    kg, vg = gather(k), gather(v)
    qg = q.reshape(b, h, rows, n_cb, NA_QCOLS, dh)
    bias = rpb[:, (dr + NA_ROWS_MAX - 1)[:, None, None, :, None],
               jnp.clip(dc + NA_COLS - 1, 0, 2 * NA_COLS - 2)[None, :, :, None, :]]
    bias = bias.reshape(h, rows, n_cb, NA_QCOLS, kh * kspan)
    valid = jnp.broadcast_to(col_ok[:, :, None, :], (n_cb, NA_QCOLS, kh, kspan)).reshape(n_cb, NA_QCOLS, kh * kspan)
    logits = jnp.einsum('bhrcqd,bhrckd->bhrcqk', qg, kg).astype(jnp.float32)
    logits = jnp.where(valid, logits + bias[None], NEG)
    p = jax.nn.softmax(logits, axis=-1).astype(v.dtype)
    out = jnp.einsum('bhrcqk,bhrckd->bhrcqd', p, vg)
    return out.reshape(b, h, s, dh)

def attention_mixer(x, w_in, w_out, rel_bias, rpb):
    b, s, _ = x.shape
    da, db = A_HEADS * HEAD_DIM, B_HEADS * HEAD_DIM
    proj = x @ w_in
    qa, ka, va, qn, kn, vn = jnp.split(proj, [da, 2 * da, 3 * da, 3 * da + db, 3 * da + 2 * db], axis=-1)
    scale = HEAD_DIM ** -0.5

    def heads(t):
        return t.reshape(b, s, -1, HEAD_DIM).transpose(0, 2, 1, 3)

    qa, ka, va = heads(qa) * scale, heads(ka), heads(va)
    outs, lses = [], []
    for g, (window, dil) in enumerate(A_GROUPS):
        sl = slice(g * A_HEADS_PER_GROUP, (g + 1) * A_HEADS_PER_GROUP)
        o, l = dilated_attention(qa[:, sl], ka[:, sl], va[:, sl], rel_bias[:, sl], window, dil)
        outs.append(o)
        lses.append(l)
    wts = jax.nn.softmax(jnp.stack(lses), axis=0)
    oa = jnp.concatenate([o * wts[g][..., None].astype(o.dtype) for g, o in enumerate(outs)], axis=1)
    ob = neighborhood_attention(heads(qn) * scale, heads(kn), heads(vn), rpb)
    o = jnp.concatenate([oa, ob], axis=1).transpose(0, 2, 1, 3).reshape(b, s, D_MODEL)
    return o @ w_out

def conv_module(x, w_pw1, b_pw1, w_dw, b_dw, g, bb, w_pw2, b_pw2):
    u = x @ w_pw1 + b_pw1
    a, gate = jnp.split(u, 2, axis=-1)
    u = a * jax.nn.sigmoid(gate)
    u = lax.conv_general_dilated(u, w_dw[:, None, :], window_strides=(1,),
                                 padding=[(CONV_WIDTH // 2, CONV_WIDTH // 2)],
                                 dimension_numbers=('NWC', 'WIO', 'NWC'),
                                 feature_group_count=D_MODEL) + b_dw
    u = jax.nn.silu(layer_norm(u, g, bb))
    return u @ w_pw2 + b_pw2

def moe(x, w_router, router_bias, w_gate, w_up, w_down):
    b, s, d = x.shape
    xt = x.reshape(-1, d)
    scores = jax.nn.sigmoid((xt @ w_router).astype(jnp.float32))
    sel = scores + router_bias.astype(jnp.float32)
    epg = N_EXPERTS // N_GROUPS
    grp = lax.top_k(sel.reshape(-1, N_GROUPS, epg), TOP_K)[0].sum(-1)
    g_idx = jnp.argmax(grp, axis=-1)
    in_grp = (jnp.arange(N_EXPERTS) // epg)[None, :] == g_idx[:, None]
    _, e_idx = lax.top_k(jnp.where(in_grp, sel, NEG), TOP_K)
    w = jnp.take_along_axis(scores, e_idx, axis=-1)
    w = w / w.sum(-1, keepdims=True)
    gates = (jax.nn.one_hot(e_idx, N_EXPERTS, dtype=jnp.float32) * w[..., None]).sum(1).astype(x.dtype)
    y = jnp.zeros_like(xt)
    for e in range(N_EXPERTS):
        hid = jax.nn.silu(xt @ w_gate[e]) * (xt @ w_up[e])
        y = y + gates[:, e:e + 1] * (hid @ w_down[e])
    return y.reshape(b, s, d)

def setup_inputs(seed: int = 0) -> dict:
    key = jax.random.key(seed)
    ks = jax.random.split(key, 24)
    f32 = jnp.float32
    d = D_MODEL
    n_even = (DEPTH + 1) // 2
    n_odd = DEPTH // 2

    def nrm(k, shape, scale):
        return jax.random.normal(k, shape, f32) * scale

    return {
        'x': nrm(ks[0], (BATCH, SEQ, d), 1.0),
        'w_in_attn': nrm(ks[1], (n_even, d, 3 * d), d ** -0.5),
        'w_out_attn': nrm(ks[2], (n_even, d, d), d ** -0.5 * BETA),
        'rel_bias': nrm(ks[3], (T5_BUCKETS, A_HEADS), 0.2),
        'rpb_2d': nrm(ks[4], (n_even, B_HEADS, 2 * NA_ROWS_MAX - 1, 2 * NA_COLS - 1), 0.2),
        'w_pw1': nrm(ks[5], (n_odd, d, 2 * d), d ** -0.5),
        'b_pw1': nrm(ks[6], (n_odd, 2 * d), 0.02),
        'w_dw': nrm(ks[7], (n_odd, CONV_WIDTH, d), CONV_WIDTH ** -0.5),
        'b_dw': nrm(ks[8], (n_odd, d), 0.02),
        'conv_ln_g': 1.0 + nrm(ks[9], (n_odd, d), 0.05),
        'conv_ln_b': nrm(ks[10], (n_odd, d), 0.02),
        'w_pw2': nrm(ks[11], (n_odd, d, d), d ** -0.5 * BETA),
        'b_pw2': nrm(ks[12], (n_odd, d), 0.02),
        'ln_mix_g': 1.0 + nrm(ks[13], (DEPTH, d), 0.05),
        'ln_mix_b': nrm(ks[14], (DEPTH, d), 0.02),
        'ln_ffn_g': 1.0 + nrm(ks[15], (DEPTH, d), 0.05),
        'ln_ffn_b': nrm(ks[16], (DEPTH, d), 0.02),
        'w_router': nrm(ks[17], (d, N_EXPERTS), d ** -0.5),
        'router_bias': nrm(ks[18], (N_EXPERTS,), 0.01),
        'w_gate': nrm(ks[19], (DEPTH, N_EXPERTS, d, D_EXPERT), d ** -0.5),
        'w_up': nrm(ks[20], (DEPTH, N_EXPERTS, d, D_EXPERT), d ** -0.5),
        'w_down': nrm(ks[21], (DEPTH, N_EXPERTS, D_EXPERT, d), D_EXPERT ** -0.5 * BETA),
    }

def reference(x, w_in_attn, w_out_attn, rel_bias, rpb_2d, w_pw1, b_pw1, w_dw, b_dw,
              conv_ln_g, conv_ln_b, w_pw2, b_pw2, ln_mix_g, ln_mix_b, ln_ffn_g, ln_ffn_b,
              w_router, router_bias, w_gate, w_up, w_down):
    for layer in range(DEPTH):
        i = layer // 2
        if layer % 2 == 0:
            m = attention_mixer(x, w_in_attn[i], w_out_attn[i], rel_bias, rpb_2d[i])
        else:
            m = conv_module(x, w_pw1[i], b_pw1[i], w_dw[i], b_dw[i], conv_ln_g[i], conv_ln_b[i],
                            w_pw2[i], b_pw2[i])
        x = layer_norm(ALPHA * x + m, ln_mix_g[layer], ln_mix_b[layer])
        f = moe(x, w_router, router_bias, w_gate[layer], w_up[layer], w_down[layer])
        x = layer_norm(ALPHA * x + f, ln_ffn_g[layer], ln_ffn_b[layer])
    return x


_drawn_inputs = setup_inputs


def setup_inputs(seed=0):
    import zlib

    import numpy as np

    out = dict(_drawn_inputs(seed))
    spreads = {}
    factors = {'rel_bias': 3.398,
     'rpb_2d': 3.16,
     'b_pw1': 8.0,
     'b_dw': 3.338,
     'conv_ln_b': 3.807,
     'b_pw2': 3.007,
     'conv_ln_g': 2.758}
    for name, (base, spread) in spreads.items():
        noise = np.random.default_rng([zlib.crc32(name.encode()), seed]).standard_normal(out[name].shape)
        drawn = base * np.exp(spread * noise) if base else spread * noise
        out[name] = __import__('jax').numpy.asarray(drawn.astype(out[name].dtype))
    for name, factor in factors.items():
        out[name] = (out[name] * factor).astype(out[name].dtype)
    return out
```

```python
import math
from contextlib import ExitStack

import numpy as np
import concourse.bass as bass
from concourse import mybir

F32 = mybir.dt.float32
BF16 = mybir.dt.bfloat16
I32 = mybir.dt.int32
ALU = mybir.AluOpType
ACT = mybir.ActivationFunctionType
X_AXIS = mybir.AxisListType.X

P = 128
D = 1024
SEQ = 512
NT = SEQ // P
KD = D // P
HD = 64
GRID_W = 64
NE = 16
NG = 4
EPG = NE // NG
DE = 512
KE = DE // P
NTAP = 31
PAD = NTAP // 2
ALPHA = 4 ** 0.25
LN_EPS = 1e-5
NEG = -1e30
SCALE = HD ** -0.5
SLOTS = 6
CH = 4096
NOVER = SEQ * 2 // P - 1
W0, W1 = 512, 256
NX = 48
RW = 64


def t5_bucket(rel):
    nb, max_exact = 16, 8
    n = abs(rel)
    big = max_exact + int(math.log(max(n, 1) / max_exact) / math.log(1024 / max_exact) * (nb - max_exact)) \
        if n >= max_exact else n
    return (nb if rel > 0 else 0) + min(big, nb - 1)


def bucket_table():
    t = np.zeros((33, W0 + 2 * W1), np.float32)

    def put(col, rel, ok):
        if ok:
            t[t5_bucket(rel), col] = 1.0
        else:
            t[32, col] = NEG

    for j in range(W0):
        put(j, j - 255, abs(j - 255) <= 64 and j <= 510)
    for j in range(W1):
        d = j - 127
        put(W0 + j, 4 * d, abs(d) <= 64 and j <= 254)
        put(W0 + W1 + j, 4 * d, d % 4 == 0 and j <= 254)
    return t


def window_mask():
    m = np.full((P, 4, NX), NEG, np.float32)
    for q in range(P):
        for b in range(4):
            col = 16 * b + q % 16
            w0 = min(max(col - 8, 0), GRID_W - 16)
            for x in range(NX):
                if w0 <= 16 * (b - 1) + x < w0 + 16:
                    m[q, b, x] = 0.0
    return m


def small_table():
    t = np.zeros((P, 96), np.float32)
    t[:, 0:4] = [4, 3, 2, 1]
    t[:, 4:20] = np.tril(np.ones((4, 4)), -1).ravel()
    t[:, 20:36] = np.arange(NE)
    for tile in range(NT):
        t[:, 36 + 4 * tile] = np.arange(P)
        t[:, 37 + 4 * tile] = P * tile
        t[:, 39 + 4 * tile] = 1.0
    return t


def matrices():
    return np.stack([np.eye(P), np.triu(np.ones((P, P)), 1), np.tile(np.arange(1, P + 1), (P, 1))]).astype(np.float32)


class Chain:

    def __init__(self, eng, sem):
        self.eng, self.sem, self.n, self.shift = eng, sem, 0, None

    def __call__(self, ins):
        self.n += 1
        ins.then_inc(self.sem, 1)
        self.eng.wait_ge(self.sem, self.n if self.shift is None else self.shift + self.n)


def trunk(nc, x, w_in_attn, w_out_attn, rel_bias, rpb_2d, w_pw1, b_pw1, w_dw, b_dw, conv_ln_g,
          conv_ln_b, w_pw2, b_pw2, ln_mix_g, ln_mix_b, ln_ffn_g, ln_ffn_b, w_router, router_bias,
          w_gate, w_up, w_down, c_bucket, c_window, c_small, c_mats, out):
    ctx = ExitStack()
    with ctx:
        def sb(name, shape, dt=F32):
            return ctx.enter_context(nc.sbuf_tensor(name, shape, dt))

        def sem(name):
            return ctx.enter_context(nc.semaphore(name))

        ring = sb("ring", [P, SLOTS, CH])
        x_tok = sb("x_tok", [P, NT, D])
        x_feat = sb("x_feat", [P, KD, SEQ])
        K4 = 1024
        arena = sb("arena", [P, 73 * 256])

        def at(kib, n):
            return arena[:, kib * 256:kib * 256 + n]

        qT = at(0, 4096).rearrange("p (r n) -> p r n", r=8)
        kT = at(16, 4096).rearrange("p (r n) -> p r n", r=8)
        vt = at(32, 4096).rearrange("p (g t n) -> p g t n", g=4, t=NT)
        bias0 = at(48, 4 * 384).rearrange("p (h n) -> p h n", h=4)
        bias12 = at(54, 8 * 128).rearrange("p (h n) -> p h n", h=8)
        bias_n = at(58, 4 * 384).rearrange("p (h n) -> p h n", h=4)
        probs = at(64, 4 * 384).rearrange("p (b n) -> p b n", b=4)
        bias_nr = at(64, 4 * 384).rearrange("p (h n) -> p h n", h=4)
        vgT = at(64, 2 * 512).rearrange("p (b n) -> p b n", b=2)
        probsT = at(70, 2 * 384).rearrange("p (b n) -> p b n", b=2)
        bucket_sb = at(32, 1024)
        rel_rep = at(36, 12 * P).rearrange("p (h n) -> p h n", h=12)
        rpb_row = at(48, 4 * 15 * RW)
        stage = at(64, 3 * 512).rearrange("p (b n) -> p b n", b=3)
        nmax_b = x_feat[:, 0:3, :]
        sums_b = x_feat[:, 3:6, :]
        den_b = x_feat[:, 6, :]
        ln_g = at(16, D)
        ln_b = at(20, D)
        xg = at(24, 2 * D).rearrange("p (b n) -> p b n", b=2)
        xgT = at(32, 2 * D).rearrange("p (b k n) -> p b k n", b=2, k=KD)
        y_sb = at(40, 2 * D).rearrange("p (b n) -> p b n", b=2)
        hid = at(48, DE)
        sig = at(50, DE)
        hidT = at(52, DE).rearrange("p (k n) -> p k n", k=KE)
        picks = at(0, 4096).bitcast(BF16).rearrange("p (t e n) -> p t e n", t=NT, e=NE)
        over_w = at(0, 4096)
        over_picks = at(54, 512).bitcast(BF16).rearrange("p (a t n) -> p a t n", a=2, t=NT)
        yload = at(24, 4 * D).rearrange("p (b k n) -> p b k n", b=2, k=2)
        rsm = at(56, 16 * 256)
        conv_o = at(0, 4096).rearrange("p (c n) -> p c n", c=8)
        NPAD = SEQ + 2 * PAD
        upad = at(24, 2 * 544).rearrange("p (b n) -> p b n", b=2)
        gsig = at(29, 2 * 512).rearrange("p (b n) -> p b n", b=2)
        csq = at(33, 2 * 512).rearrange("p (b n) -> p b n", b=2)
        cmean = at(37, 512)
        crstd = at(39, 512)
        taps = at(41, 8 * 32).rearrange("p (c n) -> p c n", c=8)
        cvec = at(42, 64)
        crow = at(43, 1024)
        vrow = at(47, P)
        ctmp = at(48, 2 * 512).rearrange("p (b n) -> p b n", b=2)
        bpw2 = at(52, D)

        ident = sb("ident", [P, P])
        ones = sb("ones", [P, P])
        mats = sb("mats", [P, 2, P])
        before_bf = sb("before_bf", [P, P], BF16)
        ones_bf = sb("ones_bf", [P, P], BF16)
        slot_bf = sb("slot_bf", [P, P], BF16)
        small = sb("small", [P, 96])
        window = sb("window", [P, 4, NX])
        nmax = sb("nmax", [P, 64])
        psum_e = sb("psum_e", [P, 64])
        rinv = sb("rinv", [P, 64])
        wr = sb("wr", [P, KD, NE])
        rb = sb("rb", [P, NE])
        rel_sb = sb("rel_sb", [33, 12])
        stats = sb("stats", [P, 2, 6])
        mv = sb("mv", [P, 4])

        ps = [ctx.enter_context(nc.psum_tensor(f"ps{i}", [P, 512], F32)) for i in range(8)]

        bias_d0 = nc.dram_tensor("bias_d0", [4, P * W0], F32).ap()
        bias_d12 = nc.dram_tensor("bias_d12", [8, P * W1], F32).ap()
        bias_dn = nc.dram_tensor("bias_dn", [4, P * 15 * RW], F32).ap()
        xs = [nc.dram_tensor(f"xs{n}", [SEQ, D], F32).ap() for n in range(2)]
        Y = [nc.dram_tensor(f"Y{n}", [2 * SEQ, D], F32).ap() for n in range(2)]

        def pk(w):
            return w.rearrange("(p k) n -> p k n", p=P)

        def kp(w):
            return w.rearrange("(k p) n -> p k n", p=P)

        ATT = 0
        MOE = [8, 8 + 48 + 6]
        CONV = 8 + 48


        w_full = [sem(f"w_full{s}") for s in range(SLOTS)]
        w_free = [sem(f"w_free{s}") for s in range(SLOTS)]

        def slot(c, kk=KD):
            return ring[:, c % SLOTS, :].rearrange("p (k n) -> p k n", k=kk)

        def filled(eng, c, i=None):
            v = 16 * (c // SLOTS + 1)
            eng.wait_ge(w_full[c % SLOTS], v if i is None else i * 16 + v)

        S = {n: sem(n) for n in (
            "x_in", "consts", "bucket_in", "rel_in", "rpb_in", "router_in", "preset", "rel_rep", "rpb_zero", "bf_ready",
            "row_mm", "row_cp", "row_out0", "row_out1", "row_out2", "bias_in", "bias_n", "biases_in", "xf0_mm", "xf0_cp",
            "vg_mm", "vg_cp", "proj_mm", "proj_cpA", "proj_cpV", "scores", "sc_read", "nmax", "probs", "pnorm", "pT", "pT_cp",
            "pv", "stat", "evac", "mg_min", "mg_diff", "mg_exp", "mg_den", "mg_inv", "mg_done",
            "dve_chain", "pool_chain", "cvec_in", "cvec_mm", "cvec_cp", "pw1_mm", "gate_sig",
            "u_ready", "conv_done", "csum_mm", "c_dev", "c_sq", "cvar_mm", "c_ve", "c_std",
            "c_z", "c_act", "bpw2_in", "xres", "store_out", "act_chain", "passed")}
        PER_LAYER = {
            "mo_mm": 8, "mo_read": 8, "ln_ve": NT, "ln_std": NT, "ln_done": NT, "xf_mm": 8, "xf_cp": 8, "lnp_in": 32,
            "xs_st": 16 * NT, "lnp2_in": 32, "logit_mm": NT, "score": 1, "mask": 1, "pos_mm": 1, "picks": NT,
            "idx_mm": 1, "idx": 1, "nover": 1, "g_full0": 128, "g_full1": 128, "s_done0": 128, "s_done1": 128,
            "xt_mm": 32, "xt_cpA": 16, "xt_cpV": 16, "gu_mm": 32, "silu": 16, "hid": 16, "ht_mm": 16, "ht_cp": 16,
            "dn_mm": 32, "y_cpA": 16, "y_cpV": 16, "y_in0": 64, "y_in1": 64, "y_used": NT, "ln2_ve": NT,
            "ln2_std": NT, "ln2_done": NT, "xf2_mm": 8, "xf2_cp": 8}
        shared = {n: sem(n) for n in PER_LAYER}
        OWN = ("o_pick", "o_imm", "o_idx", "o_gath", "o_w", "o_mm", "o_tr", "o_silu", "o_cp", "o_scat", "o_chain",
               "o_y", "p_chain")

        class Layer:

            def __init__(self, l):
                self.l = l
                self.own = {n: sem(f"{n}_{l}") for n in OWN}

            def __getitem__(self, name):
                return self.own[name] if name in self.own else shared[name]

            def value(self, name, v):
                return v if name in self.own else v + self.l * PER_LAYER[name]

            def wait(self, eng, name, v, i=None, k=0):
                v = self.value(name, v)
                eng.wait_ge(self[name], v if i is None else i * k + v)

        L = [Layer(l) for l in range(2)]

        class First(Layer):

            def __init__(self):
                self.own = S

        FIRST = First()


        def in_tiles(v, g):
            if g == 0:
                return v
            if g < 3:
                return v.rearrange("p (i t) -> p t i", t=4)
            return v.rearrange("p (r b c) -> p b r c", r=8, c=16)

        def tiles_of(v, g):
            if g == 0:
                return v
            if g < 3:
                return v.rearrange("p (t i) -> p t i", t=4)
            return v.rearrange("p (b r c) -> p b r c", r=8, c=16)

        def tokens(v, g, t):
            return v[:, t * P:(t + 1) * P] if g == 0 else v[:, t::4]

        def key_tiles(g, t):
            return [b for b in (t - 1, t, t + 1) if 0 <= b < NT] if g in (0, 3) else [t]

        def keys(v, g, t):
            b = key_tiles(g, t)
            if g == 0:
                return v[:, b[0] * P:(b[-1] + 1) * P]
            if g == 3:
                return in_tiles(v, g)[:, b[0]:b[-1] + 1]
            return tokens(v, g, t)

        PAIRS = [0, 2, 4, 1, 3, 5, 6, 7]
        UNITS = [(h, t) for pr in PAIRS for h in (2 * pr, 2 * pr + 1) for t in range(NT)]
        LAG_T, LAG_V = 2, 3
        NU = len(UNITS)
        NA = 48

        def group(h):
            return h // 4

        ITEMS = []
        for c, cols in enumerate([[("q", p) for p in range(4)], [("q", 4), ("q", 5), ("k", 0), ("k", 1)],
                                  [("k", p) for p in range(2, 6)]]):
            ITEMS += [(kind, p, c, P * i) for i, (kind, p) in enumerate(cols)]
        ITEMS += [("v", (g, a), 3, 256 * g) for g in range(2) for a in range(2)]
        ITEMS += [("v", (2, a), 4, 0) for a in range(2)] + [("q", 6, 4, 256), ("q", 7, 4, 384)]
        ITEMS += [("vT", 0, 5, 256), ("vT", 1, 5, 384), ("k", 6, 5, 0), ("k", 7, 5, P)]
        NI = len(ITEMS)

        off = [0]

        def small_buf(n, dt=F32):
            v = rsm[:, off[0]:off[0] + n]
            off[0] += n
            return v if dt == F32 else v.bitcast(dt)

        def t3(v, b):
            return v.rearrange("p (a b) -> p a b", b=b)

        scores_s, sel, pairsum = small_buf(64), small_buf(64), small_buf(96)
        gtop, gmax, geq = small_buf(16), small_buf(4), small_buf(16)
        gone = small_buf(16)
        selw, v4 = small_buf(64), small_buf(16)
        beats, ties, rank = small_buf(64), small_buf(64), small_buf(16)
        r0, r1 = small_buf(16), small_buf(16)
        m0, m1, msk = small_buf(64), small_buf(64), small_buf(64)
        mtmp = small_buf(64)
        g01 = small_buf(8)
        gden = small_buf(4)
        posm = small_buf(64)
        pos_bf = small_buf(32, BF16)
        msk_bf = small_buf(32, BF16)
        meta = small_buf(2 * NT * NE, BF16)
        idx_f = small_buf(4 * NE)
        idx_a = small_buf(NE)
        idxg = small_buf(NE, I32)
        idxs = small_buf(NE, I32)
        curs = small_buf(8, I32)
        cnt = small_buf(NE)
        ind = small_buf(48)
        cum = small_buf(48)
        cum2 = small_buf(48)
        over = small_buf(64)
        otmp = small_buf(64)
        ovk = small_buf(8)
        mcur = small_buf(1)
        nov_f = small_buf(1)
        nover_i = small_buf(1, I32)
        over_e_i = small_buf(1, I32)
        ocmp = small_buf(1)
        ometa = small_buf(16, BF16)
        assert off[0] <= 16 * 256, off[0]

        def on4(c0, n, reps):
            return small[:, c0:c0 + n].unsqueeze(1).broadcast_to([P, reps, n])

        NBIAS = 2 + 4 * 8

        def over_partitions(v):
            return bass.AP(tensor=v.tensor, offset=v.offset, ap=[[0, P], [1, v.shape[-1]]])

        def skewed(v, start, pattern):
            return bass.AP(tensor=v.tensor, offset=v.offset + start, ap=pattern)

        def item_dst(item):
            kind, what = item[0], item[1]
            if kind == "v":
                g, a = what
                return vt[:, g, 2 * a:2 * a + 2, :].rearrange("p t n -> p (t n)")
            return {"q": qT, "k": kT, "vT": vgT}[kind][:, what, :]

        def item_views(n):
            kind, what = ITEMS[n][:2]
            dst, src = item_dst(ITEMS[n]), ps[n % 4][:, :]
            if kind in ("q", "vT"):
                g = what // 2 if kind == "q" else 3
                dst, src = tiles_of(dst, g), in_tiles(src, g)
            return dst, src


        ITEM_END = {c: max(n for n, it in enumerate(ITEMS) if it[2] == c) + 1 for c in range(6)}

        def reader_done(c):
            if c < 6:
                return S["proj_mm"], ITEM_END[c]
            if c < 8:
                return L[0]["mo_mm"], L[0].value("mo_mm", 7 + c - 6)
            if CONV <= c < CONV + 4:
                return S["pw1_mm"], (7, 8, 15, 16)[c - CONV]
            if CONV + 4 <= c < CONV + 6:
                return L[1]["mo_mm"], L[1].value("mo_mm", 7 + c - CONV - 4)
            l = 0 if c < CONV else 1
            p = c - MOE[l]
            if p < 2:
                name, v = "gu_mm", p + 1
            elif p == 47:
                name, v = "dn_mm", 32
            else:
                n, which = divmod(p - 2, 3)
                name, v = ("dn_mm", 2 * n + 2) if which == 2 else ("gu_mm", 2 * (n + 1) + which + 1)
            return L[l][name], L[l].value(name, v)

        def load(sp, c, src, kk=KD):
            if c >= SLOTS:
                sp.wait_ge(*reader_done(c - SLOTS))
            sp.dma_start(slot(c, kk), src).then_inc(w_full[c % SLOTS], 16)

        ROUNDS = 6

        block = ctx.enter_context(nc.Block())

        @block.sync
        def _(sp):
            for c in range(6):
                load(sp, c, pk(w_in_attn[0])[:, :, c * 512:(c + 1) * 512])
            for c in range(2):
                load(sp, 6 + c, kp(w_out_attn[0])[:, :, c * 512:(c + 1) * 512])

            def experts(l):
                m, base = L[l], MOE[l]

                def expert_w(e, which):
                    w = (w_gate, w_up, w_down)[which][l]
                    src = w[e] if isinstance(e, int) else w[bass.ds(e, 1)].rearrange("o a n -> (o a) n")
                    return kp(src) if which == 2 else pk(src)

                load(sp, base, expert_w(0, 0))
                load(sp, base + 1, expert_w(0, 1))
                for n in range(2):
                    load(sp, base + 2 + 3 * n, expert_w(n + 1, 0))
                    load(sp, base + 3 + 3 * n, expert_w(n + 1, 1))
                    load(sp, base + 4 + 3 * n, expert_w(n, 2), KE)
                with sp.Fori(0, ROUNDS) as i:
                    for u in range(2):
                        n = 2 + u
                        for which in range(3):
                            c = base + 2 + 3 * n + which
                            if which == 2:
                                m.wait(sp, "dn_mm", 2 * (n - 2) + 2, i, 4)
                            else:
                                m.wait(sp, "gu_mm", 2 * (n - 1) + which + 1, i, 4)
                            e = i * 2 + (n if which == 2 else n + 1)
                            sp.dma_start(slot(c, KE if which == 2 else KD), expert_w(e, which))\
                              .then_inc(w_full[c % SLOTS], 16)
                load(sp, base + 44, expert_w(15, 0))
                load(sp, base + 45, expert_w(15, 1))
                load(sp, base + 46, expert_w(14, 2), KE)
                load(sp, base + 47, expert_w(15, 2), KE)
                m.wait(sp, "nover", 1)
                n = sp.value_load(nover_i[0:1, 0:1], min_val=0, max_val=NOVER)
                with sp.If(n > 0):
                    with sp.Fori(0, n) as j:
                        m.wait(sp, "o_idx", 1, j, 1)
                        sp.sem_inc(S["passed"], 1)
                        e = sp.value_load(over_e_i[0:1, 0:1], min_val=0, max_val=NE - 1)
                        for which in range(3):
                            if which:
                                m.wait(sp, "o_mm", which, j, 3)
                            dst = over_w.rearrange("p (k n) -> p k n", k=KE if which == 2 else KD)
                            sp.dma_start(dst, expert_w(e, which)).then_inc(m["o_w"], 16)

            experts(0)
            for c, col in enumerate((0, 1024, 512, 1536)):
                load(sp, CONV + c, pk(w_pw1[0])[:, :, col:col + 512])
            for c in range(2):
                load(sp, CONV + 4 + c, kp(w_pw2[0])[:, :, c * 512:(c + 1) * 512])
            experts(1)

        @block.tensor
        def _(pe):
            def mm(out_, lhsT, rhs, first=True, last=True):
                return pe.matmul(out_, lhsT, rhs, start=first, stop=last)

            def to_features(t, m, mm_sem, cp_sem):
                for half in range(2):
                    n = 2 * t + half
                    if n >= 2:
                        m.wait(pe, cp_sem, n - 1)
                    for k in range(4):
                        ins = pe.transpose(ps[6 + half][:, k * P:(k + 1) * P],
                                           x_tok[:, t, 4 * half + k::8], ident[:, :])
                    ins.then_inc(m[mm_sem], 1)

            pe.wait_ge(S["consts"], 16 * 3)
            pe.wait_ge(S["bucket_in"], 16)
            pe.wait_ge(S["rel_rep"], 1)
            pe.wait_ge(S["preset"], 1)
            for n in range(16):
                if n >= 2:
                    pe.wait_ge(S["row_cp"], n - 1)
                if n < 4:
                    ins = mm(ps[n % 2][:, :], rel_rep[0:33, n, :], bucket_sb[0:33, 0:W0])
                elif n < 8:
                    for a in range(2):
                        h = 4 + 2 * (n - 4) + a
                        c0 = W0 + (W1 if h >= 8 else 0)
                        ins = mm(ps[n % 2][:, a * W1:(a + 1) * W1], rel_rep[0:33, h, :], bucket_sb[0:33, c0:c0 + W1])
                else:
                    if n == 8:
                        pe.wait_ge(S["rpb_in"], 16)
                    ins = mm(ps[n % 2][:, 0:480], ones[0:1, :], rpb_row[0:1, (n - 8) * 480:(n - 7) * 480])
                ins.then_inc(S["row_mm"], 1)

            pe.wait_ge(S["x_in"], 16)
            for t in range(NT):
                to_features(t, FIRST, "xf0_mm", "xf0_cp")
            pe.wait_ge(S["xf0_cp"], 2 * NT)
            pe.wait_ge(S["row_cp"], 16)

            def copied(n):
                pe.wait_ge(S["proj_cpA" if n % 2 == 0 else "proj_cpV"], n // 2 + 1)

            for n, (kind, what, c, col) in enumerate(ITEMS):
                if n == 0 or ITEMS[n - 1][2] != c:
                    filled(pe, c)
                if n >= 4:
                    copied(n - 4)
                w = slot(c)
                if kind == "v":
                    g, a = what
                    for half in range(2):
                        for k in range(KD):
                            ins = mm(ps[n % 4][:, 256 * half:256 * (half + 1)], tokens(x_feat[:, k, :], g, 2 * a + half),
                                     w[:, k, col:col + 256], k == 0, k == KD - 1)
                else:
                    for k in range(KD):
                        ins = mm(ps[n % 4][:, :], w[:, k, col:col + P], x_feat[:, k, :], k == 0, k == KD - 1)
                ins.then_inc(S["proj_mm"], 1)
            copied(NI - 1)
            copied(NI - 2)
            for pr in range(2):
                for t in range(NT):
                    ins = pe.transpose(ps[4 + pr][:, t * P:(t + 1) * P], vgT[:, pr, t * P:(t + 1) * P], ident[:, :])
                ins.then_inc(S["vg_mm"], 1)
            pe.wait_ge(S["vg_cp"], 2)

            for step in range(NU + LAG_V):
                if step < NU:
                    u = step
                    h, t = UNITS[u]
                    g, lo = group(h), HD * (h % 2)
                    if u >= 2:
                        pe.wait_ge(S["sc_read"], u - 1)
                    nk = P * len(key_tiles(g, t))
                    mm(ps[u % 2][:, 0:nk], qT[lo:lo + HD, h // 2, t * P:(t + 1) * P],
                       keys(kT[lo:lo + HD, h // 2, :], g, t)).then_inc(S["scores"], 1)
                if 0 <= step - LAG_T < NU:
                    u = step - LAG_T
                    h, t = UNITS[u]
                    g = group(h)
                    if u < NA:
                        pe.wait_ge(S["probs"], u + 1)
                    else:
                        pe.wait_ge(S["pnorm"], u - NA + 1)
                    if u >= 2:
                        pe.wait_ge(S["pT_cp"], u - 1)
                    nb = len(key_tiles(g, t))
                    for i in range(nb):
                        ins = pe.transpose(ps[2 + u % 2][:, P * i:P * (i + 1)], probs[:, u % 4, P * i:P * (i + 1)],
                                           ident[:, :])
                    ins.then_inc(S["pT"], 1)
                if step - LAG_V >= 0:
                    u = step - LAG_V
                    h, t = UNITS[u]
                    g, lo, seq = group(h), HD * (h % 2), u // 8
                    pe.wait_ge(S["pT_cp"], u + 1)
                    if u % 8 == 0 and seq >= 2:
                        pe.wait_ge(S["evac"], seq - 1)
                    kb = key_tiles(g, t)
                    for i, b in enumerate(kb):
                        ins = mm(ps[4 + seq % 2][lo:lo + HD, t * P:(t + 1) * P],
                                 vt[:, g, b, HD * (h % 4):HD * (h % 4 + 1)], probsT[:, u % 2, P * i:P * (i + 1)],
                                 i == 0, i == len(kb) - 1)
                    ins.then_inc(S["pv"], 1)
                    if u % 8 == 7 and u < NA:
                        if seq >= 1:
                            pe.wait_ge(S["evac"], seq)
                        for src, bank in ((nmax, 6), (psum_e, 7)):
                            for tt in range(NT):
                                for a in range(2):
                                    col = 8 * seq + 4 * a + tt
                                    ins = mm(ps[bank][HD * a:HD * (a + 1), tt * P:(tt + 1) * P],
                                             src[:, col:col + 1].broadcast_to([P, HD]), ident[:, :])
                        ins.then_inc(S["stat"], 1)

            def mixer_out(l, src, c0, ready):
                m = L[l]

                def logits(t):
                    m.wait(pe, "xf_cp", 2 * t + 2)
                    for k in range(KD):
                        ins = mm(ps[5][:, t * NE:(t + 1) * NE], x_feat[:, k, t * P:(t + 1) * P], wr[:, k, :],
                                 k == 0, k == KD - 1)
                    ins.then_inc(m["logit_mm"], 1)

                for t in range(NT):
                    for half in range(2):
                        if t == 0:
                            filled(pe, c0 + half)
                        n = 2 * t + half
                        if n >= 4:
                            m.wait(pe, "mo_read", n - 3)
                        for k in range(KD):
                            if n == 0:
                                ready(k)
                            ins = mm(ps[n % 4][:, :], src(k, t), slot(c0 + half)[:, k, :], k == 0, k == KD - 1)
                        ins.then_inc(m["mo_mm"], 1)
                    if t >= 1:
                        m.wait(pe, "ln_done", t)
                        to_features(t - 1, m, "xf_mm", "xf_cp")
                if l == 0:
                    pe.wait_ge(S["router_in"], 32)
                for t in range(NT - 1):
                    logits(t)
                m.wait(pe, "ln_done", NT)
                to_features(NT - 1, m, "xf_mm", "xf_cp")
                logits(NT - 1)

            def routing(l):
                m = L[l]
                m.wait(pe, "mask", 1)
                mk = t3(msk_bf, NE)
                for t in range(NT):
                    for a in range(t):
                        mm(ps[0][:, t * NE:(t + 1) * NE], ones_bf[:, :], mk[:, a], a == 0, False)
                    mm(ps[0][:, t * NE:(t + 1) * NE], before_bf[:, :], mk[:, t], t == 0, True)
                for t in range(NT):
                    ins = mm(ps[0][:, 4 * NE:5 * NE], ones_bf[:, :], mk[:, t], t == 0, t == NT - 1)
                ins.then_inc(m["pos_mm"], 1)
                mt = meta.rearrange("p (t e c) -> p t e c", t=NT, e=NE)
                m.wait(pe, "picks", NT)
                for e in range(NE):
                    for t in range(NT):
                        ins = mm(ps[1][:, 4 * e:4 * e + 4], picks[:, t, e, :], mt[:, t, e, :], t == 0, t == NT - 1)
                ins.then_inc(m["idx_mm"], 1)

            def experts(l):
                m, base = L[l], MOE[l]

                def rows_T(e, i=None):
                    par = e % 2
                    m.wait(pe, f"g_full{par}", 16 * (e // 2 + 1), i, 16)
                    if e > 0:
                        m.wait(pe, "xt_cpA", e, i, 2)
                        m.wait(pe, "xt_cpV", e, i, 2)
                    for half in range(2):
                        for k in range(4):
                            ins = pe.transpose(ps[2 + half][:, k * P:(k + 1) * P], xg[:, par, 4 * half + k::8], ident[:, :])
                        ins.then_inc(m["xt_mm"], 1)

                def gate_up(e, i=None):
                    m.wait(pe, "xt_cpA", e + 1, i, 2)
                    m.wait(pe, "xt_cpV", e + 1, i, 2)
                    if e > 0:
                        m.wait(pe, "hid", e, i, 2)
                    c = base + (3 * e - 1 if e else 0)
                    for half in range(2):
                        filled(pe, c + half, i)
                        for k in range(KD):
                            ins = mm(ps[half][:, :], xgT[:, e % 2, k, :], slot(c + half)[:, k, :], k == 0, k == KD - 1)
                        ins.then_inc(m["gu_mm"], 1)

                def hidden_T(e, i=None):
                    m.wait(pe, "hid", e + 1, i, 2)
                    for k in range(KE):
                        ins = pe.transpose(ps[4][:, k * P:(k + 1) * P], hid[:, k * P:(k + 1) * P], ident[:, :])
                    ins.then_inc(m["ht_mm"], 1)

                def down(e, i=None):
                    m.wait(pe, "ht_cp", e + 1, i, 2)
                    if e > 0:
                        m.wait(pe, "y_cpA", e, i, 2)
                        m.wait(pe, "y_cpV", e, i, 2)
                    c = base + (47 if e == 15 else 4 + 3 * e)
                    filled(pe, c, i)
                    for half in range(2):
                        for k in range(KE):
                            ins = mm(ps[5 + half][:, :], hidT[:, k, :], slot(c, KE)[:, k, half * 512:(half + 1) * 512],
                                     k == 0, k == KE - 1)
                        ins.then_inc(m["dn_mm"], 1)

                rows_T(0)
                gate_up(0)
                rows_T(1)
                hidden_T(0)
                gate_up(1)
                rows_T(2)
                down(0)
                hidden_T(1)
                with pe.Fori(0, ROUNDS) as i:
                    for e in (2, 3):
                        gate_up(e, i)
                        rows_T(e + 1, i)
                        down(e - 1, i)
                        hidden_T(e, i)
                gate_up(14)
                rows_T(15)
                down(13)
                hidden_T(14)
                gate_up(15)
                down(14)
                hidden_T(15)
                down(15)

            def more_tiles(l):
                m = L[l]
                m.wait(pe, "nover", 1)
                m.wait(pe, "y_cpA", NE)
                m.wait(pe, "y_cpV", NE)
                n = pe.value_load(nover_i[0:1, 0:1], min_val=0, max_val=NOVER)
                om = ometa.rearrange("p (k t c) -> p k t c", k=2, t=NT)
                with pe.If(n > 0):
                    with pe.Fori(0, n) as j:
                        m.wait(pe, "o_pick", 1, j, 1)
                        for a in range(2):
                            for t in range(NT):
                                ins = mm(ps[7][:, 0:4], over_picks[:, a, t, :], om[:, a, t, :], a + t == 0, a + t == NT)
                        ins.then_inc(m["o_imm"], 1)
                        m.wait(pe, "o_gath", 16, j, 16)
                        for k in range(KD):
                            ins = pe.transpose(ps[2 + k // 4][:, k % 4 * P:(k % 4 + 1) * P], xg[:, 0, k::8], ident[:, :])
                        ins.then_inc(m["o_tr"], 1)
                        m.wait(pe, "o_cp", 1, j, 3)
                        for half in range(2):
                            m.wait(pe, "o_w", 16 * (half + 1), j, 48)
                            for k in range(KD):
                                ins = mm(ps[half][:, :], xgT[:, 0, k, :], over_w.rearrange("p (k n) -> p k n", k=KD)[:, k, :],
                                         k == 0, k == KD - 1)
                            ins.then_inc(m["o_mm"], 1)
                        m.wait(pe, "o_cp", 2, j, 3)
                        for k in range(KE):
                            ins = pe.transpose(ps[4][:, k * P:(k + 1) * P], hid[:, k * P:(k + 1) * P], ident[:, :])
                        ins.then_inc(m["o_tr"], 1)
                        m.wait(pe, "o_cp", 3, j, 3)
                        m.wait(pe, "o_w", 48, j, 48)
                        for half in range(2):
                            for k in range(KE):
                                ins = mm(ps[5 + half][:, :], hidT[:, k, :],
                                         over_w.rearrange("p (k n) -> p k n", k=KE)[:, k, half * 512:(half + 1) * 512],
                                         k == 0, k == KE - 1)
                        ins.then_inc(m["o_mm"], 1)

            def conv():
                for t in range(NT):
                    L[0].wait(pe, "ln2_done", t + 1)
                    to_features(t, L[0], "xf2_mm", "xf2_cp")
                pe.wait_ge(S["cvec_in"], 16 * 5)
                pe.transpose(ps[4][:, 0:40], vrow[0:40, :], ident[0:40, 0:40])
                for c in range(8):
                    ins = pe.transpose(ps[5][:, c * 32:c * 32 + NTAP], crow[0:NTAP, c * P:(c + 1) * P], ident[0:NTAP, 0:NTAP])
                ins.then_inc(S["cvec_mm"], 1)
                L[0].wait(pe, "xf2_cp", 2 * NT)
                for c in range(8):
                    for gate in range(2):
                        ch = CONV + 2 * (c // 4) + gate
                        if c % 4 == 0:
                            filled(pe, ch)
                        if c >= 2:
                            pe.wait_ge(S["u_ready"], c - 1)
                        for k in range(KD):
                            ins = mm(ps[2 * gate + c % 2][:, :], slot(ch)[:, k, (c % 4) * P:(c % 4 + 1) * P], x_feat[:, k, :],
                                     k == 0, k == KD - 1)
                        ins.then_inc(S["pw1_mm"], 1)
                pe.wait_ge(S["cvec_cp"], 1)
                for c in range(8):
                    pe.wait_ge(S["conv_done"], c + 1)
                    ins = mm(ps[4][:, :], ones[:, :], conv_o[:, c, :], c == 0, c == 7)
                ins.then_inc(S["csum_mm"], 1)
                for c in range(8):
                    pe.wait_ge(S["c_sq"], c + 1)
                    mm(ps[5][:, :], ones[:, :], csq[:, c % 2, :], c == 0, c == 7).then_inc(S["cvar_mm"], 1)

            pe.wait_ge(S["mg_done"], 2)
            pe.wait_ge(S["evac"], 8)
            mixer_out(0, lambda k, t: qT[:, k, t * P:(t + 1) * P], 6, lambda k: None)
            routing(0)
            experts(0)
            more_tiles(0)
            conv()
            mixer_out(1, lambda k, t: conv_o[:, k, t * P:(t + 1) * P], CONV + 4,
                      lambda k: pe.wait_ge(S["c_act"], k + 1))
            routing(1)
            experts(1)
            more_tiles(1)

        @block.scalar
        def _(act):
            def copy(out_, in_):
                return act.activation(out_, in_, ACT.Copy)

            act.dma_start(ident[:, :], c_mats[0]).then_inc(S["consts"], 16)
            act.dma_start(bucket_sb[0:33, :], c_bucket).then_inc(S["bucket_in"], 16)
            act.wait_ge(S["preset"], 2)
            act.dma_start(rel_sb[0:32, :], rel_bias).then_inc(S["rel_in"], 16)
            act.dma_start(rpb_row[0:1, :].rearrange("p (h j) -> p h j", j=RW)[:, :, 16:47],
                          rpb_2d.rearrange("o h r j -> o (h r) j")).then_inc(S["rpb_in"], 16)
            act.dma_start(x_tok[:, :, :], x[0].rearrange("(t p) d -> p t d", p=P)).then_inc(S["x_in"], 16)
            act.dma_start(mats[:, :, :], c_mats[1:3].rearrange("m p n -> p m n")).then_inc(S["consts"], 16)
            act.dma_start(small[:, :], c_small).then_inc(S["consts"], 16)
            act.dma_start(window[:, :, :], c_window).then_inc(S["bias_in"], 16)
            act.dma_start(wr[:, :, :], pk(w_router)).then_inc(S["router_in"], 16)
            act.dma_start(rb[:, :], over_partitions(router_bias)).then_inc(S["router_in"], 16)

            for n in range(16):
                act.wait_ge(S["row_mm"], n + 1)
                if n >= 3:
                    act.wait_ge(S[f"row_out{n % 3}"], 16 * (n // 3))
                wid = 512 if n < 8 else 480
                copy(stage[:, n % 3, 0:wid], ps[n % 2][:, 0:wid]).then_inc(S["row_cp"], 1)
                act.wait_ge(S["row_cp"], n + 1)
                if n < 4:
                    dst = bias_d0[n].rearrange("(p w) -> p w", p=P)
                elif n < 8:
                    dst = bias_d12[2 * (n - 4):2 * (n - 4) + 2].rearrange("h (p w) -> p h w", p=P)
                else:
                    h, half = divmod(n - 8, 2)
                    dst = bias_dn[h].rearrange("(p w) -> p w", p=P)[:, 480 * half:480 * (half + 1)]
                src = stage[:, n % 3, 0:wid]
                if 4 <= n < 8:
                    src = src.rearrange("p (h w) -> p h w", h=2)
                act.dma_start(dst, src).then_inc(S[f"row_out{n % 3}"], 16)

            def features_copy(t, m, mm_sem, cp_sem):
                for half in range(2):
                    m.wait(act, mm_sem, 2 * t + half + 1)
                    copy(x_feat[:, 4 * half:4 * half + 4, t * P:(t + 1) * P],
                         ps[6 + half][:, :].rearrange("p (k n) -> p k n", k=4)).then_inc(m[cp_sem], 1)

            for t in range(NT):
                features_copy(t, FIRST, "xf0_mm", "xf0_cp")

            for n in range(0, NI, 2):
                act.wait_ge(S["proj_mm"], n + 1)
                if ITEMS[n][0] == "vT":
                    act.wait_ge(S["bias_n"], 1)
                copy(*item_views(n)).then_inc(S["proj_cpA"], 1)

            for pr in range(2):
                act.wait_ge(S["vg_mm"], pr + 1)
                copy(vt[:, 3, :, P * pr:P * (pr + 1)], ps[4 + pr][:, :].rearrange("p (t n) -> p t n", t=NT))\
                    .then_inc(S["vg_cp"], 1)

            def evacuate(seq):
                act.wait_ge(S["pv"], 8 * (seq + 1))
                pr = PAIRS[seq]
                g = pr // 2
                todo = [(qT[:, pr, :], 4 + seq % 2)]
                if g < 3:
                    act.wait_ge(S["stat"], seq + 1)
                    if seq >= 3:
                        act.wait_ge(S["mg_done"], 1)
                    todo += [(nmax_b[:, g, :], 6), (sums_b[:, g, :], 7)]
                for dst, bank in todo:
                    ins = copy(in_tiles(dst, g), tiles_of(ps[bank][:, :], g))
                ins.then_inc(S["evac"], 1)

            def merge_exp(jp):
                act.wait_ge(S["mg_diff"], jp + 1)
                act.activation(nmax_b, nmax_b, ACT.Exp).then_inc(S["mg_exp"], 1)

            for step in range(NU + 12):
                if step < NU:
                    u = step
                    h, t = UNITS[u]
                    nk = P * len(key_tiles(group(h), t))
                    act.wait_ge(S["nmax"], u + 1)
                    act.activation(probs[:, u % 4, 0:nk], probs[:, u % 4, 0:nk], ACT.Exp, bias=nmax[:, u:u + 1],
                                   accum_out=psum_e[:, u:u + 1]).then_inc(S["probs"], 1)
                if 0 <= step - LAG_T < NU:
                    u = step - LAG_T
                    h, t = UNITS[u]
                    nk = P * len(key_tiles(group(h), t))
                    act.wait_ge(S["pT"], u + 1)
                    if u >= 2:
                        act.wait_ge(S["pv"], u - 1)
                    copy(probsT[:, u % 2, 0:nk], ps[2 + u % 2][:, 0:nk]).then_inc(S["pT_cp"], 1)
                if step >= 12 and (step - 12) % 8 == 0 and (step - 12) // 8 < 8:
                    evacuate((step - 12) // 8)
                if step in (32, 60):
                    merge_exp(0 if step == 32 else 1)

            def root(m, ve, std, n):
                m.wait(act, ve, n)
                act.activation(mv[:, 3:4], mv[:, 2:3], ACT.Sqrt).then_inc(m[std], 1)

            def mixer(l):
                m = L[l]
                for t in range(NT):
                    root(m, "ln_ve", "ln_std", t + 1)
                    if t >= 1:
                        features_copy(t - 1, m, "xf_mm", "xf_cp")
                features_copy(NT - 1, m, "xf_mm", "xf_cp")
                m.wait(act, "logit_mm", NT)
                act.activation(scores_s, ps[5][:, 0:NT * NE], ACT.Sigmoid).then_inc(m["score"], 1)

            def experts(l):
                m = L[l]

                def rows_copy(e, i=None):
                    m.wait(act, "xt_mm", 2 * e + 1, i, 4)
                    if e >= 2:
                        m.wait(act, "gu_mm", 2 * (e - 1), i, 4)
                    copy(xgT[:, e % 2, 0:4, :], ps[2][:, :].rearrange("p (k n) -> p k n", k=4)).then_inc(m["xt_cpA"], 1)

                def silu(e, i=None):
                    m.wait(act, "gu_mm", 2 * e + 1, i, 4)
                    if e >= 1:
                        m.wait(act, "hid", e, i, 2)
                    act.activation(sig, ps[0][:, :], ACT.Silu).then_inc(m["silu"], 1)

                def hidden_copy(e, i=None):
                    m.wait(act, "ht_mm", e + 1, i, 2)
                    if e >= 1:
                        m.wait(act, "dn_mm", 2 * e, i, 4)
                    copy(hidT, ps[4][:, :].rearrange("p (k n) -> p k n", k=KE)).then_inc(m["ht_cp"], 1)

                def rows_out(e, i=None):
                    m.wait(act, "dn_mm", 2 * e + 1, i, 4)
                    if e >= 2:
                        m.wait(act, f"s_done{e % 2}", 16 * (e // 2), i, 16)
                    copy(y_sb[:, e % 2, 0:512], ps[5][:, :]).then_inc(m["y_cpA"], 1)

                rows_copy(0)
                silu(0)
                rows_copy(1)
                hidden_copy(0)
                silu(1)
                rows_copy(2)
                rows_out(0)
                hidden_copy(1)
                silu(2)
                rows_copy(3)
                rows_out(1)
                hidden_copy(2)
                with act.Fori(0, ROUNDS - 1) as i:
                    for e in (3, 4):
                        silu(e, i)
                        rows_copy(e + 1, i)
                        rows_out(e - 1, i)
                        hidden_copy(e, i)
                for e in (13, 14):
                    silu(e)
                    rows_copy(e + 1)
                    rows_out(e - 1)
                    hidden_copy(e)
                silu(15)
                rows_out(14)
                hidden_copy(15)
                rows_out(15)

            def more_tiles(l):
                m = L[l]
                m.wait(act, "nover", 1)
                n = act.value_load(nover_i[0:1, 0:1], min_val=0, max_val=NOVER)
                with act.If(n > 0):
                    with act.Fori(0, n) as j:
                        m.wait(act, "o_mm", 1, j, 3)
                        act.activation(sig, ps[0][:, :], ACT.Silu).then_inc(m["o_silu"], 1)

            def moe_norm(l):
                m = L[l]
                for t in range(NT):
                    root(m, "ln2_ve", "ln2_std", t + 1)
                    if l == 0 and t >= 1:
                        features_copy(t - 1, m, "xf2_mm", "xf2_cp")
                if l == 0:
                    features_copy(NT - 1, m, "xf2_mm", "xf2_cp")

            def conv():
                act.wait_ge(S["cvec_mm"], 1)
                copy(cvec[:, 0:40], ps[4][:, 0:40]).then_inc(S["act_chain"], 1)
                copy(taps[:, :, 0:NTAP], ps[5][:, 0:256].rearrange("p (c n) -> p c n", c=8)[:, :, 0:NTAP])\
                    .then_inc(S["cvec_cp"], 1)
                act.wait_ge(S["act_chain"], 1)
                for c in range(8):
                    act.wait_ge(S["pw1_mm"], 2 * c + 2)
                    if c >= 2:
                        act.wait_ge(S["u_ready"], c - 1)
                    act.activation(gsig[:, c % 2, :], ps[2 + c % 2][:, :], ACT.Sigmoid, bias=cvec[:, 8 + c:9 + c])\
                        .then_inc(S["gate_sig"], 1)
                for c in range(8):
                    act.wait_ge(S["c_dev"], c + 1)
                    if c >= 2:
                        act.wait_ge(S["cvar_mm"], c - 1)
                    act.activation(csq[:, c % 2, :], conv_o[:, c, :], ACT.Square).then_inc(S["c_sq"], 1)
                act.wait_ge(S["c_ve"], 1)
                act.activation(crstd, crstd, ACT.Sqrt).then_inc(S["c_std"], 1)
                for c in range(8):
                    act.wait_ge(S["c_z"], c + 1)
                    act.activation(conv_o[:, c, :], conv_o[:, c, :], ACT.Silu, bias=cvec[:, 32 + c:33 + c],
                                   scale=cvec[:, 24 + c:25 + c]).then_inc(S["c_act"], 1)

            mixer(0)
            experts(0)
            more_tiles(0)
            moe_norm(0)
            conv()
            mixer(1)
            experts(1)
            more_tiles(1)
            moe_norm(1)

        @block.vector
        def _(dve):
            link = Chain(dve, S["dve_chain"])
            tt, ts, stt = dve.tensor_tensor, dve.tensor_scalar, dve.scalar_tensor_tensor

            dve.memset(rel_sb[:, :], 1.0).then_inc(S["dve_chain"], 1)
            link.n = 1
            dve.wait_ge(S["dve_chain"], 1)
            dve.memset(ones[:, :], 1.0).then_inc(S["preset"], 1)
            dve.memset(rpb_row[0:1, :], 0.0).then_inc(S["preset"], 1)
            dve.wait_ge(S["rel_in"], 16)
            dve.tensor_copy(rel_rep[0:33], rel_sb[:, :].unsqueeze(2).broadcast_to([33, 12, P])).then_inc(S["rel_rep"], 1)
            dve.wait_ge(S["consts"], 48)
            dve.tensor_copy(before_bf[:, :], mats[:, 0, :])
            dve.tensor_copy(slot_bf[:, :], mats[:, 1, :])
            dve.memset(ones_bf[:, :], 1.0).then_inc(S["bf_ready"], 1)

            for n in range(1, NI, 2):
                dve.wait_ge(S["proj_mm"], n + 1)
                if n == 13:
                    dve.wait_ge(S["biases_in"], 16 * NBIAS)
                    for h in range(4):
                        ins = dve.tensor_copy(bias_n[:, h].rearrange("p (b r c) -> p b r c", b=3, c=16),
                                              bias_nr[:, h].rearrange("p (r b c) -> p b r c", b=3, c=16))
                    ins.then_inc(S["bias_n"], 1)
                    dve.wait_ge(S["bias_n"], 1)
                dve.tensor_copy(*item_views(n)).then_inc(S["proj_cpV"], 1)

            def normalize(u):
                h, t = UNITS[u]
                nk = P * len(key_tiles(group(h), t))
                dve.wait_ge(S["probs"], u + 1)
                link(dve.reciprocal(rinv[:, u:u + 1], psum_e[:, u:u + 1]))
                ts(probs[:, u % 4, 0:nk], probs[:, u % 4, 0:nk], rinv[:, u:u + 1], None, ALU.mult).then_inc(S["pnorm"], 1)

            dve.wait_ge(S["bias_in"], 16)
            for u, (h, t) in enumerate(UNITS):
                g = group(h)
                kb = key_tiles(g, t)
                nk = P * len(kb)
                x0 = kb[0] - (t - 1)
                lg = probs[:, u % 4, 0:nk]
                raw = ps[u % 2][:, 0:nk]
                if u >= 4:
                    dve.wait_ge(S["pT"], u - 3)
                dve.wait_ge(S["scores"], u + 1)
                if g == 3:
                    stt(lg, raw, SCALE, bias_n[:, h - 12, P * x0:P * x0 + nk], ALU.mult, ALU.add).then_inc(S["sc_read"], 1)
                    dve.wait_ge(S["sc_read"], u + 1)
                    win = window[:, t, 16 * x0:16 * (x0 + len(kb))].rearrange("p (b c) -> p b c", c=16)
                    win = win.unsqueeze(2).broadcast_to([P, len(kb), 8, 16])
                    lg4 = lg.rearrange("p (b r c) -> p b r c", r=8, c=16)
                    link(tt(lg4, lg4, win, ALU.add))
                else:
                    b = bias0[:, h, P * x0:P * x0 + nk] if g == 0 else bias12[:, h - 4, :]
                    stt(lg, raw, SCALE, b, ALU.mult, ALU.add).then_inc(S["sc_read"], 1)
                    dve.wait_ge(S["sc_read"], u + 1)
                link(dve.reduce_max(rinv[:, u:u + 1], lg, X_AXIS))
                ts(nmax[:, u:u + 1], rinv[:, u:u + 1], -1.0, None, ALU.mult).then_inc(S["nmax"], 1)
                if u - 1 >= NA:
                    normalize(u - 1)
                if u in (30, 55):
                    dve.wait_ge(S["evac"], 3 if u == 30 else 6)
                    link(tt(den_b, nmax_b[:, 0, :], nmax_b[:, 1, :], ALU.min))
                    tt(den_b, den_b, nmax_b[:, 2, :], ALU.min).then_inc(S["mg_min"], 1)
                if u in (36, 63):
                    dve.wait_ge(S["mg_den"], 1 if u == 36 else 2)
                    dve.reciprocal(den_b, den_b).then_inc(S["mg_inv"], 1)
            normalize(NU - 1)

            def norm(t, m, ve, std, done):
                row = x_tok[:, t, :]
                dve.bn_stats(stats[:, 0, :], row[:, 0:512])
                link(dve.bn_stats(stats[:, 1, :], row[:, 512:1024]))
                link(dve.bn_aggr(mv[:, 0:2], stats[:, :, :]))
                ts(mv[:, 2:3], mv[:, 1:2], LN_EPS, None, ALU.add).then_inc(m[ve], 1)
                m.wait(dve, std, t + 1)
                link(dve.reciprocal(mv[:, 2:3], mv[:, 3:4]))
                link(ts(row, row, mv[:, 0:1], mv[:, 2:3], ALU.subtract, ALU.mult))
                link(tt(row, row, ln_g, ALU.mult))
                tt(row, row, ln_b, ALU.add).then_inc(m[done], 1)
                m.wait(dve, done, t + 1)

            def mixer(l):
                m = L[l]
                if l == 1:
                    dve.wait_ge(S["xres"], NT)
                for t in range(NT):
                    for half in range(2):
                        n = 2 * t + half
                        m.wait(dve, "mo_mm", n + 1)
                        row = x_tok[:, t, 512 * half:512 * (half + 1)]
                        if l == 0:
                            stt(row, row, ALPHA, ps[n % 4][:, :], ALU.mult, ALU.add).then_inc(m["mo_read"], 1)
                        else:
                            tt(row, ps[n % 4][:, :], row, ALU.add).then_inc(m["mo_read"], 1)
                    m.wait(dve, "mo_read", 2 * t + 2)
                    if t == 0:
                        m.wait(dve, "lnp_in", 32)
                    norm(t, m, "ln_ve", "ln_std", "ln_done")

            def routing(l):
                m = L[l]
                g4 = lambda v: v.rearrange("p (t g i) -> p t g i", t=NT, g=NG)
                pg = lambda v: v.rearrange("p (a i) -> p a i", i=EPG)
                m.wait(dve, "score", 1)
                link(tt(t3(sel, NE), t3(scores_s, NE), rb[:, :].unsqueeze(1).broadcast_to([P, NT, NE]), ALU.add))
                a, q = pg(sel), t3(pairsum, 6)
                tt(q[:, :, 0:3], a[:, :, 0:3], a[:, :, 1:4], ALU.add)
                tt(q[:, :, 3:5], a[:, :, 0:2], a[:, :, 2:4], ALU.add)
                link(tt(q[:, :, 5:6], a[:, :, 0:1], a[:, :, 3:4], ALU.add))
                link(dve.reduce_max(gtop, q, X_AXIS))
                link(dve.reduce_max(gmax, t3(gtop, NG), X_AXIS))
                link(tt(t3(geq, NG), t3(gtop, NG), gmax.unsqueeze(2).broadcast_to([P, NT, NG]), ALU.is_equal))
                link(tt(t3(geq, NG), t3(geq, NG), on4(0, NG, NT), ALU.mult))
                link(dve.reduce_max(gmax, t3(geq, NG), X_AXIS))
                link(tt(t3(gone, NG), t3(geq, NG), gmax.unsqueeze(2).broadcast_to([P, NT, NG]), ALU.is_equal))
                by_group = t3(gone, NG).unsqueeze(3).broadcast_to([P, NT, NG, EPG])
                link(tt(g4(selw), g4(sel), by_group, ALU.mult))
                link(dve.reduce_sum(t3(v4, EPG), g4(selw).rearrange("p t g i -> p t i g"), X_AXIS))
                mine = t3(v4, EPG).unsqueeze(3).broadcast_to([P, NT, EPG, EPG])
                other = t3(v4, EPG).unsqueeze(2).broadcast_to([P, NT, EPG, EPG])
                tt(g4(beats), other, mine, ALU.is_gt)
                link(tt(g4(ties), other, mine, ALU.is_equal))
                link(tt(t3(ties, 16), t3(ties, 16), on4(4, 16, NT), ALU.mult))
                link(tt(beats, beats, ties, ALU.add))
                link(dve.reduce_sum(t3(rank, EPG), g4(beats), X_AXIS))
                ts(r0, rank, 0.0, None, ALU.is_equal)
                link(ts(r1, rank, 1.0, None, ALU.is_equal))
                for dst, r in ((m0, r0), (m1, r1)):
                    last = tt(g4(dst), by_group, t3(r, EPG).unsqueeze(2).broadcast_to([P, NT, NG, EPG]), ALU.mult)
                link(last)
                link(tt(msk, m0, m1, ALU.add))
                dve.tensor_copy(msk_bf, msk).then_inc(m["mask"], 1)
                link(tt(mtmp, m0, scores_s, ALU.mult))
                link(dve.reduce_sum(g01[:, 0:4], t3(mtmp, NE), X_AXIS))
                link(tt(mtmp, m1, scores_s, ALU.mult))
                link(dve.reduce_sum(g01[:, 4:8], t3(mtmp, NE), X_AXIS))
                link(tt(gden, g01[:, 0:4], g01[:, 4:8], ALU.add))
                link(dve.reciprocal(gden, gden))
                link(tt(g01.rearrange("p (k t) -> p k t", k=2), g01.rearrange("p (k t) -> p k t", k=2),
                        gden.unsqueeze(1).broadcast_to([P, 2, NT]), ALU.mult))
                mt = meta.rearrange("p (t e c) -> p t e c", t=NT, e=NE)
                parts = small[:, 36:52].rearrange("p (t c) -> p t c", t=NT)
                link(dve.tensor_copy(mt, parts.unsqueeze(2).broadcast_to([P, NT, NE, 4])))
                link(ts(mt[:, :, :, 2], t3(m1, NE), float(SEQ), None, ALU.mult))
                m.wait(dve, "pos_mm", 1)
                link(stt(posm, ps[0][:, 0:64], 1.0, msk, ALU.add, ALU.mult))
                link(dve.tensor_copy(pos_bf, posm))
                for t in range(NT):
                    tt(picks[:, t], slot_bf[:, :].unsqueeze(1).broadcast_to([P, NE, P]),
                       t3(pos_bf, NE)[:, t].unsqueeze(2).broadcast_to([P, NE, P]), ALU.is_equal).then_inc(m["picks"], 1)
                link(dve.tensor_copy(cnt, ps[0][:, 64:80]))
                for j in range(3):
                    last = ts(ind[:, 16 * j:16 * (j + 1)], cnt, float(P * (j + 1)), None, ALU.is_gt)
                link(last)
                link(dve.reduce_sum(nov_f, ind, X_AXIS))
                dve.tensor_copy(nover_i, nov_f).then_inc(m["nover"], 1)
                slots_to_rows(link, m, "idx_mm", "idx", ps[1], idx_f, NE, idxg, idxs, idx_a)

            def slots_to_rows(link, m, mm_sem, done, bank, f, n, rows_in, rows_out, tmp, j=None):
                m.wait(dve, mm_sem, 1, j, 1)
                link(dve.tensor_copy(f, bank[:, 0:4 * n]))
                f4 = t3(f, 4)
                link(ts(tmp, f4[:, :, 3], -4096.0, 4096.0, ALU.mult, ALU.add))
                link(tt(tmp, tmp, f4[:, :, 0], ALU.add))
                link(tt(tmp, tmp, f4[:, :, 1], ALU.add))
                link(dve.tensor_copy(rows_in, tmp))
                tt(rows_out, tmp, f4[:, :, 2], ALU.add).then_inc(m[done], 1)

            def experts(l):
                m = L[l]

                def rows_copy(e, i=None):
                    m.wait(dve, "xt_mm", 2 * e + 2, i, 4)
                    if e >= 2:
                        m.wait(dve, "gu_mm", 2 * (e - 1), i, 4)
                    dve.tensor_copy(xgT[:, e % 2, 4:8, :], ps[3][:, :].rearrange("p (k n) -> p k n", k=4))\
                        .then_inc(m["xt_cpV"], 1)

                def hidden(e, i=None):
                    m.wait(dve, "silu", e + 1, i, 2)
                    m.wait(dve, "gu_mm", 2 * e + 2, i, 4)
                    if e >= 1:
                        m.wait(dve, "ht_mm", e, i, 2)
                    tt(hid, ps[1][:, :], sig, ALU.mult).then_inc(m["hid"], 1)

                def rows_out(e, i=None):
                    m.wait(dve, "dn_mm", 2 * e + 2, i, 4)
                    if e >= 2:
                        m.wait(dve, f"s_done{e % 2}", 16 * (e // 2), i, 16)
                    dve.tensor_copy(y_sb[:, e % 2, 512:1024], ps[6][:, :]).then_inc(m["y_cpV"], 1)

                rows_copy(0)
                hidden(0)
                rows_copy(1)
                hidden(1)
                rows_copy(2)
                rows_out(0)
                hidden(2)
                rows_copy(3)
                rows_out(1)
                with dve.Fori(0, ROUNDS - 1) as i:
                    for e in (3, 4):
                        hidden(e, i)
                        rows_copy(e + 1, i)
                        rows_out(e - 1, i)
                for e in (13, 14):
                    hidden(e)
                    rows_copy(e + 1)
                    rows_out(e - 1)
                hidden(15)
                rows_out(14)
                rows_out(15)

            def more_tiles(l):
                m = L[l]
                n = dve.value_load(nover_i[0:1, 0:1], min_val=0, max_val=NOVER)
                with dve.If(n > 0):
                    m.wait(dve, "s_done0", 16 * 8)
                    m.wait(dve, "gu_mm", 32)
                    m.wait(dve, "y_cpA", NE)
                    ol = Chain(dve, m["o_chain"])
                    ol(ts(cum[:, 0:1], ind[:, 0:1], 0.0, None, ALU.mult))
                    ol(dve.tensor_copy(cum[:, 1:48], ind[:, 0:47]))
                    src, dst = cum, cum2
                    for d in (1, 2, 4, 8, 16, 32):
                        dve.tensor_copy(dst[:, 0:d], src[:, 0:d])
                        ol(tt(dst[:, d:48], src[:, d:48], src[:, 0:48 - d], ALU.add))
                        src, dst = dst, src
                    ol(ts(over, posm, 0.0, None, ALU.mult))
                    for j in range(3):
                        lo, hi = float(P * (j + 1)), float(P * (j + 2))
                        base = src[:, 16 * j:16 * (j + 1)].unsqueeze(1).broadcast_to([P, NT, NE])
                        ol(ts(t3(otmp, NE), base, float(P), -lo, ALU.mult, ALU.add))
                        ol(tt(otmp, otmp, posm, ALU.add))
                        ol(stt(otmp, posm, lo, otmp, ALU.is_gt, ALU.mult))
                        ol(stt(otmp, posm, hi, otmp, ALU.is_le, ALU.mult))
                        ol(tt(over, over, otmp, ALU.add))
                    for a, mk in ((0, m0), (1, m1)):
                        ol(tt(otmp, over, mk, ALU.mult))
                        ol(dve.reduce_sum(ovk[:, 4 * a:4 * a + 4], t3(otmp, NE), X_AXIS))
                    om = ometa.rearrange("p (k t c) -> p k t c", k=2, t=NT)
                    parts = small[:, 36:52].rearrange("p (t c) -> p t c", t=NT)
                    ol(dve.tensor_copy(om, parts.unsqueeze(1).broadcast_to([P, 2, NT, 4])))
                    ol(dve.memset(om[:, 1, :, 2], float(SEQ)))
                    ol(dve.memset(mcur, 0.0))
                    per, first = 12, ol.n
                    with dve.Fori(0, n) as j:
                        ol.n, ol.shift = first, j * per
                        for a in range(2):
                            for t in range(NT):
                                last = ts(over_picks[:, a, t, :], mats[:, 1, :], ovk[:, 4 * a + t:4 * a + t + 1], None,
                                          ALU.is_equal)
                        last.then_inc(m["o_pick"], 1)
                        m.wait(dve, "o_pick", 1, j, 1)
                        ol(ts(ovk, ovk, float(P), None, ALU.subtract))
                        here = otmp[:, 0:48]
                        ol(ts(here, src, mcur, None, ALU.is_equal))
                        ol(tt(here, here, ind, ALU.mult))
                        ol(tt(t3(here, NE), t3(here, NE), on4(20, NE, 3), ALU.mult))
                        ol(dve.reduce_sum(ocmp, here, X_AXIS))
                        ol(dve.tensor_copy(over_e_i, ocmp))
                        ol(ts(mcur, mcur, 1.0, None, ALU.add))
                        slots_to_rows(ol, m, "o_imm", "o_idx", ps[7], idx_f[:, 0:4], 1, curs[:, 4:5], curs[:, 5:6],
                                      idx_a[:, 0:1], j)
                        assert ol.n == first + per
                        m.wait(dve, "o_tr", 1, j, 2)
                        for half in range(2):
                            last = dve.tensor_copy(xgT[:, 0, 4 * half:4 * half + 4, :],
                                                   ps[2 + half][:, :].rearrange("p (k n) -> p k n", k=4))
                        last.then_inc(m["o_cp"], 1)
                        m.wait(dve, "o_silu", 1, j, 1)
                        m.wait(dve, "o_mm", 2, j, 3)
                        tt(hid, ps[1][:, :], sig, ALU.mult).then_inc(m["o_cp"], 1)
                        m.wait(dve, "o_tr", 2, j, 2)
                        dve.tensor_copy(hidT, ps[4][:, :].rearrange("p (k n) -> p k n", k=KE)).then_inc(m["o_cp"], 1)
                        m.wait(dve, "o_mm", 3, j, 3)
                        for half in range(2):
                            last = dve.tensor_copy(y_sb[:, 0, 512 * half:512 * (half + 1)], ps[5 + half][:, :])
                        last.then_inc(m["o_y"], 1)
                        m.wait(dve, "o_scat", 16, j, 16)

            def moe_norm(l):
                m = L[l]
                for t in range(NT):
                    par = t % 2
                    row = x_tok[:, t, :]
                    m.wait(dve, f"y_in{par}", 32 * (t // 2 + 1))
                    link(ts(yload[:, par, 0, :], yload[:, par, 0, :], g01[:, t:t + 1], None, ALU.mult))
                    link(stt(row, row, ALPHA, yload[:, par, 0, :], ALU.mult, ALU.add))
                    stt(row, yload[:, par, 1, :], g01[:, 4 + t:5 + t], row, ALU.mult, ALU.add).then_inc(m["y_used"], 1)
                    m.wait(dve, "y_used", t + 1)
                    if t == 0:
                        m.wait(dve, "lnp2_in", 32)
                    norm(t, m, "ln2_ve", "ln2_std", "ln2_done")

            def conv():
                link(dve.memset(upad, 0.0))
                dve.wait_ge(S["cvec_cp"], 1)
                for c in range(8):
                    u, acc = upad[:, c % 2, :], conv_o[:, c, :]
                    dve.wait_ge(S["gate_sig"], c + 1)
                    stt(u[:, PAD:PAD + SEQ], ps[c % 2][:, :], cvec[:, c:c + 1], gsig[:, c % 2, :], ALU.add, ALU.mult)\
                        .then_inc(S["u_ready"], 1)
                    dve.wait_ge(S["u_ready"], c + 1)
                    link(ts(acc, u[:, 0:SEQ], taps[:, c, 0:1], cvec[:, 16 + c:17 + c], ALU.mult, ALU.add))
                    for j in range(1, NTAP):
                        ins = stt(acc, u[:, j:j + SEQ], taps[:, c, j:j + 1], acc, ALU.mult, ALU.add)
                        if j < NTAP - 1:
                            link(ins)
                    ins.then_inc(S["conv_done"], 1)
                dve.wait_ge(S["csum_mm"], 1)
                link(ts(cmean, ps[4][:, :], 1.0 / D, None, ALU.mult))
                for c in range(8):
                    tt(conv_o[:, c, :], conv_o[:, c, :], cmean, ALU.subtract).then_inc(S["c_dev"], 1)
                dve.wait_ge(S["cvar_mm"], 8)
                ts(crstd, ps[5][:, :], 1.0 / D, LN_EPS, ALU.mult, ALU.add).then_inc(S["c_ve"], 1)
                dve.wait_ge(S["c_std"], 1)
                link(dve.reciprocal(crstd, crstd))
                for c in range(8):
                    tt(conv_o[:, c, :], conv_o[:, c, :], crstd, ALU.mult).then_inc(S["c_z"], 1)

            mixer(0)
            routing(0)
            experts(0)
            more_tiles(0)
            moe_norm(0)
            conv()
            mixer(1)
            routing(1)
            experts(1)
            more_tiles(1)
            moe_norm(1)

        @block.gpsimd
        def _(pool):
            link = Chain(pool, S["pool_chain"])

            for n in range(3):
                pool.wait_ge(S[f"row_out{n}"], 16 * (6 if n == 0 else 5))
            pool.dma_start(bias0, skewed(bias_d0, 127, [[W0 - 1, P], [P * W0, 4], [1, 384]])).then_inc(S["biases_in"], 16)
            pool.dma_start(bias12, skewed(bias_d12, 127, [[W1 - 1, P], [P * W1, 8], [1, P]])).then_inc(S["biases_in"], 16)
            for h in range(4):
                for r in range(8):
                    src = skewed(bias_dn, h * P * 15 * RW + r * (16 * 15 * RW - RW) + 7 * RW + 15,
                                 [[15 * RW - 1, 16], [RW, 8], [1, NX]])
                    pool.dma_start(bias_nr[16 * r:16 * (r + 1), h].rearrange("p (r x) -> p r x", r=8), src).then_inc(S["biases_in"], 16)

            for jp in range(2):
                pool.wait_ge(S["mg_min"], jp + 1)
                tt = pool.tensor_tensor
                over3 = den_b.unsqueeze(1).broadcast_to([P, 3, SEQ])
                tt(nmax_b, over3, nmax_b, ALU.subtract).then_inc(S["mg_diff"], 1)
                pool.wait_ge(S["mg_exp"], jp + 1)
                link(tt(sums_b, sums_b, nmax_b, ALU.mult))
                link(tt(den_b, sums_b[:, 0, :], sums_b[:, 1, :], ALU.add))
                tt(den_b, den_b, sums_b[:, 2, :], ALU.add).then_inc(S["mg_den"], 1)
                pool.wait_ge(S["mg_inv"], jp + 1)
                link(tt(nmax_b, nmax_b, over3, ALU.mult))
                heads = qT[:, jp:jp + 5:2, :]
                tt(heads, heads, nmax_b, ALU.mult).then_inc(S["mg_done"], 1)
                pool.wait_ge(S["mg_done"], jp + 1)

            def norm_params(g, b, done):
                pool.dma_start(ln_g, over_partitions(g)).then_inc(done, 16)
                pool.dma_start(ln_b, over_partitions(b)).then_inc(done, 16)

            pool.wait_ge(S["scores"], NU)
            norm_params(ln_mix_g[0], ln_mix_b[0], L[0]["lnp_in"])

            def moe(l):
                m = L[l]
                for t in range(NT):
                    m.wait(pool, "ln_done", t + 1)
                    pool.dma_start(xs[l][t * P:(t + 1) * P, :], x_tok[:, t, :]).then_inc(m["xs_st"], 16)
                norm_params(ln_ffn_g[l], ln_ffn_b[l], m["lnp2_in"])
                chain = Chain(pool, m["p_chain"])

                def column(tab, e, dst):
                    chain(pool.tensor_copy(dst, tab[:, e:e + 1] if isinstance(e, int) else tab[:, bass.ds(e, 1)]))

                def gather(e, at_e, i=None):
                    par = e % 2
                    if e >= 2:
                        m.wait(pool, "xt_mm", 2 * (e - 1), i, 4)
                        m.wait(pool, f"g_full{par}", 16 * (e // 2), i, 16)
                    column(idxg, at_e, curs[:, par:par + 1])
                    pool.sem_inc(S["passed"], 1)
                    pool.indirect_dma_start(
                        out=xg[:, par, :], out_offset=None, in_=xs[l],
                        in_offset=bass.IndirectOffsetOnAxis(ap=curs[:, par:par + 1], axis=0),
                        bounds_check=SEQ - 1, oob_is_err=False).then_inc(m[f"g_full{par}"], 16)

                def scatter(e, at_e, i=None):
                    par = e % 2
                    if e >= 2:
                        m.wait(pool, f"s_done{par}", 16 * (e // 2), i, 16)
                    column(idxs, at_e, curs[:, 2 + par:3 + par])
                    m.wait(pool, "y_cpA", e + 1, i, 2)
                    m.wait(pool, "y_cpV", e + 1, i, 2)
                    pool.sem_inc(S["passed"], 1)
                    pool.indirect_dma_start(
                        out=Y[l], out_offset=bass.IndirectOffsetOnAxis(ap=curs[:, 2 + par:3 + par], axis=0),
                        in_=y_sb[:, par, :], in_offset=None,
                        bounds_check=2 * SEQ - 1, oob_is_err=False).then_inc(m[f"s_done{par}"], 16)

                chain(pool.memset(xg, 0.0))
                m.wait(pool, "idx", 1)
                m.wait(pool, "xs_st", 16 * NT)
                gather(0, 0)
                gather(1, 1)
                for e in (0, 1):
                    gather(e + 2, e + 2)
                    scatter(e, e)
                per, first = 4, chain.n
                with pool.Fori(0, ROUNDS) as i:
                    chain.shift = i * per
                    for e in (2, 3):
                        gather(e + 2, i * 2 + (e + 2), i)
                        scatter(e, i * 2 + e, i)
                    assert chain.n == first + per
                chain.n, chain.shift = first + per * ROUNDS, None
                scatter(14, 14)
                scatter(15, 15)

                n = pool.value_load(nover_i[0:1, 0:1], min_val=0, max_val=NOVER)
                with pool.If(n > 0):
                    with pool.Fori(0, n) as j:
                        m.wait(pool, "o_idx", 1, j, 1)
                        pool.sem_inc(S["passed"], 1)
                        pool.indirect_dma_start(
                            out=xg[:, 0, :], out_offset=None, in_=xs[l],
                            in_offset=bass.IndirectOffsetOnAxis(ap=curs[:, 4:5], axis=0),
                            bounds_check=SEQ - 1, oob_is_err=False).then_inc(m["o_gath"], 16)
                        m.wait(pool, "o_y", 1, j, 1)
                        pool.sem_inc(S["passed"], 1)
                        pool.indirect_dma_start(
                            out=Y[l], out_offset=bass.IndirectOffsetOnAxis(ap=curs[:, 5:6], axis=0),
                            in_=y_sb[:, 0, :], in_offset=None,
                            bounds_check=2 * SEQ - 1, oob_is_err=False).then_inc(m["o_scat"], 16)
                        m.wait(pool, "o_scat", 16, j, 16)
                m.wait(pool, "s_done0", 16 * 8)
                m.wait(pool, "s_done1", 16 * 8)
                if l == 0:
                    pool.dma_start(crow[0:NTAP, :], w_dw[0]).then_inc(S["cvec_in"], 16)
                    at_row = 0
                    for v in (b_pw1, b_dw, conv_ln_g, conv_ln_b):
                        rows = v[0].rearrange("(r n) -> r n", n=P)
                        k = rows.shape[0]
                        pool.dma_start(vrow[at_row:at_row + k, :], rows).then_inc(S["cvec_in"], 16)
                        at_row += k
                for t in range(NT):
                    if t >= 2:
                        m.wait(pool, "y_used", t - 1)
                    for k in range(2):
                        pool.dma_start(yload[:, t % 2, k, :], Y[l][k * SEQ + t * P:k * SEQ + (t + 1) * P, :])\
                            .then_inc(m[f"y_in{t % 2}"], 16)
                if l == 0:
                    pool.dma_start(bpw2, over_partitions(b_pw2[0])).then_inc(S["bpw2_in"], 16)

            moe(0)
            L[0].wait(pool, "ln2_done", NT)
            norm_params(ln_mix_g[1], ln_mix_b[1], L[1]["lnp_in"])
            L[0].wait(pool, "xf2_mm", 2 * NT)
            pool.wait_ge(S["bpw2_in"], 16)
            for t in range(NT):
                link(pool.tensor_scalar(x_tok[:, t, :], x_tok[:, t, :], ALPHA, None, ALU.mult))
                pool.tensor_tensor(x_tok[:, t, :], x_tok[:, t, :], bpw2, ALU.add).then_inc(S["xres"], 1)
            moe(1)
            for t in range(NT):
                L[1].wait(pool, "ln2_done", t + 1)
                pool.dma_start(out[0].rearrange("(t p) d -> t p d", p=P)[t], x_tok[:, t, :]).then_inc(S["store_out"], 16)
            pool.wait_ge(S["store_out"], 16 * NT)


_INS = ['x', 'w_in_attn', 'w_out_attn', 'rel_bias', 'rpb_2d', 'w_pw1', 'b_pw1', 'w_dw', 'b_dw', 'conv_ln_g',
        'conv_ln_b', 'w_pw2', 'b_pw2', 'ln_mix_g', 'ln_mix_b', 'ln_ffn_g', 'ln_ffn_b', 'w_router', 'router_bias',
        'w_gate', 'w_up', 'w_down']


def kernel(**inputs):
    import numpy as _np
    import concourse.bacc as _bacc
    from concourse import mybir as _mybir
    from concourse.bass_utils import run_bass_kernel_spmd as _run

    nc = _bacc.Bacc("TRN2", target_bir_lowering=False, num_devices=1)
    arrays, args = {}, []
    consts = {"c_bucket": bucket_table(), "c_window": window_mask(), "c_small": small_table(), "c_mats": matrices()}
    for name in _INS + list(consts):
        a = _np.ascontiguousarray(inputs[name] if name in inputs else consts[name])
        arrays[f"in_{name}_dram"] = a
        args.append(nc.dram_tensor(f"in_{name}_dram", a.shape, _mybir.dt.from_np(a.dtype), kind="ExternalInput").ap())
    args.append(nc.dram_tensor("out_0_dram", (1, SEQ, D), _mybir.dt.float32, kind="ExternalOutput").ap())
    trunk(nc, *args)
    r = _run(nc, [arrays], core_ids=[0])
    return r.results[0]["out_0_dram"]
```

```python
import math
from contextlib import ExitStack

import numpy as np
import concourse.bass as bass
from concourse import mybir

F32 = mybir.dt.float32
BF16 = mybir.dt.bfloat16
I32 = mybir.dt.int32
ALU = mybir.AluOpType
ACT = mybir.ActivationFunctionType
X_AXIS = mybir.AxisListType.X

P = 128
D = 1024
SEQ = 512
NT = SEQ // P
KD = D // P
HD = 64
GRID_W = 64
NE = 16
NG = 4
EPG = NE // NG
DE = 512
KE = DE // P
NTAP = 31
PAD = NTAP // 2
NPE = [5] * 7 + [10]
ALPHA = 4 ** 0.25
LN_EPS = 1e-5
NEG = -1e30
SCALE = HD ** -0.5
SLOTS = 6
CH = 4096
NOVER = SEQ * 2 // P - 1
NB0 = 2 * NT - 1
RELW = 2 * P
NX = 48
RW = NX
HW = 16 * RW


def t5_bucket(rel):
    nb, max_exact = 16, 8
    n = abs(rel)
    big = max_exact + int(math.log(max(n, 1) / max_exact) / math.log(1024 / max_exact) * (nb - max_exact)) \
        if n >= max_exact else n
    return (nb if rel > 0 else 0) + min(big, nb - 1)


def bucket_table():
    t = np.zeros((33, NB0 + 2, RELW), np.float32)

    def put(block, col, rel, ok):
        if ok:
            t[t5_bucket(rel), block, col] = 1.0
        else:
            t[32, block, col] = NEG

    for col in range(RELW):
        d = col - 127
        for block in range(NB0):
            rel = NT * d + block - (NT - 1)
            put(block, col, rel, abs(rel) <= 64)
        put(NB0, col, 4 * d, abs(d) <= 64)
        put(NB0 + 1, col, 4 * d, d % 4 == 0)
    return t.reshape(33, -1)


def window_mask():
    m = np.full((P, 4, NX), NEG, np.float32)
    for q in range(P):
        for b in range(4):
            col = 16 * b + q % 16
            w0 = min(max(col - 8, 0), GRID_W - 16)
            for x in range(NX):
                if w0 <= 16 * (b - 1) + x < w0 + 16:
                    m[q, b, x] = 0.0
    return m


def small_table():
    t = np.zeros((P, 96), np.float32)
    t[:, 0:4] = [4, 3, 2, 1]
    t[:, 4:20] = np.tril(np.ones((4, 4)), -1).ravel()
    t[:, 20:36] = np.arange(NE)
    for tile in range(NT):
        t[:, 36 + 4 * tile] = np.arange(P)
        t[:, 37 + 4 * tile] = P * tile
        t[:, 39 + 4 * tile] = 1.0
    return t


def matrices():
    return np.stack([np.eye(P), np.triu(np.ones((P, P)), 1), np.tile(np.arange(1, P + 1), (P, 1))]).astype(np.float32)


class Chain:

    def __init__(self, eng, sem):
        self.eng, self.sem, self.n, self.shift = eng, sem, 0, None

    def __call__(self, ins):
        self.n += 1
        ins.then_inc(self.sem, 1)
        self.eng.wait_ge(self.sem, self.n if self.shift is None else self.shift + self.n)


def trunk(nc, x, w_in_attn, w_out_attn, rel_bias, rpb_2d, w_pw1, b_pw1, w_dw, b_dw, conv_ln_g,
          conv_ln_b, w_pw2, b_pw2, ln_mix_g, ln_mix_b, ln_ffn_g, ln_ffn_b, w_router, router_bias,
          w_gate, w_up, w_down, c_bucket, c_window, c_small, c_mats, out):
    ctx = ExitStack()
    with ctx:
        def sb(name, shape, dt=F32):
            return ctx.enter_context(nc.sbuf_tensor(name, shape, dt))

        def sem(name):
            return ctx.enter_context(nc.semaphore(name))

        ring = sb("ring", [P, SLOTS, CH])
        x_tok = sb("x_tok", [P, NT, D])
        x_feat = sb("x_feat", [P, KD, SEQ])
        K4 = 1024
        arena = sb("arena", [P, 73 * 256])

        def at(kib, n):
            return arena[:, kib * 256:kib * 256 + n]

        qT = at(0, 4096).rearrange("p (r n) -> p r n", r=8)
        kT = at(16, 4096).rearrange("p (r n) -> p r n", r=8)
        vt = at(32, NT * 768).rearrange("p (t n) -> p t n", t=NT)
        vt3 = at(44, NT * 256).rearrange("p (t n) -> p t n", t=NT)
        vgT = at(44, 2 * 512).rearrange("p (b n) -> p b n", b=2)
        bias = at(48, (4 * NB0 + 8) * P)
        bias0 = bias[:, 0:4 * NB0 * P].rearrange("p (h n) -> p h n", h=4)
        bias12 = bias[:, 4 * NB0 * P:].rearrange("p (h n) -> p h n", h=4)
        bias_n = at(66, 4 * 384).rearrange("p (h n) -> p h n", h=4)
        bucket_sb = at(32, (NB0 + 2) * RELW)
        rel_rows = at(62, (NB0 + 2) * RELW)
        rpb_row = at(48, 4 * HW)
        work = x_tok.rearrange("p t n -> p (t n)")
        probs = work[:, 0:4 * 768].rearrange("p (b n) -> p b n", b=4)
        probsT = work[:, 3072:3072 + 2 * 384].rearrange("p (b n) -> p b n", b=2)
        bias_nr = work[:, 0:4 * 384].rearrange("p (h n) -> p h n", h=4)
        x_res = at(16, 4096).rearrange("p (t n) -> p t n", t=NT)
        ln_g0 = at(48, D)
        ln_b0 = at(52, D)
        ln_g = at(16, D)
        ln_b = at(20, D)
        xg = at(24, 2 * D).rearrange("p (b n) -> p b n", b=2)
        xgT = at(32, 2 * D).rearrange("p (b k n) -> p b k n", b=2, k=KD)
        y_sb = at(40, 2 * D).rearrange("p (b n) -> p b n", b=2)
        hid = at(48, DE)
        sig = at(50, DE)
        hidT = at(52, DE).rearrange("p (k n) -> p k n", k=KE)
        picks = at(0, 4096).bitcast(BF16).rearrange("p (t e n) -> p t e n", t=NT, e=NE)
        over_w = at(0, 4096)
        over_picks = at(54, 512).bitcast(BF16).rearrange("p (a t n) -> p a t n", a=2, t=NT)
        yload = [at(kib, 2 * D).rearrange("p (k n) -> p k n", k=2) for kib in (24, 32, 0, 8)]
        rsm = at(56, 16 * 256)
        conv_o = at(0, 4096).rearrange("p (c n) -> p c n", c=8)
        NPAD = SEQ + 2 * PAD
        upad = at(24, 3 * 544).rearrange("p (b n) -> p b n", b=3)
        gsig = at(31, 2 * 512).rearrange("p (b n) -> p b n", b=2)
        diag = at(63, 2 * max(NPE) * P).rearrange("p (b j n) -> p b j n", b=2, j=max(NPE))
        csq = at(24, 2 * 512).rearrange("p (b n) -> p b n", b=2)
        cmean = at(37, 512)
        crstd = at(39, 512)
        taps = at(41, 8 * 32).rearrange("p (c n) -> p c n", c=8)
        cvec = at(42, 64)
        crow = at(43, 1024)
        vrow = at(47, P)
        odd_taps = at(48, 512)
        bpw2 = at(52, D)

        ident = sb("ident", [P, P])
        ones = sb("ones", [P, P])
        mats = sb("mats", [P, 2, P])
        before_bf = sb("before_bf", [P, P], BF16)
        ones_bf = sb("ones_bf", [P, P], BF16)
        slot_bf = sb("slot_bf", [P, P], BF16)
        small = sb("small", [P, 96])
        window = sb("window", [P, 4, NX])
        nmax = sb("nmax", [P, 64])
        psum_e = sb("psum_e", [P, 64])
        rinv = sb("rinv", [P, 64])
        wr = sb("wr", [P, KD, NE])
        rb = sb("rb", [P, NE])
        mx = sb("mx", [P, 64])
        rel_sb = sb("rel_sb", [33, 12])
        stats = sb("stats", [P, NT, 2, 6])
        mv = sb("mv", [P, NT, 5])
        lnf = sb("lnf", [P, 2, KD])

        ps = [ctx.enter_context(nc.psum_tensor(f"ps{i}", [P, 512], F32)) for i in range(8)]

        bias_one = nc.dram_tensor("bias_one", [(4 * NB0 + 8) * RELW], F32).ap()
        bias_rep = nc.dram_tensor("bias_rep", [P, (4 * NB0 + 8) * RELW], F32).ap()
        bias_dn = nc.dram_tensor("bias_dn", [16, 4 * HW], F32).ap()
        xs = [nc.dram_tensor(f"xs{n}", [SEQ, D], F32).ap() for n in range(2)]
        Y = [nc.dram_tensor(f"Y{n}", [2 * SEQ, D], F32).ap() for n in range(2)]

        def pk(w):
            return w.rearrange("(p k) n -> p k n", p=P)

        def kp(w):
            return w.rearrange("(k p) n -> p k n", p=P)

        ATT = 0
        MOE = [8, 8 + 48 + 6]
        CONV = 8 + 48


        w_full = [sem(f"w_full{s}") for s in range(SLOTS)]
        w_free = [sem(f"w_free{s}") for s in range(SLOTS)]

        def slot(c, kk=KD):
            return ring[:, c % SLOTS, :].rearrange("p (k n) -> p k n", k=kk)

        def filled(eng, c, i=None):
            v = 16 * (c // SLOTS + 1)
            eng.wait_ge(w_full[c % SLOTS], v if i is None else i * 16 + v)

        S = {n: sem(n) for n in (
            "x_in", "consts", "bucket_in", "rel_in", "rpb_in", "router_in", "preset", "bf_ready",
            "row_mm", "row_cp", "row_out", "row_rep", "rpb_out", "bias_in", "bias_n", "biases_in", "xf0_mm", "xf0_cp",
            "vg_mm", "vg_cp", "proj_mm", "proj_cpA", "proj_cpV", "scores", "sc_read", "nmax", "probs", "pnorm", "pT", "pT_cp",
            "pv", "evac", "res_in",
            "dve_chain", "pool_chain", "cvec_in", "cvec_mm", "cvec_cp", "pw1_mm", "gate_sig",
            "u_ready", "conv_done", "out_gain", "out_ready", "lnf_in", "csum_mm", "c_dev", "c_sq", "cvar_mm", "c_ve", "c_std",
            "c_z", "c_act", "diag", "side_mm", "tap", "bpw2_in", "xres", "store_out", "act_chain", "passed")}
        PER_LAYER = {
            "mo_mm": 8, "mo_read": 8, "ln_ve": NT, "ln_std": NT, "ln_done": NT, "xf_mm": 8, "xf_cp": 8, "lnp_in": 32,
            "xs_st": 16 * NT, "lnp2_in": 32, "logit_mm": NT, "score": 1, "mask": 1, "pos_mm": 1, "picks": NG,
            "idx_mm": NG, "idx": 2, "nover": 1, "g_full0": 128, "g_full1": 128, "s_done0": 128, "s_done1": 128,
            "xt_mm": 32, "xt_cpA": 16, "xt_cpV": 16, "gu_mm": 32, "silu": 16, "hid": 16, "ht_mm": 16, "ht_cp": 16,
            "dn_mm": 32, "y_cpA": 16, "y_cpV": 16, "y_in0": 32, "y_in1": 32, "y_in2": 32, "y_in3": 32,
            "x_scaled": NT, "y_all": 1, "ln2_rs": NT, "ln2_z": NT, "ln2_ve": NT,
            "ln2_std": NT, "xf2_mm": 8, "xf2_cp": 8}
        shared = {n: sem(n) for n in PER_LAYER}
        OWN = ("o_pick", "o_imm", "o_idx", "o_gath", "o_w", "o_mm", "o_tr", "o_silu", "o_cp", "o_scat", "o_chain",
               "o_y", "p_chain")

        class Layer:

            def __init__(self, l):
                self.l = l
                self.own = {n: sem(f"{n}_{l}") for n in OWN}

            def __getitem__(self, name):
                return self.own[name] if name in self.own else shared[name]

            def value(self, name, v):
                return v if name in self.own else v + self.l * PER_LAYER[name]

            def wait(self, eng, name, v, i=None, k=0):
                v = self.value(name, v)
                eng.wait_ge(self[name], v if i is None else i * k + v)

        L = [Layer(l) for l in range(2)]

        class First(Layer):

            def __init__(self):
                self.own = S

        FIRST = First()


        def in_tiles(v, pair):
            if pair < 6:
                return v.rearrange("p (i t) -> p t i", t=4)
            return v.rearrange("p (r b c) -> p b r c", r=8, c=16)

        def tiles_of(v, pair):
            if pair < 6:
                return v.rearrange("p (t i) -> p t i", t=4)
            return v.rearrange("p (b r c) -> p b r c", r=8, c=16)

        def tokens(v, t):
            return v[:, t::4]

        def grid_tiles(t):
            return [b for b in (t - 1, t, t + 1) if 0 <= b < NT]

        UNITS = [(kind, 2 * jp + par, t) for kind in ("dilated", "grid") for jp in range(2)
                 for t in range(NT) for par in range(2)]
        NU = len(UNITS)
        LAG = 2

        def key_blocks(u):
            kind, j, t = UNITS[u]
            return NT + 2 if kind == "dilated" else len(grid_tiles(t))

        PARTS = [(u, b, min(b + 3, key_blocks(u))) for u in range(NU) for b in range(0, key_blocks(u), 3)]
        PART_END = {u: n + 1 for n, (u, _, _) in enumerate(PARTS)}

        def parts_of(u):
            return [n for n, part in enumerate(PARTS) if part[0] == u]

        ITEMS = []
        for c, cols in enumerate([[("q", p) for p in range(4)], [("q", 4), ("q", 5), ("k", 0), ("k", 1)],
                                  [("k", p) for p in range(2, 6)]]):
            ITEMS += [(kind, p, c, P * i) for i, (kind, p) in enumerate(cols)]
        ITEMS += [("v", t, 3, 0) for t in range(NT)]
        ITEMS += [("v2", a, 4, 0) for a in range(2)] + [("q", 6, 4, 256), ("q", 7, 4, 384)]
        ITEMS += [("vT", 0, 5, 256), ("vT", 1, 5, 384), ("k", 6, 5, 0), ("k", 7, 5, P)]
        NI = len(ITEMS)

        off = [0]

        def small_buf(n, dt=F32):
            v = rsm[:, off[0]:off[0] + n]
            off[0] += n
            return v if dt == F32 else v.bitcast(dt)

        def t3(v, b):
            return v.rearrange("p (a b) -> p a b", b=b)

        scores_s, sel, pairsum = small_buf(64), small_buf(64), small_buf(96)
        gtop, gmax, geq = small_buf(16), small_buf(4), small_buf(16)
        gone = small_buf(16)
        selw, v4 = small_buf(64), small_buf(16)
        beats, ties, rank = small_buf(64), small_buf(64), small_buf(16)
        r0, r1 = small_buf(16), small_buf(16)
        m0, m1, msk = small_buf(64), small_buf(64), small_buf(64)
        mtmp = small_buf(64)
        g01 = small_buf(8)
        gden = small_buf(4)
        posm = small_buf(64)
        pos_bf = small_buf(32, BF16)
        msk_bf = small_buf(32, BF16)
        meta = small_buf(2 * NT * NE, BF16)
        idx_f = small_buf(4 * NE)
        idx_a = small_buf(NE)
        idxg = small_buf(NE, I32)
        idxs = small_buf(NE, I32)
        curs = small_buf(8, I32)
        cnt = small_buf(NE)
        ind = small_buf(48)
        cum = small_buf(48)
        cum2 = small_buf(48)
        over = small_buf(64)
        otmp = small_buf(64)
        ovk = small_buf(8)
        mcur = small_buf(1)
        nov_f = small_buf(1)
        nover_i = small_buf(1, I32)
        over_e_i = small_buf(1, I32)
        ocmp = small_buf(1)
        ometa = small_buf(16, BF16)
        assert off[0] <= 7 * 256, off[0]

        def on4(c0, n, reps):
            return small[:, c0:c0 + n].unsqueeze(1).broadcast_to([P, reps, n])

        def over_partitions(v):
            return bass.AP(tensor=v.tensor, offset=v.offset, ap=[[0, P], [1, v.shape[-1]]])

        def skewed(v, start, pattern):
            return bass.AP(tensor=v.tensor, offset=v.offset + start, ap=pattern)

        def item_views(n):
            kind, what = ITEMS[n][:2]
            bank = ps[n % 4][:, :]
            if kind == "v":
                return vt[:, what, 0:512], bank
            if kind == "v2":
                return vt[:, 2 * what:2 * what + 2, 512:768], bank.rearrange("p (t n) -> p t n", t=2)
            pair = what + 6 if kind == "vT" else what
            return tiles_of({"q": qT, "k": kT, "vT": vgT}[kind][:, what, :], pair), in_tiles(bank, pair)

        ITEM_END = {c: max(n for n, it in enumerate(ITEMS) if it[2] == c) + 1 for c in range(6)}

        def reader_done(c):
            if c < 6:
                return S["proj_mm"], ITEM_END[c]
            if c < 8:
                return L[0]["mo_mm"], L[0].value("mo_mm", 7 + c - 6)
            if CONV <= c < CONV + 4:
                return S["pw1_mm"], (7, 8, 15, 16)[c - CONV]
            if CONV + 4 <= c < CONV + 6:
                return L[1]["mo_mm"], L[1].value("mo_mm", 7 + c - CONV - 4)
            l = 0 if c < CONV else 1
            p = c - MOE[l]
            if p < 2:
                name, v = "gu_mm", p + 1
            elif p == 47:
                name, v = "dn_mm", 32
            else:
                n, which = divmod(p - 2, 3)
                name, v = ("dn_mm", 2 * n + 2) if which == 2 else ("gu_mm", 2 * (n + 1) + which + 1)
            return L[l][name], L[l].value(name, v)

        def load(sp, c, src, kk=KD):
            if c >= SLOTS:
                sp.wait_ge(*reader_done(c - SLOTS))
            sp.dma_start(slot(c, kk), src).then_inc(w_full[c % SLOTS], 16)

        NROW = -(-(NB0 + 2) * RELW // 512)
        ROUNDS = 6

        block = ctx.enter_context(nc.Block())

        @block.sync
        def _(sp):
            sp.dma_start(x_tok[:, :, :], x[0].rearrange("(t p) d -> p t d", p=P)).then_inc(S["x_in"], 16)
            for c in range(6):
                load(sp, c, pk(w_in_attn[0])[:, :, c * 512:(c + 1) * 512])
            for c in range(2):
                load(sp, 6 + c, kp(w_out_attn[0])[:, :, c * 512:(c + 1) * 512])

            def experts(l):
                m, base = L[l], MOE[l]

                def expert_w(e, which):
                    w = (w_gate, w_up, w_down)[which][l]
                    src = w[e] if isinstance(e, int) else w[bass.ds(e, 1)].rearrange("o a n -> (o a) n")
                    return kp(src) if which == 2 else pk(src)

                load(sp, base, expert_w(0, 0))
                load(sp, base + 1, expert_w(0, 1))
                for n in range(2):
                    load(sp, base + 2 + 3 * n, expert_w(n + 1, 0))
                    load(sp, base + 3 + 3 * n, expert_w(n + 1, 1))
                    load(sp, base + 4 + 3 * n, expert_w(n, 2), KE)
                with sp.Fori(0, ROUNDS) as i:
                    for u in range(2):
                        n = 2 + u
                        for which in range(3):
                            c = base + 2 + 3 * n + which
                            if which == 2:
                                m.wait(sp, "dn_mm", 2 * (n - 2) + 2, i, 4)
                            else:
                                m.wait(sp, "gu_mm", 2 * (n - 1) + which + 1, i, 4)
                            e = i * 2 + (n if which == 2 else n + 1)
                            sp.dma_start(slot(c, KE if which == 2 else KD), expert_w(e, which))\
                              .then_inc(w_full[c % SLOTS], 16)
                load(sp, base + 44, expert_w(15, 0))
                load(sp, base + 45, expert_w(15, 1))
                load(sp, base + 46, expert_w(14, 2), KE)
                load(sp, base + 47, expert_w(15, 2), KE)
                m.wait(sp, "nover", 1)
                n = sp.value_load(nover_i[0:1, 0:1], min_val=0, max_val=NOVER)
                with sp.If(n > 0):
                    with sp.Fori(0, n) as j:
                        m.wait(sp, "o_idx", 1, j, 1)
                        sp.sem_inc(S["passed"], 1)
                        e = sp.value_load(over_e_i[0:1, 0:1], min_val=0, max_val=NE - 1)
                        for which in range(3):
                            if which:
                                m.wait(sp, "o_mm", which, j, 3)
                            dst = over_w.rearrange("p (k n) -> p k n", k=KE if which == 2 else KD)
                            sp.dma_start(dst, expert_w(e, which)).then_inc(m["o_w"], 16)

            experts(0)
            for c, col in enumerate((0, 1024, 512, 1536)):
                load(sp, CONV + c, pk(w_pw1[0])[:, :, col:col + 512])
            for c in range(2):
                load(sp, CONV + 4 + c, kp(w_pw2[0])[:, :, c * 512:(c + 1) * 512])
            experts(1)
            for t in range(NT):
                sp.wait_ge(S["out_ready"], t + 1)
                sp.dma_start(out[0].rearrange("(t p) d -> t p d", p=P)[t], x_tok[:, t, :]).then_inc(S["store_out"], 16)
            sp.wait_ge(S["store_out"], 16 * NT)

        @block.tensor
        def _(pe):
            def mm(out_, lhsT, rhs, first=True, last=True):
                return pe.matmul(out_, lhsT, rhs, start=first, stop=last)

            def to_features(t, m, mm_sem, cp_sem):
                for half in range(2):
                    n = 2 * t + half
                    if n >= 2:
                        m.wait(pe, cp_sem, n - 1)
                    for k in range(4):
                        ins = pe.transpose(ps[6 + half][:, k * P:(k + 1) * P],
                                           x_tok[:, t, 4 * half + k::8], ident[:, :])
                    ins.then_inc(m[mm_sem], 1)

            pe.wait_ge(S["x_in"], 16)
            pe.wait_ge(S["consts"], 16)
            for t in range(NT):
                to_features(t, FIRST, "xf0_mm", "xf0_cp")

            pe.wait_ge(S["bucket_in"], 16)
            pe.wait_ge(S["rel_in"], 16)
            for n in range(NROW):
                if n >= 2:
                    pe.wait_ge(S["row_cp"], n - 1)
                c0, c1 = 512 * n, min(512 * (n + 1), (NB0 + 2) * RELW)
                mm(ps[n % 2][0:12, 0:c1 - c0], rel_sb[:, :], bucket_sb[0:33, c0:c1]).then_inc(S["row_mm"], 1)
            pe.wait_ge(S["xf0_cp"], 2 * NT)
            pe.wait_ge(S["row_cp"], NROW)

            def copied(n):
                pe.wait_ge(S["proj_cpA" if n % 2 == 0 else "proj_cpV"], n // 2 + 1)

            for n, (kind, what, c, col) in enumerate(ITEMS):
                if n == 0 or ITEMS[n - 1][2] != c:
                    filled(pe, c)
                if n >= 4:
                    copied(n - 4)
                w, bank = slot(c), ps[n % 4]
                if kind == "v":
                    for k in range(KD):
                        ins = mm(bank[:, :], tokens(x_feat[:, k, :], what), w[:, k, 0:512], k == 0, k == KD - 1)
                elif kind == "v2":
                    for half in range(2):
                        for k in range(KD):
                            ins = mm(bank[:, 256 * half:256 * (half + 1)], tokens(x_feat[:, k, :], 2 * what + half),
                                     w[:, k, 0:256], k == 0, k == KD - 1)
                else:
                    for k in range(KD):
                        ins = mm(bank[:, :], w[:, k, col:col + P], x_feat[:, k, :], k == 0, k == KD - 1)
                ins.then_inc(S["proj_mm"], 1)
            copied(NI - 4)
            copied(NI - 3)
            for pr in range(2):
                for t in range(NT):
                    ins = pe.transpose(ps[4 + pr][:, t * P:(t + 1) * P], vgT[:, pr, t * P:(t + 1) * P], ident[:, :])
                ins.then_inc(S["vg_mm"], 1)
            copied(NI - 2)
            copied(NI - 1)

            def scores(u):
                kind, j, t = UNITS[u]
                jp, lo = j // 2, HD * (j % 2)
                if u >= 2:
                    pe.wait_ge(S["sc_read"], u - 1)
                bank = 2 * (u % 2)

                def q(pair):
                    return qT[lo:lo + HD, pair, t * P:(t + 1) * P]

                if kind == "dilated":
                    mm(ps[bank][:, :], q(jp), kT[lo:lo + HD, jp, :])
                    for g in (1, 2):
                        ins = mm(ps[bank + 1][:, (g - 1) * P:g * P], q(2 * g + jp), kT[lo:lo + HD, 2 * g + jp, t * P:(t + 1) * P])
                else:
                    b = grid_tiles(t)
                    ins = mm(ps[bank][:, 0:len(b) * P], q(6 + jp), kT[lo:lo + HD, 6 + jp, b[0] * P:(b[-1] + 1) * P])
                ins.then_inc(S["scores"], 1)

            def transposes(n):
                u, b0, b1 = PARTS[n]
                if b0 == 0:
                    pe.wait_ge(S["pnorm"], u + 1)
                if n >= 2:
                    pe.wait_ge(S["pT_cp"], n - 1)
                for b in range(b0, b1):
                    ins = pe.transpose(ps[4 + n % 2][:, P * (b - b0):P * (b - b0 + 1)], probs[:, u % 4, P * b:P * (b + 1)],
                                       ident[:, :])
                ins.then_inc(S["pT"], 1)

            def values(n):
                u, b0, b1 = PARTS[n]
                kind, j, t = UNITS[u]
                e, lo = u // 2, HD * (j % 2)
                pe.wait_ge(S["pT_cp"], n + 1)
                if u % 2 == 0 and b0 == 0 and e >= 2:
                    pe.wait_ge(S["evac"], e - 1)
                for b in range(b0, b1):
                    if kind == "dilated":
                        g = max(0, b - NT + 1)
                        tile = b if g == 0 else t
                        v = vt[:, tile, 256 * g + HD * j:256 * g + HD * (j + 1)]
                        first, last = (b == 0, b == NT - 1) if g == 0 else (True, True)
                    else:
                        g = 0
                        v = vt3[:, grid_tiles(t)[b], HD * j:HD * (j + 1)]
                        first, last = b == 0, b == b1 - 1
                    ins = mm(ps[6 + e % 2][lo:lo + HD, g * P:(g + 1) * P], v, probsT[:, n % 2, P * (b - b0):P * (b - b0 + 1)],
                             first, last)
                ins.then_inc(S["pv"], 1)

            for step in range(NU + LAG):
                if step < NU:
                    scores(step)
                if step >= LAG:
                    for n in parts_of(step - LAG):
                        if n == 0:
                            pe.wait_ge(S["vg_cp"], 2)
                        transposes(n)
                        if n >= 1:
                            values(n - 1)
            values(len(PARTS) - 1)

            def mixer_out(l, src, c0, ready):
                m = L[l]

                def logits(t):
                    m.wait(pe, "xf_cp", 2 * t + 2)
                    for k in range(KD):
                        ins = mm(ps[5][:, t * NE:(t + 1) * NE], x_feat[:, k, t * P:(t + 1) * P], wr[:, k, :],
                                 k == 0, k == KD - 1)
                    ins.then_inc(m["logit_mm"], 1)

                for t in range(NT):
                    for half in range(2):
                        if t == 0:
                            filled(pe, c0 + half)
                        n = 2 * t + half
                        if n >= 4:
                            m.wait(pe, "mo_read", n - 3)
                        for k in range(KD):
                            if n == 0:
                                ready(k)
                            ins = mm(ps[n % 4][:, :], src(k, t), slot(c0 + half)[:, k, :], k == 0, k == KD - 1)
                        ins.then_inc(m["mo_mm"], 1)
                    if t >= 1:
                        m.wait(pe, "ln_done", t)
                        to_features(t - 1, m, "xf_mm", "xf_cp")
                if l == 0:
                    pe.wait_ge(S["router_in"], 32)
                for t in range(NT - 1):
                    logits(t)
                m.wait(pe, "ln_done", NT)
                to_features(NT - 1, m, "xf_mm", "xf_cp")
                logits(NT - 1)

            def routing(l):
                m = L[l]
                m.wait(pe, "mask", 1)
                mk = t3(msk_bf, NE)
                for t in range(NT):
                    for a in range(t):
                        mm(ps[0][:, t * NE:(t + 1) * NE], ones_bf[:, :], mk[:, a], a == 0, False)
                    mm(ps[0][:, t * NE:(t + 1) * NE], before_bf[:, :], mk[:, t], t == 0, True)
                for t in range(NT):
                    ins = mm(ps[0][:, 4 * NE:5 * NE], ones_bf[:, :], mk[:, t], t == 0, t == NT - 1)
                ins.then_inc(m["pos_mm"], 1)
                mt = meta.rearrange("p (t e c) -> p t e c", t=NT, e=NE)
                for g in range(NG):
                    m.wait(pe, "picks", g + 1)
                    for e in range(EPG * g, EPG * (g + 1)):
                        for t in range(NT):
                            ins = mm(ps[7 if g == 0 else 1][:, 4 * e:4 * e + 4], picks[:, t, e, :], mt[:, t, e, :], t == 0, t == NT - 1)
                    ins.then_inc(m["idx_mm"], 1)

            def experts(l):
                m, base = L[l], MOE[l]

                def rows_T(e, i=None):
                    par = e % 2
                    m.wait(pe, f"g_full{par}", 16 * (e // 2 + 1), i, 16)
                    if e > 0:
                        m.wait(pe, "xt_cpA", e, i, 2)
                        m.wait(pe, "xt_cpV", e, i, 2)
                    for half in range(2):
                        for k in range(4):
                            ins = pe.transpose(ps[2 + half][:, k * P:(k + 1) * P], xg[:, par, 4 * half + k::8], ident[:, :])
                        ins.then_inc(m["xt_mm"], 1)

                def gate_up(e, i=None):
                    m.wait(pe, "xt_cpA", e + 1, i, 2)
                    m.wait(pe, "xt_cpV", e + 1, i, 2)
                    if e > 0:
                        m.wait(pe, "hid", e, i, 2)
                    c = base + (3 * e - 1 if e else 0)
                    for half in range(2):
                        filled(pe, c + half, i)
                        for k in range(KD):
                            ins = mm(ps[half][:, :], xgT[:, e % 2, k, :], slot(c + half)[:, k, :], k == 0, k == KD - 1)
                        ins.then_inc(m["gu_mm"], 1)

                def hidden_T(e, i=None):
                    m.wait(pe, "hid", e + 1, i, 2)
                    for k in range(KE):
                        ins = pe.transpose(ps[4][:, k * P:(k + 1) * P], hid[:, k * P:(k + 1) * P], ident[:, :])
                    ins.then_inc(m["ht_mm"], 1)

                def down(e, i=None):
                    m.wait(pe, "ht_cp", e + 1, i, 2)
                    if e > 0:
                        m.wait(pe, "y_cpA", e, i, 2)
                        m.wait(pe, "y_cpV", e, i, 2)
                    c = base + (47 if e == 15 else 4 + 3 * e)
                    filled(pe, c, i)
                    for half in range(2):
                        for k in range(KE):
                            ins = mm(ps[5 + half][:, :], hidT[:, k, :], slot(c, KE)[:, k, half * 512:(half + 1) * 512],
                                     k == 0, k == KE - 1)
                        ins.then_inc(m["dn_mm"], 1)

                rows_T(0)
                gate_up(0)
                rows_T(1)
                hidden_T(0)
                gate_up(1)
                rows_T(2)
                down(0)
                hidden_T(1)
                with pe.Fori(0, ROUNDS) as i:
                    for e in (2, 3):
                        gate_up(e, i)
                        rows_T(e + 1, i)
                        down(e - 1, i)
                        hidden_T(e, i)
                gate_up(14)
                rows_T(15)
                down(13)
                hidden_T(14)
                gate_up(15)
                down(14)
                hidden_T(15)
                down(15)

            def more_tiles(l):
                m = L[l]
                m.wait(pe, "nover", 1)
                m.wait(pe, "y_cpA", NE)
                m.wait(pe, "y_cpV", NE)
                n = pe.value_load(nover_i[0:1, 0:1], min_val=0, max_val=NOVER)
                om = ometa.rearrange("p (k t c) -> p k t c", k=2, t=NT)
                with pe.If(n > 0):
                    with pe.Fori(0, n) as j:
                        m.wait(pe, "o_pick", 1, j, 1)
                        for a in range(2):
                            for t in range(NT):
                                ins = mm(ps[7][:, 0:4], over_picks[:, a, t, :], om[:, a, t, :], a + t == 0, a + t == NT)
                        ins.then_inc(m["o_imm"], 1)
                        m.wait(pe, "o_gath", 16, j, 16)
                        for k in range(KD):
                            ins = pe.transpose(ps[2 + k // 4][:, k % 4 * P:(k % 4 + 1) * P], xg[:, 0, k::8], ident[:, :])
                        ins.then_inc(m["o_tr"], 1)
                        m.wait(pe, "o_cp", 1, j, 3)
                        for half in range(2):
                            m.wait(pe, "o_w", 16 * (half + 1), j, 48)
                            for k in range(KD):
                                ins = mm(ps[half][:, :], xgT[:, 0, k, :], over_w.rearrange("p (k n) -> p k n", k=KD)[:, k, :],
                                         k == 0, k == KD - 1)
                            ins.then_inc(m["o_mm"], 1)
                        m.wait(pe, "o_cp", 2, j, 3)
                        for k in range(KE):
                            ins = pe.transpose(ps[4][:, k * P:(k + 1) * P], hid[:, k * P:(k + 1) * P], ident[:, :])
                        ins.then_inc(m["o_tr"], 1)
                        m.wait(pe, "o_cp", 3, j, 3)
                        m.wait(pe, "o_w", 48, j, 48)
                        for half in range(2):
                            for k in range(KE):
                                ins = mm(ps[5 + half][:, :], hidT[:, k, :],
                                         over_w.rearrange("p (k n) -> p k n", k=KE)[:, k, half * 512:(half + 1) * 512],
                                         k == 0, k == KE - 1)
                        ins.then_inc(m["o_mm"], 1)

            def conv():
                for t in range(NT):
                    L[0].wait(pe, "ln2_z", t + 1)
                    to_features(t, L[0], "xf2_mm", "xf2_cp")
                pe.wait_ge(S["cvec_in"], 16 * 5)
                pe.transpose(ps[4][:, 0:40], vrow[0:40, :], ident[0:40, 0:40])
                for c in range(8):
                    ins = pe.transpose(ps[5][:, c * 32:c * 32 + NTAP], crow[0:NTAP, c * P:(c + 1) * P], ident[0:NTAP, 0:NTAP])
                ins.then_inc(S["cvec_mm"], 1)
                L[0].wait(pe, "xf2_cp", 2 * NT)

                def side_taps(c):
                    pe.wait_ge(S["u_ready"], c + 1)
                    pe.wait_ge(S["diag"], c + 1)
                    if c >= 2:
                        pe.wait_ge(S["conv_done"], c - 1)
                    for j in range(NPE[c]):
                        tap = NTAP - NPE[c] + j
                        ins = mm(ps[6 + c % 2][:, :], diag[:, c % 2, j, :], upad[:, c % 3, tap:tap + SEQ],
                                 j == 0, j == NPE[c] - 1)
                    ins.then_inc(S["side_mm"], 1)

                for c in range(8):
                    for gate in range(2):
                        ch = CONV + 2 * (c // 4) + gate
                        if c % 4 == 0:
                            filled(pe, ch)
                        if c >= 2:
                            pe.wait_ge(S["u_ready"], c - 1)
                        for k in range(KD):
                            ins = mm(ps[2 * gate + c % 2][:, :], slot(ch)[:, k, (c % 4) * P:(c % 4 + 1) * P], x_feat[:, k, :],
                                     k == 0, k == KD - 1)
                        ins.then_inc(S["pw1_mm"], 1)
                    if c >= 1:
                        side_taps(c - 1)
                side_taps(7)
                for c in range(8):
                    pe.wait_ge(S["conv_done"], c + 1)
                    ins = mm(ps[4][:, :], ones[:, :], conv_o[:, c, :], c == 0, c == 7)
                ins.then_inc(S["csum_mm"], 1)
                for c in range(8):
                    pe.wait_ge(S["c_sq"], c + 1)
                    mm(ps[5][:, :], ones[:, :], csq[:, c % 2, :], c == 0, c == 7).then_inc(S["cvar_mm"], 1)

            pe.wait_ge(S["evac"], NU // 2)
            mixer_out(0, lambda k, t: x_feat[:, k, t * P:(t + 1) * P], 6, lambda k: None)
            routing(0)
            experts(0)
            more_tiles(0)
            conv()
            mixer_out(1, lambda k, t: conv_o[:, k, t * P:(t + 1) * P], CONV + 4,
                      lambda k: pe.wait_ge(S["c_act"], k + 1))
            routing(1)
            experts(1)
            more_tiles(1)

        @block.scalar
        def _(act):
            def copy(out_, in_):
                return act.activation(out_, in_, ACT.Copy)

            act.dma_start(ident[:, :], c_mats[0]).then_inc(S["consts"], 16)
            act.wait_ge(S["preset"], 1)
            act.dma_start(rel_sb[0:32, :], rel_bias).then_inc(S["rel_in"], 16)
            act.dma_start(bucket_sb[0:33, :], c_bucket).then_inc(S["bucket_in"], 16)

            def features_copy(t, m, mm_sem, cp_sem):
                for half in range(2):
                    m.wait(act, mm_sem, 2 * t + half + 1)
                    copy(x_feat[:, 4 * half:4 * half + 4, t * P:(t + 1) * P],
                         ps[6 + half][:, :].rearrange("p (k n) -> p k n", k=4)).then_inc(m[cp_sem], 1)

            for t in range(NT):
                features_copy(t, FIRST, "xf0_mm", "xf0_cp")
            for n in range(NROW):
                act.wait_ge(S["row_mm"], n + 1)
                c0, c1 = 512 * n, min(512 * (n + 1), (NB0 + 2) * RELW)
                copy(rel_rows[0:12, c0:c1], ps[n % 2][0:12, 0:c1 - c0]).then_inc(S["row_cp"], 1)
            act.wait_ge(S["row_cp"], NROW)
            w0 = NB0 * RELW
            act.dma_start(bias_one[0:4 * w0].rearrange("(h n) -> h n", h=4), rel_rows[0:4, 0:w0]).then_inc(S["row_out"], 16)
            both = bias_one[4 * w0:].rearrange("(h g n) -> h g n", g=2, n=RELW)
            for g in range(2):
                act.dma_start(both[:, g, :], rel_rows[4 * (g + 1):4 * (g + 2), w0 + g * RELW:w0 + (g + 1) * RELW])\
                   .then_inc(S["row_out"], 16)
            act.dma_start(mats[:, :, :], c_mats[1:3].rearrange("m p n -> p m n")).then_inc(S["consts"], 16)
            act.dma_start(small[:, :], c_small).then_inc(S["consts"], 16)
            act.dma_start(window[:, :, :], c_window).then_inc(S["bias_in"], 16)
            act.dma_start(wr[:, :, :], pk(w_router)).then_inc(S["router_in"], 16)
            act.dma_start(rb[:, :], over_partitions(router_bias)).then_inc(S["router_in"], 16)
            act.wait_ge(S["row_out"], 48)
            act.dma_start(bias_rep, over_partitions(bias_one)).then_inc(S["row_rep"], 16)

            for n in range(0, NI, 2):
                act.wait_ge(S["proj_mm"], n + 1)
                dst, src = item_views(n)
                act.activation(dst, src, ACT.Copy, scale=SCALE if ITEMS[n][0] == "q" else 1.0)\
                   .then_inc(S["proj_cpA"], 1)

            act.wait_ge(S["vg_mm"], 2)
            for pr in range(2):
                copy(vt3[:, :, P * pr:P * (pr + 1)], ps[4 + pr][:, :].rearrange("p (t n) -> p t n", t=NT))\
                    .then_inc(S["vg_cp"], 1)

            def part_copy(n):
                u, b0, b1 = PARTS[n]
                act.wait_ge(S["pT"], n + 1)
                if n >= 2:
                    act.wait_ge(S["pv"], n - 1)
                wid = P * (b1 - b0)
                copy(probsT[:, n % 2, 0:wid], ps[4 + n % 2][:, 0:wid]).then_inc(S["pT_cp"], 1)

            def exponentials(u):
                nk = P * key_blocks(u)
                act.wait_ge(S["nmax"], u + 1)
                act.activation(probs[:, u % 4, 0:nk], probs[:, u % 4, 0:nk], ACT.Exp, bias=nmax[:, u:u + 1],
                               accum_out=psum_e[:, u:u + 1]).then_inc(S["probs"], 1)

            def evacuate(e):
                act.wait_ge(S["pv"], PART_END[2 * e + 1])
                kind, j, t = UNITS[2 * e]
                if kind == "dilated":
                    dst = x_feat[:, j // 2:j // 2 + 5:2, t::4]
                    src = ps[6 + e % 2][:, 0:3 * P].rearrange("p (g i) -> p g i", g=3)
                else:
                    dst = in_tiles(x_feat[:, 6 + j // 2, :], 6)[:, t]
                    src = ps[6 + e % 2][:, 0:P].rearrange("p (r c) -> p r c", c=16)
                copy(dst, src).then_inc(S["evac"], 1)

            for step in range(NU + LAG + 1):
                parts = parts_of(step - LAG) if LAG <= step < NU + LAG else []
                if parts:
                    part_copy(parts[0])
                if step < NU:
                    exponentials(step)
                for n in parts[1:]:
                    part_copy(n)
                done = step - LAG - 1
                if done >= 0 and done % 2 == 1:
                    evacuate(done // 2)

            def root(m, ve, std, t):
                m.wait(act, ve, t + 1)
                act.activation(mv[:, t, 3:4], mv[:, t, 2:3], ACT.Sqrt).then_inc(m[std], 1)

            def mixer(l):
                m = L[l]
                for t in range(NT):
                    root(m, "ln_ve", "ln_std", t)
                    if t >= 1:
                        features_copy(t - 1, m, "xf_mm", "xf_cp")
                features_copy(NT - 1, m, "xf_mm", "xf_cp")
                m.wait(act, "logit_mm", NT)
                act.activation(scores_s, ps[5][:, 0:NT * NE], ACT.Sigmoid).then_inc(m["score"], 1)

            def experts(l):
                m = L[l]

                def rows_copy(e, i=None):
                    m.wait(act, "xt_mm", 2 * e + 1, i, 4)
                    if e >= 2:
                        m.wait(act, "gu_mm", 2 * (e - 1), i, 4)
                    copy(xgT[:, e % 2, 0:4, :], ps[2][:, :].rearrange("p (k n) -> p k n", k=4)).then_inc(m["xt_cpA"], 1)

                def silu(e, i=None):
                    m.wait(act, "gu_mm", 2 * e + 1, i, 4)
                    if e >= 1:
                        m.wait(act, "hid", e, i, 2)
                    act.activation(sig, ps[0][:, :], ACT.Silu).then_inc(m["silu"], 1)

                def hidden_copy(e, i=None):
                    m.wait(act, "ht_mm", e + 1, i, 2)
                    if e >= 1:
                        m.wait(act, "dn_mm", 2 * e, i, 4)
                    copy(hidT, ps[4][:, :].rearrange("p (k n) -> p k n", k=KE)).then_inc(m["ht_cp"], 1)

                def rows_out(e, i=None):
                    m.wait(act, "dn_mm", 2 * e + 1, i, 4)
                    if e >= 2:
                        m.wait(act, f"s_done{e % 2}", 16 * (e // 2), i, 16)
                    copy(y_sb[:, e % 2, 0:512], ps[5][:, :]).then_inc(m["y_cpA"], 1)

                m.wait(act, "xs_st", 16 * NT)
                m.wait(act, "xf_mm", 2 * NT)
                for t in range(NT):
                    act.activation(x_tok[:, t, :], x_tok[:, t, :], ACT.Copy, scale=ALPHA).then_inc(m["x_scaled"], 1)
                rows_copy(0)
                silu(0)
                rows_copy(1)
                hidden_copy(0)
                silu(1)
                rows_copy(2)
                rows_out(0)
                hidden_copy(1)
                silu(2)
                rows_copy(3)
                rows_out(1)
                hidden_copy(2)
                with act.Fori(0, ROUNDS - 1) as i:
                    for e in (3, 4):
                        silu(e, i)
                        rows_copy(e + 1, i)
                        rows_out(e - 1, i)
                        hidden_copy(e, i)
                for e in (13, 14):
                    silu(e)
                    rows_copy(e + 1)
                    rows_out(e - 1)
                    hidden_copy(e)
                silu(15)
                rows_out(14)
                hidden_copy(15)
                rows_out(15)

            def more_tiles(l):
                m = L[l]
                m.wait(act, "nover", 1)
                n = act.value_load(nover_i[0:1, 0:1], min_val=0, max_val=NOVER)
                with act.If(n > 0):
                    with act.Fori(0, n) as j:
                        m.wait(act, "o_mm", 1, j, 3)
                        act.activation(sig, ps[0][:, :], ACT.Silu).then_inc(m["o_silu"], 1)

            def moe_norm(l):
                m = L[l]
                m.wait(act, "y_all", 1)
                for t in range(NT):
                    for k in range(2):
                        act.dma_start(yload[t][:, k, :], Y[l][k * SEQ + t * P:k * SEQ + (t + 1) * P, :])\
                           .then_inc(m[f"y_in{t}"], 16)

                def features(t):
                    for half in range(2):
                        m.wait(act, "xf2_mm", 2 * t + half + 1)
                        for k in range(4 * half, 4 * half + 4):
                            ins = act.activation(x_feat[:, k, t * P:(t + 1) * P], ps[6 + half][:, (k % 4) * P:(k % 4 + 1) * P],
                                                 ACT.Identity, scale=lnf[:, 0, k:k + 1], bias=lnf[:, 1, k:k + 1])
                        ins.then_inc(m["xf2_cp"], 1)

                if l == 0:
                    act.wait_ge(S["lnf_in"], 32)
                for t in range(NT):
                    root(m, "ln2_ve", "ln2_std", t)
                    m.wait(act, "ln2_rs", t + 1)
                    act.activation(x_tok[:, t, :], x_tok[:, t, :], ACT.Identity, scale=mv[:, t, 2:3], bias=mv[:, t, 4:5])\
                       .then_inc(m["ln2_z"], 1)
                    if l == 0 and t >= 1:
                        features(t - 1)
                if l == 0:
                    features(NT - 1)

            def conv():
                act.wait_ge(S["cvec_mm"], 1)
                copy(cvec[:, 0:40], ps[4][:, 0:40]).then_inc(S["act_chain"], 1)
                copy(taps[:, :, 0:NTAP], ps[5][:, 0:256].rearrange("p (c n) -> p c n", c=8)[:, :, 0:NTAP])\
                    .then_inc(S["cvec_cp"], 1)
                act.wait_ge(S["act_chain"], 1)
                act.wait_ge(S["cvec_cp"], 1)

                def diagonals(c):
                    if c >= 2:
                        act.wait_ge(S["side_mm"], c - 1)
                    for j in range(NPE[c]):
                        tap = NTAP - NPE[c] + j
                        ins = act.activation(diag[:, c % 2, j, :], ident[:, :], ACT.Copy, scale=taps[:, c, tap:tap + 1])
                    ins.then_inc(S["diag"], 1)

                for c in range(8):
                    diagonals(c)
                    act.wait_ge(S["pw1_mm"], 2 * c + 2)
                    if c >= 2:
                        act.wait_ge(S["u_ready"], c - 1)
                    act.activation(gsig[:, c % 2, :], ps[2 + c % 2][:, :], ACT.Sigmoid, bias=cvec[:, 8 + c:9 + c])\
                        .then_inc(S["gate_sig"], 1)
                for c in range(8):
                    act.wait_ge(S["c_dev"], c + 1)
                    if c >= 2:
                        act.wait_ge(S["cvar_mm"], c - 1)
                    act.activation(csq[:, c % 2, :], conv_o[:, c, :], ACT.Square).then_inc(S["c_sq"], 1)
                act.wait_ge(S["c_ve"], 1)
                act.activation(crstd, crstd, ACT.Sqrt).then_inc(S["c_std"], 1)
                for c in range(8):
                    act.wait_ge(S["c_z"], c + 1)
                    act.activation(conv_o[:, c, :], conv_o[:, c, :], ACT.Silu, bias=cvec[:, 32 + c:33 + c],
                                   scale=cvec[:, 24 + c:25 + c]).then_inc(S["c_act"], 1)

            mixer(0)
            experts(0)
            more_tiles(0)
            moe_norm(0)
            conv()
            mixer(1)
            experts(1)
            more_tiles(1)
            moe_norm(1)

        @block.vector
        def _(dve):
            link = Chain(dve, S["dve_chain"])
            tt, ts, stt = dve.tensor_tensor, dve.tensor_scalar, dve.scalar_tensor_tensor

            dve.memset(rel_sb[:, :], 1.0).then_inc(S["preset"], 1)
            dve.memset(rpb_row[0:1, :], 0.0).then_inc(S["preset"], 1)
            dve.memset(ones[:, :], 1.0)
            dve.wait_ge(S["consts"], 48)
            dve.tensor_copy(before_bf[:, :], mats[:, 0, :])
            dve.tensor_copy(slot_bf[:, :], mats[:, 1, :])
            dve.memset(ones_bf[:, :], 1.0).then_inc(S["bf_ready"], 1)

            for n in range(1, NI, 2):
                dve.wait_ge(S["proj_mm"], n + 1)
                dst, src = item_views(n)
                if ITEMS[n][0] == "q":
                    ins = ts(dst, src, SCALE, None, ALU.mult)
                else:
                    ins = dve.tensor_copy(dst, src)
                ins.then_inc(S["proj_cpV"], 1)
            dve.wait_ge(S["biases_in"], 16 * 9)
            for h in range(4):
                ins = dve.tensor_copy(bias_n[:, h].rearrange("p (b r c) -> p b r c", b=3, c=16),
                                      bias_nr[:, h].rearrange("p (r b c) -> p b r c", b=3, c=16))
            ins.then_inc(S["bias_n"], 1)
            dve.wait_ge(S["bias_n"], 1)
            dve.wait_ge(S["bias_in"], 16)

            def biased(out_, raw, add, col):
                return dve.tensor_tensor_reduce(out_, raw, add, 1.0, -3e38, ALU.add, ALU.max, accum_out=mx[:, col:col + 1])

            def logits(u):
                kind, j, t = UNITS[u]
                bank = 2 * (u % 2)
                lg = probs[:, u % 4, :]
                if u >= 4:
                    dve.wait_ge(S["pT"], PART_END[u - 4])
                dve.wait_ge(S["scores"], u + 1)
                if kind == "dilated":
                    biased(lg[:, 0:512], ps[bank][:, :], bias0[:, j, (NT - 1 - t) * P:(2 * NT - 1 - t) * P], 2 * u)
                    biased(lg[:, 512:768], ps[bank + 1][:, 0:256], bias12[:, j, :], 2 * u + 1).then_inc(S["sc_read"], 1)
                    dve.wait_ge(S["sc_read"], u + 1)
                    dve.reduce_max(nmax[:, u:u + 1], mx[:, 2 * u:2 * u + 2], X_AXIS, negate=True).then_inc(S["nmax"], 1)
                else:
                    b = grid_tiles(t)
                    nk, x0 = P * len(b), b[0] - (t - 1)
                    win = window[:, t, 16 * x0:16 * (x0 + len(b))].rearrange("p (b c) -> p b c", c=16)
                    win = win.unsqueeze(2).broadcast_to([P, len(b), 8, 16])
                    tt(lg[:, 0:nk].rearrange("p (b r c) -> p b r c", r=8, c=16),
                       ps[bank][:, 0:nk].rearrange("p (b r c) -> p b r c", r=8, c=16), win, ALU.add).then_inc(S["sc_read"], 1)
                    dve.wait_ge(S["sc_read"], u + 1)
                    link(biased(lg[:, 0:nk], lg[:, 0:nk], bias_n[:, j, P * x0:P * x0 + nk], 2 * u))
                    ts(nmax[:, u:u + 1], mx[:, 2 * u:2 * u + 1], -1.0, None, ALU.mult).then_inc(S["nmax"], 1)

            def normalize(u):
                nk = P * key_blocks(u)
                dve.wait_ge(S["probs"], u + 1)
                link(dve.reciprocal(rinv[:, u:u + 1], psum_e[:, u:u + 1]))
                ts(probs[:, u % 4, 0:nk], probs[:, u % 4, 0:nk], rinv[:, u:u + 1], None, ALU.mult).then_inc(S["pnorm"], 1)

            for u in range(NU):
                logits(u)
                if u >= 1:
                    normalize(u - 1)
            normalize(NU - 1)

            def moments(t, row, m, ve):
                dve.bn_stats(stats[:, t, 0, :], row[:, 0:512])
                link(dve.bn_stats(stats[:, t, 1, :], row[:, 512:1024]))
                link(dve.bn_aggr(mv[:, t, 0:2], stats[:, t]))
                ts(mv[:, t, 2:3], mv[:, t, 1:2], LN_EPS, None, ALU.add).then_inc(m[ve], 1)

            def norm(t, m, ve, std, done, g=ln_g, b=ln_b):
                row = x_tok[:, t, :]
                moments(t, row, m, ve)
                m.wait(dve, std, t + 1)
                link(dve.reciprocal(mv[:, t, 2:3], mv[:, t, 3:4]))
                link(ts(row, row, mv[:, t, 0:1], mv[:, t, 2:3], ALU.subtract, ALU.mult))
                link(tt(row, row, g, ALU.mult))
                tt(row, row, b, ALU.add).then_inc(m[done], 1)
                m.wait(dve, done, t + 1)

            def mixer(l):
                m = L[l]
                if l == 1:
                    dve.wait_ge(S["xres"], NT)
                else:
                    dve.wait_ge(S["res_in"], 16)
                for t in range(NT):
                    for half in range(2):
                        n = 2 * t + half
                        m.wait(dve, "mo_mm", n + 1)
                        row = x_tok[:, t, 512 * half:512 * (half + 1)]
                        if l == 0:
                            stt(row, x_res[:, t, 512 * half:512 * (half + 1)], ALPHA, ps[n % 4][:, :], ALU.mult, ALU.add).then_inc(m["mo_read"], 1)
                        else:
                            tt(row, ps[n % 4][:, :], row, ALU.add).then_inc(m["mo_read"], 1)
                    m.wait(dve, "mo_read", 2 * t + 2)
                    if t == 0:
                        m.wait(dve, "lnp_in", 32)
                    norm(t, m, "ln_ve", "ln_std", "ln_done", *((ln_g0, ln_b0) if l == 0 else (ln_g, ln_b)))

            def routing(l):
                m = L[l]
                g4 = lambda v: v.rearrange("p (t g i) -> p t g i", t=NT, g=NG)
                pg = lambda v: v.rearrange("p (a i) -> p a i", i=EPG)
                mt = meta.rearrange("p (t e c) -> p t e c", t=NT, e=NE)
                parts = small[:, 36:52].rearrange("p (t c) -> p t c", t=NT)
                link(dve.tensor_copy(mt, parts.unsqueeze(2).broadcast_to([P, NT, NE, 4])))
                m.wait(dve, "score", 1)
                link(tt(t3(sel, NE), t3(scores_s, NE), rb[:, :].unsqueeze(1).broadcast_to([P, NT, NE]), ALU.add))
                a, q = pg(sel), t3(pairsum, 6)
                tt(q[:, :, 0:3], a[:, :, 0:3], a[:, :, 1:4], ALU.add)
                tt(q[:, :, 3:5], a[:, :, 0:2], a[:, :, 2:4], ALU.add)
                link(tt(q[:, :, 5:6], a[:, :, 0:1], a[:, :, 3:4], ALU.add))
                link(dve.reduce_max(gtop, q, X_AXIS))
                link(dve.reduce_max(gmax, t3(gtop, NG), X_AXIS))
                link(tt(t3(geq, NG), t3(gtop, NG), gmax.unsqueeze(2).broadcast_to([P, NT, NG]), ALU.is_equal))
                link(tt(t3(geq, NG), t3(geq, NG), on4(0, NG, NT), ALU.mult))
                link(dve.reduce_max(gmax, t3(geq, NG), X_AXIS))
                link(tt(t3(gone, NG), t3(geq, NG), gmax.unsqueeze(2).broadcast_to([P, NT, NG]), ALU.is_equal))
                by_group = t3(gone, NG).unsqueeze(3).broadcast_to([P, NT, NG, EPG])
                link(tt(g4(selw), g4(sel), by_group, ALU.mult))
                link(dve.reduce_sum(t3(v4, EPG), g4(selw).rearrange("p t g i -> p t i g"), X_AXIS))
                mine = t3(v4, EPG).unsqueeze(3).broadcast_to([P, NT, EPG, EPG])
                other = t3(v4, EPG).unsqueeze(2).broadcast_to([P, NT, EPG, EPG])
                tt(g4(beats), other, mine, ALU.is_gt)
                link(tt(g4(ties), other, mine, ALU.is_equal))
                link(tt(t3(ties, 16), t3(ties, 16), on4(4, 16, NT), ALU.mult))
                link(tt(beats, beats, ties, ALU.add))
                link(dve.reduce_sum(t3(rank, EPG), g4(beats), X_AXIS))
                ts(r0, rank, 0.0, None, ALU.is_equal)
                link(ts(r1, rank, 1.0, None, ALU.is_equal))
                for dst, r in ((m0, r0), (m1, r1)):
                    last = tt(g4(dst), by_group, t3(r, EPG).unsqueeze(2).broadcast_to([P, NT, NG, EPG]), ALU.mult)
                link(last)
                link(tt(msk, m0, m1, ALU.add))
                dve.tensor_copy(msk_bf, msk).then_inc(m["mask"], 1)
                link(ts(mt[:, :, :, 2], t3(m1, NE), float(SEQ), None, ALU.mult))
                m.wait(dve, "pos_mm", 1)
                link(stt(posm, ps[0][:, 0:64], 1.0, msk, ALU.add, ALU.mult))
                link(dve.tensor_copy(pos_bf, posm))

                def pick(g):
                    e = slice(EPG * g, EPG * (g + 1))
                    tt(picks[:, :, e, :], slot_bf[:, :].unsqueeze(1).unsqueeze(1).broadcast_to([P, NT, EPG, P]),
                       t3(pos_bf, NE)[:, :, e].unsqueeze(3).broadcast_to([P, NT, EPG, P]), ALU.is_equal).then_inc(m["picks"], 1)

                pick(0)
                pick(1)
                slots_to_rows(link, m, "idx_mm", "idx", ps[7][:, 0:4 * EPG], idx_f[:, 0:4 * EPG], EPG, idxg[:, 0:EPG],
                              idxs[:, 0:EPG], idx_a[:, 0:EPG])
                pick(2)
                pick(3)
                link(tt(mtmp, m0, scores_s, ALU.mult))
                link(dve.reduce_sum(g01[:, 0:4], t3(mtmp, NE), X_AXIS))
                link(tt(mtmp, m1, scores_s, ALU.mult))
                link(dve.reduce_sum(g01[:, 4:8], t3(mtmp, NE), X_AXIS))
                link(tt(gden, g01[:, 0:4], g01[:, 4:8], ALU.add))
                link(dve.reciprocal(gden, gden))
                link(tt(g01.rearrange("p (k t) -> p k t", k=2), g01.rearrange("p (k t) -> p k t", k=2),
                        gden.unsqueeze(1).broadcast_to([P, 2, NT]), ALU.mult))
                slots_to_rows(link, m, "idx_mm", "idx", ps[1][:, 4 * EPG:64], idx_f[:, 4 * EPG:64], NE - EPG, idxg[:, EPG:NE],
                              idxs[:, EPG:NE], idx_a[:, EPG:NE], count=NG)
                link(dve.tensor_copy(cnt, ps[0][:, 64:80]))
                for j in range(3):
                    last = ts(ind[:, 16 * j:16 * (j + 1)], cnt, float(P * (j + 1)), None, ALU.is_gt)
                link(last)
                link(dve.reduce_sum(nov_f, ind, X_AXIS))
                dve.tensor_copy(nover_i, nov_f).then_inc(m["nover"], 1)

            def slots_to_rows(link, m, mm_sem, done, bank, f, n, rows_in, rows_out, tmp, j=None, count=1):
                m.wait(dve, mm_sem, count, j, 1)
                link(dve.tensor_copy(f, bank[:, 0:4 * n]))
                f4 = t3(f, 4)
                link(ts(tmp, f4[:, :, 3], -4096.0, 4096.0, ALU.mult, ALU.add))
                link(tt(tmp, tmp, f4[:, :, 0], ALU.add))
                link(tt(tmp, tmp, f4[:, :, 1], ALU.add))
                link(dve.tensor_copy(rows_in, tmp))
                tt(rows_out, tmp, f4[:, :, 2], ALU.add).then_inc(m[done], 1)

            def experts(l):
                m = L[l]

                def rows_copy(e, i=None):
                    m.wait(dve, "xt_mm", 2 * e + 2, i, 4)
                    if e >= 2:
                        m.wait(dve, "gu_mm", 2 * (e - 1), i, 4)
                    dve.tensor_copy(xgT[:, e % 2, 4:8, :], ps[3][:, :].rearrange("p (k n) -> p k n", k=4))\
                        .then_inc(m["xt_cpV"], 1)

                def hidden(e, i=None):
                    m.wait(dve, "silu", e + 1, i, 2)
                    m.wait(dve, "gu_mm", 2 * e + 2, i, 4)
                    if e >= 1:
                        m.wait(dve, "ht_mm", e, i, 2)
                    tt(hid, ps[1][:, :], sig, ALU.mult).then_inc(m["hid"], 1)

                def rows_out(e, i=None):
                    m.wait(dve, "dn_mm", 2 * e + 2, i, 4)
                    if e >= 2:
                        m.wait(dve, f"s_done{e % 2}", 16 * (e // 2), i, 16)
                    dve.tensor_copy(y_sb[:, e % 2, 512:1024], ps[6][:, :]).then_inc(m["y_cpV"], 1)

                rows_copy(0)
                hidden(0)
                rows_copy(1)
                hidden(1)
                rows_copy(2)
                rows_out(0)
                hidden(2)
                rows_copy(3)
                rows_out(1)
                with dve.Fori(0, ROUNDS - 1) as i:
                    for e in (3, 4):
                        hidden(e, i)
                        rows_copy(e + 1, i)
                        rows_out(e - 1, i)
                for e in (13, 14):
                    hidden(e)
                    rows_copy(e + 1)
                    rows_out(e - 1)
                hidden(15)
                rows_out(14)
                rows_out(15)

            def more_tiles(l):
                m = L[l]
                n = dve.value_load(nover_i[0:1, 0:1], min_val=0, max_val=NOVER)
                with dve.If(n > 0):
                    m.wait(dve, "s_done0", 16 * 8)
                    m.wait(dve, "gu_mm", 32)
                    m.wait(dve, "y_cpA", NE)
                    ol = Chain(dve, m["o_chain"])
                    ol(ts(cum[:, 0:1], ind[:, 0:1], 0.0, None, ALU.mult))
                    ol(dve.tensor_copy(cum[:, 1:48], ind[:, 0:47]))
                    src, dst = cum, cum2
                    for d in (1, 2, 4, 8, 16, 32):
                        dve.tensor_copy(dst[:, 0:d], src[:, 0:d])
                        ol(tt(dst[:, d:48], src[:, d:48], src[:, 0:48 - d], ALU.add))
                        src, dst = dst, src
                    ol(ts(over, posm, 0.0, None, ALU.mult))
                    for j in range(3):
                        lo, hi = float(P * (j + 1)), float(P * (j + 2))
                        base = src[:, 16 * j:16 * (j + 1)].unsqueeze(1).broadcast_to([P, NT, NE])
                        ol(ts(t3(otmp, NE), base, float(P), -lo, ALU.mult, ALU.add))
                        ol(tt(otmp, otmp, posm, ALU.add))
                        ol(stt(otmp, posm, lo, otmp, ALU.is_gt, ALU.mult))
                        ol(stt(otmp, posm, hi, otmp, ALU.is_le, ALU.mult))
                        ol(tt(over, over, otmp, ALU.add))
                    for a, mk in ((0, m0), (1, m1)):
                        ol(tt(otmp, over, mk, ALU.mult))
                        ol(dve.reduce_sum(ovk[:, 4 * a:4 * a + 4], t3(otmp, NE), X_AXIS))
                    om = ometa.rearrange("p (k t c) -> p k t c", k=2, t=NT)
                    parts = small[:, 36:52].rearrange("p (t c) -> p t c", t=NT)
                    ol(dve.tensor_copy(om, parts.unsqueeze(1).broadcast_to([P, 2, NT, 4])))
                    ol(dve.memset(om[:, 1, :, 2], float(SEQ)))
                    ol(dve.memset(mcur, 0.0))
                    per, first = 12, ol.n
                    with dve.Fori(0, n) as j:
                        ol.n, ol.shift = first, j * per
                        for a in range(2):
                            for t in range(NT):
                                last = ts(over_picks[:, a, t, :], mats[:, 1, :], ovk[:, 4 * a + t:4 * a + t + 1], None,
                                          ALU.is_equal)
                        last.then_inc(m["o_pick"], 1)
                        m.wait(dve, "o_pick", 1, j, 1)
                        ol(ts(ovk, ovk, float(P), None, ALU.subtract))
                        here = otmp[:, 0:48]
                        ol(ts(here, src, mcur, None, ALU.is_equal))
                        ol(tt(here, here, ind, ALU.mult))
                        ol(tt(t3(here, NE), t3(here, NE), on4(20, NE, 3), ALU.mult))
                        ol(dve.reduce_sum(ocmp, here, X_AXIS))
                        ol(dve.tensor_copy(over_e_i, ocmp))
                        ol(ts(mcur, mcur, 1.0, None, ALU.add))
                        slots_to_rows(ol, m, "o_imm", "o_idx", ps[7], idx_f[:, 0:4], 1, curs[:, 4:5], curs[:, 5:6],
                                      idx_a[:, 0:1], j)
                        assert ol.n == first + per
                        m.wait(dve, "o_tr", 1, j, 2)
                        for half in range(2):
                            last = dve.tensor_copy(xgT[:, 0, 4 * half:4 * half + 4, :],
                                                   ps[2 + half][:, :].rearrange("p (k n) -> p k n", k=4))
                        last.then_inc(m["o_cp"], 1)
                        m.wait(dve, "o_silu", 1, j, 1)
                        m.wait(dve, "o_mm", 2, j, 3)
                        tt(hid, ps[1][:, :], sig, ALU.mult).then_inc(m["o_cp"], 1)
                        m.wait(dve, "o_tr", 2, j, 2)
                        dve.tensor_copy(hidT, ps[4][:, :].rearrange("p (k n) -> p k n", k=KE)).then_inc(m["o_cp"], 1)
                        m.wait(dve, "o_mm", 3, j, 3)
                        for half in range(2):
                            last = dve.tensor_copy(y_sb[:, 0, 512 * half:512 * (half + 1)], ps[5 + half][:, :])
                        last.then_inc(m["o_y"], 1)
                        m.wait(dve, "o_scat", 16, j, 16)

            def moe_norm(l):
                m = L[l]

                def gain(t):
                    m.wait(dve, "ln2_z", t + 1)
                    tt(x_tok[:, t, :], x_tok[:, t, :], ln_g, ALU.mult).then_inc(S["out_gain"], 1)

                def scale_and_shift(t):
                    m.wait(dve, "ln2_std", t + 1)
                    link(dve.reciprocal(mv[:, t, 2:3], mv[:, t, 3:4]))
                    stt(mv[:, t, 4:5], mv[:, t, 0:1], -1.0, mv[:, t, 2:3], ALU.mult, ALU.mult).then_inc(m["ln2_rs"], 1)

                for t in range(NT):
                    row = x_tok[:, t, :]
                    m.wait(dve, "x_scaled", t + 1)
                    m.wait(dve, f"y_in{t}", 32)
                    if l == 1 and t == 0:
                        m.wait(dve, "lnp2_in", 32)
                    link(stt(row, yload[t][:, 0, :], g01[:, t:t + 1], row, ALU.mult, ALU.add))
                    if t >= 1:
                        scale_and_shift(t - 1)
                    link(stt(row, yload[t][:, 1, :], g01[:, 4 + t:5 + t], row, ALU.mult, ALU.add))
                    moments(t, row, m, "ln2_ve")
                    if l == 1 and t >= 1:
                        gain(t - 1)
                scale_and_shift(NT - 1)
                if l == 1:
                    gain(NT - 1)

            def conv():
                link(dve.memset(upad, 0.0))
                dve.wait_ge(S["cvec_cp"], 1)

                def gated(c):
                    dve.wait_ge(S["gate_sig"], c + 1)
                    if c >= 3:
                        dve.wait_ge(S["side_mm"], c - 2)
                    stt(upad[:, c % 3, PAD:PAD + SEQ], ps[c % 2][:, :], cvec[:, c:c + 1], gsig[:, c % 2, :],
                        ALU.add, ALU.mult).then_inc(S["u_ready"], 1)

                gated(0)
                n = 0
                for c in range(8):
                    u, sums = upad[:, c % 3, :], (conv_o[:, c, :], odd_taps)
                    dve.wait_ge(S["u_ready"], c + 1)
                    for j in range(NTAP - NPE[c]):
                        if j == 14 and c + 1 < 8:
                            gated(c + 1)
                        if j >= 2:
                            dve.wait_ge(S["tap"], n - 1)
                        if j == 0:
                            ins = ts(sums[0], u[:, 0:SEQ], taps[:, c, 0:1], cvec[:, 16 + c:17 + c], ALU.mult, ALU.add)
                        elif j == 1:
                            if c >= 1:
                                dve.wait_ge(S["conv_done"], c)
                            ins = ts(sums[1], u[:, 1:1 + SEQ], taps[:, c, 1:2], None, ALU.mult)
                        else:
                            ins = stt(sums[j % 2], u[:, j:j + SEQ], taps[:, c, j:j + 1], sums[j % 2], ALU.mult, ALU.add)
                        ins.then_inc(S["tap"], 1)
                        n += 1
                    dve.wait_ge(S["side_mm"], c + 1)
                    dve.wait_ge(S["tap"], n if (NTAP - NPE[c]) % 2 else n - 1)
                    tt(sums[0], ps[6 + c % 2][:, :], sums[0], ALU.add).then_inc(S["tap"], 1)
                    n += 1
                    dve.wait_ge(S["tap"], n)
                    tt(sums[0], sums[0], odd_taps, ALU.add).then_inc(S["conv_done"], 1)
                dve.wait_ge(S["csum_mm"], 1)
                link(ts(cmean, ps[4][:, :], 1.0 / D, None, ALU.mult))
                for c in range(8):
                    tt(conv_o[:, c, :], conv_o[:, c, :], cmean, ALU.subtract).then_inc(S["c_dev"], 1)
                dve.wait_ge(S["cvar_mm"], 8)
                ts(crstd, ps[5][:, :], 1.0 / D, LN_EPS, ALU.mult, ALU.add).then_inc(S["c_ve"], 1)
                dve.wait_ge(S["c_std"], 1)
                link(dve.reciprocal(crstd, crstd))
                for c in range(8):
                    tt(conv_o[:, c, :], conv_o[:, c, :], crstd, ALU.mult).then_inc(S["c_z"], 1)

            mixer(0)
            routing(0)
            experts(0)
            more_tiles(0)
            moe_norm(0)
            conv()
            mixer(1)
            routing(1)
            experts(1)
            more_tiles(1)
            moe_norm(1)

        @block.gpsimd
        def _(pool):
            link = Chain(pool, S["pool_chain"])

            pool.wait_ge(S["preset"], 2)
            rows = rpb_row[0:1, :].rearrange("p (h r x) -> p h r x", h=4, x=RW)[:, :, 0:15, 16:47]
            for h in range(4):
                pool.dma_start(rows[:, h], rpb_2d[:, h]).then_inc(S["rpb_in"], 16)
            pool.wait_ge(S["rpb_in"], 64)
            pool.dma_start(bias_dn.rearrange("c n -> (c n)").rearrange("(o c n) -> o c n", o=1, c=16),
                           rpb_row[0:1, :].unsqueeze(1).broadcast_to([1, 16, 4 * HW])).then_inc(S["rpb_out"], 16)
            pool.wait_ge(S["rpb_out"], 16)
            pool.wait_ge(S["xf0_mm"], 2 * NT)
            for r in range(8):
                src = skewed(bias_dn, (7 - r) * RW + 15, [[4 * HW - 1, 16], [HW, 4], [1, 8 * NX]])
                pool.dma_start(bias_nr[16 * r:16 * (r + 1)], src).then_inc(S["biases_in"], 16)
            pool.wait_ge(S["row_rep"], 16)
            src = skewed(bias_rep, P - 1, [[(4 * NB0 + 8) * RELW - 1, P], [RELW, 4 * NB0 + 8], [1, P]])
            pool.dma_start(bias.rearrange("p (b n) -> p b n", n=P), src).then_inc(S["biases_in"], 16)

            def norm_params(g, b, done, to_g=ln_g, to_b=ln_b):
                pool.dma_start(to_g, over_partitions(g)).then_inc(done, 16)
                pool.dma_start(to_b, over_partitions(b)).then_inc(done, 16)

            pool.wait_ge(S["scores"], NU)
            pool.dma_start(x_res, x[0].rearrange("(t p) d -> p t d", p=P)).then_inc(S["res_in"], 16)
            for k, v in enumerate((ln_ffn_g[0], ln_ffn_b[0])):
                pool.dma_start(lnf[:, k, :], v.rearrange("(p k) -> p k", p=P)).then_inc(S["lnf_in"], 16)
            pool.wait_ge(S["sc_read"], NU)
            norm_params(ln_mix_g[0], ln_mix_b[0], L[0]["lnp_in"], ln_g0, ln_b0)

            def moe(l):
                m = L[l]
                for t in range(NT):
                    m.wait(pool, "ln_done", t + 1)
                    pool.dma_start(xs[l][t * P:(t + 1) * P, :], x_tok[:, t, :]).then_inc(m["xs_st"], 16)
                norm_params(ln_ffn_g[l], ln_ffn_b[l], m["lnp2_in"])
                chain = Chain(pool, m["p_chain"])

                def column(tab, e, dst):
                    chain(pool.tensor_copy(dst, tab[:, e:e + 1] if isinstance(e, int) else tab[:, bass.ds(e, 1)]))

                def gather(e, at_e, i=None):
                    par = e % 2
                    if e >= 2:
                        m.wait(pool, "xt_mm", 2 * (e - 1), i, 4)
                        m.wait(pool, f"g_full{par}", 16 * (e // 2), i, 16)
                    column(idxg, at_e, curs[:, par:par + 1])
                    pool.sem_inc(S["passed"], 1)
                    pool.indirect_dma_start(
                        out=xg[:, par, :], out_offset=None, in_=xs[l],
                        in_offset=bass.IndirectOffsetOnAxis(ap=curs[:, par:par + 1], axis=0),
                        bounds_check=SEQ - 1, oob_is_err=False).then_inc(m[f"g_full{par}"], 16)

                def scatter(e, at_e, i=None):
                    par = e % 2
                    if e >= 2:
                        m.wait(pool, f"s_done{par}", 16 * (e // 2), i, 16)
                    column(idxs, at_e, curs[:, 2 + par:3 + par])
                    m.wait(pool, "y_cpA", e + 1, i, 2)
                    m.wait(pool, "y_cpV", e + 1, i, 2)
                    pool.sem_inc(S["passed"], 1)
                    pool.indirect_dma_start(
                        out=Y[l], out_offset=bass.IndirectOffsetOnAxis(ap=curs[:, 2 + par:3 + par], axis=0),
                        in_=y_sb[:, par, :], in_offset=None,
                        bounds_check=2 * SEQ - 1, oob_is_err=False).then_inc(m[f"s_done{par}"], 16)

                chain(pool.memset(xg, 0.0))
                m.wait(pool, "idx", 1)
                m.wait(pool, "xs_st", 16 * NT)
                gather(0, 0)
                gather(1, 1)
                for e in (0, 1):
                    gather(e + 2, e + 2)
                    scatter(e, e)
                m.wait(pool, "idx", 2)
                per, first = 4, chain.n
                with pool.Fori(0, ROUNDS) as i:
                    chain.shift = i * per
                    for e in (2, 3):
                        gather(e + 2, i * 2 + (e + 2), i)
                        scatter(e, i * 2 + e, i)
                    assert chain.n == first + per
                chain.n, chain.shift = first + per * ROUNDS, None
                scatter(14, 14)
                scatter(15, 15)

                n = pool.value_load(nover_i[0:1, 0:1], min_val=0, max_val=NOVER)
                with pool.If(n > 0):
                    with pool.Fori(0, n) as j:
                        m.wait(pool, "o_idx", 1, j, 1)
                        pool.sem_inc(S["passed"], 1)
                        pool.indirect_dma_start(
                            out=xg[:, 0, :], out_offset=None, in_=xs[l],
                            in_offset=bass.IndirectOffsetOnAxis(ap=curs[:, 4:5], axis=0),
                            bounds_check=SEQ - 1, oob_is_err=False).then_inc(m["o_gath"], 16)
                        m.wait(pool, "o_y", 1, j, 1)
                        pool.sem_inc(S["passed"], 1)
                        pool.indirect_dma_start(
                            out=Y[l], out_offset=bass.IndirectOffsetOnAxis(ap=curs[:, 5:6], axis=0),
                            in_=y_sb[:, 0, :], in_offset=None,
                            bounds_check=2 * SEQ - 1, oob_is_err=False).then_inc(m["o_scat"], 16)
                        m.wait(pool, "o_scat", 16, j, 16)
                m.wait(pool, "s_done0", 16 * 8)
                m.wait(pool, "s_done1", 16 * 8)
                pool.sem_inc(m["y_all"], 1)
                if l == 0:
                    pool.dma_start(crow[0:NTAP, :], w_dw[0]).then_inc(S["cvec_in"], 16)
                    at_row = 0
                    for v in (b_pw1, b_dw, conv_ln_g, conv_ln_b):
                        rows = v[0].rearrange("(r n) -> r n", n=P)
                        k = rows.shape[0]
                        pool.dma_start(vrow[at_row:at_row + k, :], rows).then_inc(S["cvec_in"], 16)
                        at_row += k
                if l == 0:
                    pool.dma_start(bpw2, over_partitions(b_pw2[0])).then_inc(S["bpw2_in"], 16)

            moe(0)
            pool.wait_ge(S["bpw2_in"], 16)
            L[0].wait(pool, "lnp2_in", 32)
            link(pool.tensor_scalar(ln_b, ln_b, ALPHA, None, ALU.mult))
            link(pool.tensor_tensor(bpw2, bpw2, ln_b, ALU.add))
            link(pool.tensor_scalar(ln_g, ln_g, ALPHA, None, ALU.mult))
            for t in range(NT):
                L[0].wait(pool, "xf2_mm", 2 * t + 2)
                link(pool.tensor_tensor(x_tok[:, t, :], x_tok[:, t, :], ln_g, ALU.mult))
                pool.tensor_tensor(x_tok[:, t, :], x_tok[:, t, :], bpw2, ALU.add).then_inc(S["xres"], 1)
            pool.wait_ge(S["xres"], NT)
            norm_params(ln_mix_g[1], ln_mix_b[1], L[1]["lnp_in"])
            moe(1)
            for t in range(NT):
                pool.wait_ge(S["out_gain"], t + 1)
                pool.tensor_tensor(x_tok[:, t, :], x_tok[:, t, :], ln_b, ALU.add).then_inc(S["out_ready"], 1)


_INS = ['x', 'w_in_attn', 'w_out_attn', 'rel_bias', 'rpb_2d', 'w_pw1', 'b_pw1', 'w_dw', 'b_dw', 'conv_ln_g',
        'conv_ln_b', 'w_pw2', 'b_pw2', 'ln_mix_g', 'ln_mix_b', 'ln_ffn_g', 'ln_ffn_b', 'w_router', 'router_bias',
        'w_gate', 'w_up', 'w_down']


def kernel(**inputs):
    import numpy as _np
    import concourse.bacc as _bacc
    from concourse import mybir as _mybir
    from concourse.bass_utils import run_bass_kernel_spmd as _run

    nc = _bacc.Bacc("TRN2", target_bir_lowering=False, num_devices=1)
    arrays, args = {}, []
    consts = {"c_bucket": bucket_table(), "c_window": window_mask(), "c_small": small_table(), "c_mats": matrices()}
    for name in _INS + list(consts):
        a = _np.ascontiguousarray(inputs[name] if name in inputs else consts[name])
        arrays[f"in_{name}_dram"] = a
        args.append(nc.dram_tensor(f"in_{name}_dram", a.shape, _mybir.dt.from_np(a.dtype), kind="ExternalInput").ap())
    args.append(nc.dram_tensor("out_0_dram", (1, SEQ, D), _mybir.dt.float32, kind="ExternalOutput").ap())
    trunk(nc, *args)
    r = _run(nc, [arrays], core_ids=[0])
    return r.results[0]["out_0_dram"]
```

```python
import math
from contextlib import ExitStack

import numpy as np
import concourse.bass as bass
from concourse import mybir

F32 = mybir.dt.float32
F32R = mybir.dt.float32r
BF16 = mybir.dt.bfloat16
I32 = mybir.dt.int32
ALU = mybir.AluOpType
ACT = mybir.ActivationFunctionType
X_AXIS = mybir.AxisListType.X

P = 128
D = 1024
SEQ = 512
NT = SEQ // P
KD = D // P
HD = 64
GRID_W = 64
NE = 16
NG = 4
EPG = NE // NG
DE = 512
KE = DE // P
NTAP = 31
PAD = NTAP // 2
NPE = [5] * 4 + [6, 7, 8, 10]
ALPHA = 4 ** 0.25
LN_EPS = 1e-5
NEG = -1e30
SCALE = HD ** -0.5
SLOTS = 6
CH = 4096
NOVER = SEQ * 2 // P - 1
NB0 = 2 * NT - 1
RELW = 2 * P
NX = 48
RW = NX
HW = 16 * RW


def t5_bucket(rel):
    nb, max_exact = 16, 8
    n = abs(rel)
    big = max_exact + int(math.log(max(n, 1) / max_exact) / math.log(1024 / max_exact) * (nb - max_exact)) \
        if n >= max_exact else n
    return (nb if rel > 0 else 0) + min(big, nb - 1)


def bucket_table():
    t = np.zeros((33, NB0 + 2, RELW), np.float32)

    def put(block, col, rel, ok):
        if ok:
            t[t5_bucket(rel), block, col] = 1.0
        else:
            t[32, block, col] = NEG

    for col in range(RELW):
        d = col - 127
        for block in range(NB0):
            rel = NT * d + block - (NT - 1)
            put(block, col, rel, abs(rel) <= 64)
        put(NB0, col, 4 * d, abs(d) <= 64)
        put(NB0 + 1, col, 4 * d, d % 4 == 0)
    return t.reshape(33, -1)


def window_mask():
    m = np.full((P, 4, NX), NEG, np.float32)
    for q in range(P):
        for b in range(4):
            col = 16 * b + q % 16
            w0 = min(max(col - 8, 0), GRID_W - 16)
            for x in range(NX):
                if w0 <= 16 * (b - 1) + x < w0 + 16:
                    m[q, b, x] = 0.0
    return m


def small_table():
    t = np.zeros((P, 96), np.float32)
    t[:, 0:4] = [4, 3, 2, 1]
    t[:, 4:20] = np.tril(np.ones((4, 4)), -1).ravel()
    t[:, 20:36] = np.arange(NE)
    for tile in range(NT):
        t[:, 36 + 4 * tile] = np.arange(P)
        t[:, 37 + 4 * tile] = P * tile
        t[:, 39 + 4 * tile] = 1.0
    return t


def matrices():
    return np.stack([np.eye(P), np.triu(np.ones((P, P)), 1), np.tile(np.arange(1, P + 1), (P, 1))]).astype(np.float32)


class Chain:

    def __init__(self, eng, sem):
        self.eng, self.sem, self.n, self.shift = eng, sem, 0, None

    def __call__(self, ins):
        self.n += 1
        ins.then_inc(self.sem, 1)
        self.eng.wait_ge(self.sem, self.n if self.shift is None else self.shift + self.n)


def trunk(nc, x, w_in_attn, w_out_attn, rel_bias, rpb_2d, w_pw1, b_pw1, w_dw, b_dw, conv_ln_g,
          conv_ln_b, w_pw2, b_pw2, ln_mix_g, ln_mix_b, ln_ffn_g, ln_ffn_b, w_router, router_bias,
          w_gate, w_up, w_down, c_bucket, c_window, c_small, c_mats, out):
    ctx = ExitStack()
    with ctx:
        def sb(name, shape, dt=F32):
            return ctx.enter_context(nc.sbuf_tensor(name, shape, dt))

        def sem(name):
            return ctx.enter_context(nc.semaphore(name))

        ring_base = -(-nc.sbuf_base // 32) * 32
        ring = sb("ring", [P, SLOTS, CH])
        x_tok_base = -(-nc.sbuf_base // 32) * 32
        x_tok = sb("x_tok", [P, NT, D])
        x_feat_base = -(-nc.sbuf_base // 32) * 32
        x_feat = sb("x_feat", [P, KD, SEQ])
        arena_base = -(-nc.sbuf_base // 32) * 32
        arena = sb("arena", [P, 73 * 256])

        def one_pass_at(name, base, n):
            return nc.alloc_sbuf_tensor_at(name, [P, n], F32R, offset=base)[:, :]

        ring_part = one_pass_at("ring_part", ring_base, SLOTS * CH).rearrange("p (s n) -> p s n", s=SLOTS)
        x_hi = one_pass_at("x_hi", x_feat_base, KD * SEQ).rearrange("p (k n) -> p k n", k=KD)
        x_lo = one_pass_at("x_lo", x_tok_base, KD * SEQ).rearrange("p (k n) -> p k n", k=KD)

        def at(kib, n):
            return arena[:, kib * 256:kib * 256 + n]

        qT = at(0, 4096).rearrange("p (r n) -> p r n", r=8)
        kT = at(16, 4096).rearrange("p (r n) -> p r n", r=8)
        vt = at(32, NT * 768).rearrange("p (t n) -> p t n", t=NT)
        vt3 = at(44, NT * 256).rearrange("p (t n) -> p t n", t=NT)
        vgT = at(44, 2 * 512).rearrange("p (b n) -> p b n", b=2)
        bias = at(48, (4 * NB0 + 8) * P)
        bias0 = bias[:, 0:4 * NB0 * P].rearrange("p (h n) -> p h n", h=4)
        bias12 = bias[:, 4 * NB0 * P:].rearrange("p (h n) -> p h n", h=4)
        bias_n = at(66, 4 * 384).rearrange("p (h n) -> p h n", h=4)
        bucket_sb = at(32, (NB0 + 2) * RELW)
        rel_rows = at(62, (NB0 + 2) * RELW)
        rpb_row = at(48, 4 * HW)
        x_src = at(0, 4096).rearrange("p (t n) -> p t n", t=NT)
        work = x_tok.rearrange("p t n -> p (t n)")
        probs = work[:, 0:4 * 768].rearrange("p (b n) -> p b n", b=4)
        probsT = work[:, 3072:3072 + 2 * 384].rearrange("p (b n) -> p b n", b=2)
        bias_nr = [at(kib, 2 * 384).rearrange("p (h n) -> p h n", h=2) for kib in (28, 44)]
        x_res = at(16, 4096).rearrange("p (t n) -> p t n", t=NT)
        ln_g0 = at(48, D)
        ln_b0 = at(52, D)
        ln_g = at(16, D)
        ln_b = at(20, D)
        xg = at(24, 2 * D).rearrange("p (b n) -> p b n", b=2)
        xgT = at(32, 2 * D).rearrange("p (b k n) -> p b k n", b=2, k=KD)
        y_sb = at(40, 2 * D).rearrange("p (b n) -> p b n", b=2)
        hid = at(48, DE)
        sig = at(50, DE)
        hidT = at(52, DE).rearrange("p (k n) -> p k n", k=KE)
        picks = at(0, 4096).bitcast(BF16).rearrange("p (t e n) -> p t e n", t=NT, e=NE)
        over_w = at(0, 4096)
        down_hi = one_pass_at("down_hi", arena_base, 4096).rearrange("p (k n) -> p k n", k=KE)
        hidT_hi = one_pass_at("hidT_hi", arena_base + 52 * 1024, DE).rearrange("p (k n) -> p k n", k=KE)
        hidT_lo = one_pass_at("hidT_lo", arena_base + 54 * 1024, DE).rearrange("p (k n) -> p k n", k=KE)
        over_picks = at(54, 512).bitcast(BF16).rearrange("p (a t n) -> p a t n", a=2, t=NT)
        yload = [at(kib, 2 * D).rearrange("p (k n) -> p k n", k=2) for kib in (24, 32, 0, 8)]
        rsm = at(56, 16 * 256)
        conv_o = at(0, 4096).rearrange("p (c n) -> p c n", c=8)
        upad = at(24, 3 * 544).rearrange("p (b n) -> p b n", b=3)
        gsig = at(31, 2 * 512).rearrange("p (b n) -> p b n", b=2)
        diag = at(63, 2 * max(NPE) * P).rearrange("p (b j n) -> p b j n", b=2, j=max(NPE))
        csq = at(24, 2 * 512).rearrange("p (b n) -> p b n", b=2)
        cmean = at(37, 512)
        crstd = at(39, 512)
        taps = at(41, 8 * 32).rearrange("p (c n) -> p c n", c=8)
        cvec = at(42, 64)
        crow = at(43, 1024)
        vrow = at(47, P)
        odd_taps = at(48, 512)
        bpw2 = at(52, D)

        ident = sb("ident", [P, P])
        ones = sb("ones", [P, P])
        mats = sb("mats", [P, 2, P])
        before_bf = sb("before_bf", [P, P], BF16)
        ones_bf = sb("ones_bf", [P, P], BF16)
        slot_bf = sb("slot_bf", [P, P], BF16)
        small = sb("small", [P, 96])
        window = sb("window", [P, 4, NX])
        nmax = sb("nmax", [P, 64])
        psum_e = sb("psum_e", [P, 64])
        rinv = sb("rinv", [P, 64])
        wr = sb("wr", [P, KD, NE])
        rb = sb("rb", [P, NE])
        mx = sb("mx", [P, 64])
        rel_sb = sb("rel_sb", [33, 12])
        stats = sb("stats", [P, NT, 2, 6])
        mv = sb("mv", [P, NT, 5])
        warm = sb("warm", [P, 1])
        lnf = sb("lnf", [P, 2, KD])

        ps = [ctx.enter_context(nc.psum_tensor(f"ps{i}", [P, 512], F32)) for i in range(8)]

        bias_one = nc.dram_tensor("bias_one", [(4 * NB0 + 8) * RELW], F32).ap()
        bias_rep = nc.dram_tensor("bias_rep", [P, (4 * NB0 + 8) * RELW], F32).ap()
        bias_dn = nc.dram_tensor("bias_dn", [16, 4 * HW], F32).ap()
        xs = [nc.dram_tensor(f"xs{n}", [SEQ, D], F32).ap() for n in range(2)]
        Y = [nc.dram_tensor(f"Y{n}", [2 * SEQ, D], F32).ap() for n in range(2)]

        def pk(w):
            return w.rearrange("(p k) n -> p k n", p=P)

        def kp(w):
            return w.rearrange("(k p) n -> p k n", p=P)

        NP = 12
        MOE = [NP + 2, NP + 2 + 48 + 6]
        CONV = NP + 2 + 48

        w_full = [sem(f"w_full{s}") for s in range(SLOTS)]

        def slot(c, kk=KD):
            return ring[:, c % SLOTS, :].rearrange("p (k n) -> p k n", k=kk)

        def slot_part(c, kk=KD):
            return ring_part[:, c % SLOTS, :].rearrange("p (k n) -> p k n", k=kk)

        def fills(c):
            unseen = NP // SLOTS if c % 2 else c % SLOTS == 0
            return c // SLOTS + 1 - unseen

        def filled(eng, c, i=None):
            v = 16 * fills(c)
            eng.wait_ge(w_full[c % SLOTS], v if i is None else i * 16 + v)

        S = {n: sem(n) for n in (
            "x_in0", "x_in1", "first_w0", "first_w1", "consts", "bucket_in", "rel_in", "rpb_in", "router_in", "preset",
            "row_mm", "row_cp", "row_out", "row_rep", "rpb_out", "bias_in", "bias_n", "biases_in", "grid_bias", "xf0_mm", "xf0_cp", "xf0_lo", "w_hi", "w_lo",
            "vg_mm", "vg_cp", "proj_mm", "proj_cpA", "proj_cpV", "scores", "sc_read", "nmax", "probs", "pnorm", "pT", "pT_cp",
            "pv", "evac", "res_in",
            "dve_chain", "pool_chain", "cvec_in", "cvec_mm", "cvec_cp", "pw1_mm", "gate_sig",
            "u_ready", "conv_done", "xf2_cpV", "out_ready", "out_last", "lnf_in", "csum_mm", "c_dev", "c_sq", "cvar_mm", "c_ve", "c_std",
            "c_z", "c_act", "diag", "side_mm", "tap", "bpw2_in", "xres", "store_out", "act_chain", "passed")}
        PER_LAYER = {
            "mo_mm": 8, "mo_read": 8, "ln_ve": NT, "ln_std": NT, "ln_done": NT, "xf_mm": 8, "xf_cp": 8, "lnp_in": 32,
            "xs_st": 16 * NT, "lnp2_in": 32, "logit_mm": NT, "score": 1, "mask": 1, "pos_mm": 1, "picks": 3,
            "idx_mm": 3, "idx": 2, "nover": 1, "g_full0": 128, "g_full1": 128, "s_done0": 128, "s_done1": 128,
            "xt_mm": 32, "xt_cpA": 16, "xt_cpV": 16, "gu_mm": 32, "silu": 16, "hid": 16, "ht_mm": 16, "ht_cp": 16, "ht_lo": 16,
            "dn_hi": 64, "dn_lo": 64,
            "dn_mm": 32, "y_cpA": 16, "y_cpV": 16, "y_in0": 32, "y_in1": 32, "y_in2": 32, "y_in3": 32,
            "x_scaled": NT, "y_all": 1, "ln2_rs": NT, "ln2_z": NT, "ln2_ve": NT,
            "ln2_std": NT, "xf2_mm": 8, "xf2_cp": 6}
        shared = {n: sem(n) for n in PER_LAYER}
        OWN = ("o_pick", "o_imm", "o_idx", "o_gath", "o_w", "o_mm", "o_tr", "o_silu", "o_cp", "o_scat", "o_chain",
               "o_y", "p_chain")

        class Layer:

            def __init__(self, l):
                self.l = l
                self.own = {n: sem(f"{n}_{l}") for n in OWN}

            def __getitem__(self, name):
                return self.own[name] if name in self.own else shared[name]

            def value(self, name, v):
                return v if name in self.own else v + self.l * PER_LAYER[name]

            def wait(self, eng, name, v, i=None, k=0):
                v = self.value(name, v)
                eng.wait_ge(self[name], v if i is None else i * k + v)

        L = [Layer(l) for l in range(2)]

        def in_tiles(v, pair):
            if pair < 6:
                return v.rearrange("p (i t) -> p t i", t=4)
            return v.rearrange("p (r b c) -> p b r c", r=8, c=16)

        def tiles_of(v, pair):
            if pair < 6:
                return v.rearrange("p (t i) -> p t i", t=4)
            return v.rearrange("p (b r c) -> p b r c", r=8, c=16)

        def tokens(v, t):
            return v[:, t::4]

        def grid_tiles(t):
            return [b for b in (t - 1, t, t + 1) if 0 <= b < NT]

        UNITS = [(kind, 2 * jp + par, t) for kind in ("dilated", "grid") for jp in range(2)
                 for t in range(NT) for par in range(2)]
        NU = len(UNITS)
        LAG = 3

        def key_blocks(u):
            kind, j, t = UNITS[u]
            return NT + 2 if kind == "dilated" else len(grid_tiles(t))

        PARTS = [(u, b, min(b + 3, key_blocks(u))) for u in range(NU) for b in range(0, key_blocks(u), 3)]
        PART_END = {u: n + 1 for n, (u, _, _) in enumerate(PARTS)}

        def parts_of(u):
            return [n for n, part in enumerate(PARTS) if part[0] == u]

        ITEMS = []
        for c, cols in enumerate([[("q", p) for p in range(4)], [("q", 4), ("q", 5), ("k", 0), ("k", 1)],
                                  [("k", p) for p in range(2, 6)]]):
            ITEMS += [(kind, p, c, P * i) for i, (kind, p) in enumerate(cols)]
        ITEMS += [("v", t, 3, 0) for t in range(NT)]
        ITEMS += [("v2", a, 4, 0) for a in range(2)] + [("q", 6, 4, 256), ("q", 7, 4, 384)]
        ITEMS += [("vT", 0, 5, 256), ("vT", 1, 5, 384), ("k", 6, 5, 0), ("k", 7, 5, P)]
        NI = len(ITEMS)
        NPIECE, AHEAD = 24, 6

        def piece(n):
            cols = slice(P * (n % 4), P * (n % 4 + 1))
            c = 2 * (n // 4)
            return slot(c)[:, :, cols], slot_part(c + 1)[:, :, cols], slot_part(c)[:, :, cols]

        def pieces_at(n):
            done = 0 if n < 2 else min(NPIECE, n - 2 + AHEAD)
            return range(done, min(NPIECE, n + AHEAD))

        ROWS_AT = 4

        off = [0]

        def small_buf(n, dt=F32):
            v = rsm[:, off[0]:off[0] + n]
            off[0] += n
            return v if dt == F32 else v.bitcast(dt)

        def t3(v, b):
            return v.rearrange("p (a b) -> p a b", b=b)

        scores_s, sel, pairsum = small_buf(64), small_buf(64), small_buf(96)
        gtop, gmax, geq = small_buf(16), small_buf(4), small_buf(16)
        gone = small_buf(16)
        selw, v4 = small_buf(64), small_buf(16)
        beats, ties, rank = small_buf(64), small_buf(64), small_buf(16)
        r0, r1 = small_buf(16), small_buf(16)
        m0, m1, msk = small_buf(64), small_buf(64), small_buf(64)
        mtmp = small_buf(64)
        g01 = small_buf(8)
        gden = small_buf(4)
        posm = small_buf(64)
        pos_bf = small_buf(32, BF16)
        msk_bf = small_buf(32, BF16)
        meta = small_buf(2 * NT * NE, BF16)
        idx_f = small_buf(4 * NE)
        idx_a = small_buf(NE)
        idxg = small_buf(NE, I32)
        idxs = small_buf(NE, I32)
        curs = small_buf(8, I32)
        cnt = small_buf(NE)
        ind = small_buf(48)
        cum = small_buf(48)
        cum2 = small_buf(48)
        over = small_buf(64)
        otmp = small_buf(64)
        ovk = small_buf(8)
        mcur = small_buf(1)
        nov_f = small_buf(1)
        nover_i = small_buf(1, I32)
        over_e_i = small_buf(1, I32)
        ocmp = small_buf(1)
        ometa = small_buf(16, BF16)
        assert off[0] <= 7 * 256, off[0]

        def on4(c0, n, reps):
            return small[:, c0:c0 + n].unsqueeze(1).broadcast_to([P, reps, n])

        def over_partitions(v):
            return bass.AP(tensor=v.tensor, offset=v.offset, ap=[[0, P], [1, v.shape[-1]]])

        def skewed(v, start, pattern):
            return bass.AP(tensor=v.tensor, offset=v.offset + start, ap=pattern)

        def item_views(n):
            kind, what = ITEMS[n][:2]
            bank = ps[n % 4][:, :]
            if kind == "v":
                return vt[:, what, 0:512], bank
            if kind == "v2":
                return vt[:, 2 * what:2 * what + 2, 512:768], bank.rearrange("p (t n) -> p t n", t=2)
            pair = what + 6 if kind == "vT" else what
            return tiles_of({"q": qT, "k": kT, "vT": vgT}[kind][:, what, :], pair), in_tiles(bank, pair)

        def down_chunk(l, e):
            return MOE[l] + (47 if e == 15 else 4 + 3 * e)

        ITEM_END = {c: max(n for n, it in enumerate(ITEMS) if it[2] == c) + 1 for c in range(6)}

        def reader_done(c):
            if c < NP:
                return S["proj_mm"], ITEM_END[c // 2]
            if c < NP + 2:
                return L[0]["mo_mm"], L[0].value("mo_mm", 7 + c - NP)
            if CONV <= c < CONV + 4:
                return S["pw1_mm"], (7, 8, 15, 16)[c - CONV]
            if CONV + 4 <= c < CONV + 6:
                return L[1]["mo_mm"], L[1].value("mo_mm", 7 + c - CONV - 4)
            l = 0 if c < CONV else 1
            p = c - MOE[l]
            if p < 2:
                name, v = "gu_mm", p + 1
            elif p == 47:
                name, v = "dn_mm", 32
            else:
                n, which = divmod(p - 2, 3)
                name, v = ("dn_mm", 2 * n + 2) if which == 2 else ("gu_mm", 2 * (n + 1) + which + 1)
            return L[l][name], L[l].value(name, v)

        def load(sp, c, src, kk=KD):
            if c >= SLOTS:
                sp.wait_ge(*reader_done(c - SLOTS))
            sp.dma_start(slot(c, kk), src).then_inc(w_full[c % SLOTS], 16)

        NROW = -(-(NB0 + 2) * RELW // 512)
        STAGES = [(0, 2), (2, 9), (9, NE)]
        ROUNDS = 6

        block = ctx.enter_context(nc.Block())

        @block.sync
        def _(sp):
            for t in range(NT):
                sp.dma_start(x_src[:, t, :], x[0, t * P:(t + 1) * P, :]).then_inc(S[f"x_in{t // 2}"], 16)
            w = pk(w_in_attn[0])
            sp.dma_start(slot(0)[:, :, 0:P], w[:, :, 0:P]).then_inc(S["first_w0"], 16)
            sp.dma_start(slot(0)[:, :, P:512], w[:, :, P:512]).then_inc(S["first_w1"], 16)
            for c in range(1, 6):
                load(sp, 2 * c, pk(w_in_attn[0])[:, :, c * 512:(c + 1) * 512])
            for c in range(2):
                load(sp, NP + c, kp(w_out_attn[0])[:, :, c * 512:(c + 1) * 512])

            def experts(l):
                m, base = L[l], MOE[l]

                def expert_w(e, which):
                    w = (w_gate, w_up, w_down)[which][l]
                    src = w[e] if isinstance(e, int) else w[bass.ds(e, 1)].rearrange("o a n -> (o a) n")
                    return kp(src) if which == 2 else pk(src)

                load(sp, base, expert_w(0, 0))
                load(sp, base + 1, expert_w(0, 1))
                for n in range(2):
                    load(sp, base + 2 + 3 * n, expert_w(n + 1, 0))
                    load(sp, base + 3 + 3 * n, expert_w(n + 1, 1))
                    load(sp, base + 4 + 3 * n, expert_w(n, 2), KE)
                with sp.Fori(0, ROUNDS) as i:
                    for u in range(2):
                        n = 2 + u
                        for which in range(3):
                            c = base + 2 + 3 * n + which
                            if which == 2:
                                m.wait(sp, "dn_mm", 2 * (n - 2) + 2, i, 4)
                            else:
                                m.wait(sp, "gu_mm", 2 * (n - 1) + which + 1, i, 4)
                            e = i * 2 + (n if which == 2 else n + 1)
                            sp.dma_start(slot(c, KE if which == 2 else KD), expert_w(e, which))\
                              .then_inc(w_full[c % SLOTS], 16)
                load(sp, base + 44, expert_w(15, 0))
                load(sp, base + 45, expert_w(15, 1))
                load(sp, base + 46, expert_w(14, 2), KE)
                load(sp, base + 47, expert_w(15, 2), KE)
                m.wait(sp, "nover", 1)
                n = sp.value_load(nover_i[0:1, 0:1], min_val=0, max_val=NOVER)
                with sp.If(n > 0):
                    with sp.Fori(0, n) as j:
                        m.wait(sp, "o_idx", 1, j, 1)
                        sp.sem_inc(S["passed"], 1)
                        e = sp.value_load(over_e_i[0:1, 0:1], min_val=0, max_val=NE - 1)
                        for which in range(3):
                            if which:
                                m.wait(sp, "o_mm", which, j, 3)
                            dst = over_w.rearrange("p (k n) -> p k n", k=KE if which == 2 else KD)
                            sp.dma_start(dst, expert_w(e, which)).then_inc(m["o_w"], 16)

            experts(0)
            for c, col in enumerate((0, 1024, 512, 1536)):
                load(sp, CONV + c, pk(w_pw1[0])[:, :, col:col + 512])
            for c in range(2):
                load(sp, CONV + 4 + c, kp(w_pw2[0])[:, :, c * 512:(c + 1) * 512])
            experts(1)
            for t in range(NT):
                if t < NT - 1:
                    sp.wait_ge(S["out_ready"], t + 1)
                else:
                    sp.wait_ge(S["out_last"], 1)
                sp.dma_start(out[0].rearrange("(t p) d -> t p d", p=P)[t], x_tok[:, t, :]).then_inc(S["store_out"], 16)
            sp.wait_ge(S["store_out"], 16 * NT)

        @block.tensor
        def _(pe):
            def mm(out_, lhsT, rhs, first=True, last=True):
                return pe.matmul(out_, lhsT, rhs, start=first, stop=last)

            def to_features(t, m, mm_sem, cp_sem):
                for half in range(2):
                    n = 2 * t + half
                    if n >= 2:
                        m.wait(pe, cp_sem, n - 1)
                    for k in range(4):
                        ins = pe.transpose(ps[6 + half][:, k * P:(k + 1) * P],
                                           x_tok[:, t, 4 * half + k::8], ident[:, :])
                    ins.then_inc(m[mm_sem], 1)

            pe.wait_ge(S["consts"], 16)
            for t in range(NT):
                pe.wait_ge(S[f"x_in{t // 2}"], 32)
                for half in range(2):
                    for k in range(4):
                        ins = pe.transpose(ps[2 * t + half][:, k * P:(k + 1) * P], x_src[:, t, 4 * half + k::8], ident[:, :])
                    ins.then_inc(S["xf0_mm"], 1)

            def bias_rows():
                pe.wait_ge(S["bucket_in"], 16)
                pe.wait_ge(S["rel_in"], 16)
                for n in range(NROW):
                    if n >= 2:
                        pe.wait_ge(S["row_cp"], n - 1)
                    c0, c1 = 512 * n, min(512 * (n + 1), (NB0 + 2) * RELW)
                    mm(ps[4 + n % 2][0:12, 0:c1 - c0], rel_sb[:, :], bucket_sb[0:33, c0:c1]).then_inc(S["row_mm"], 1)

            pe.wait_ge(S["xf0_lo"], 2 * NT)

            def copied(n):
                pe.wait_ge(S["proj_cpA" if n % 2 == 0 else "proj_cpV"], n // 2 + 1)

            for n, (kind, what, c, col) in enumerate(ITEMS):
                if n == ROWS_AT:
                    bias_rows()
                width = {"v": 512, "v2": 256}.get(kind, P)
                pe.wait_ge(S["w_lo"], 4 * c + (col + width) // P)
                if n >= 4:
                    copied(n - 4)
                bank, w_hi, w_lo = ps[n % 4], slot_part(2 * c + 1), slot_part(2 * c)
                terms = [(x_hi, w_hi), (x_hi, w_lo), (x_lo, w_hi)]

                def product(out_, x_view, w_view, x_first):
                    for a, (xp, wp) in enumerate(terms):
                        for k in range(KD):
                            xv, wv = x_view(xp[:, k, :]), w_view(wp[:, k, :])
                            ins = mm(out_, *((xv, wv) if x_first else (wv, xv)), a == 0 and k == 0, a == 2 and k == KD - 1)
                    return ins

                if kind == "v":
                    ins = product(bank[:, :], lambda v: tokens(v, what), lambda v: v, True)
                elif kind == "v2":
                    for half in range(2):
                        ins = product(bank[:, 256 * half:256 * (half + 1)], lambda v: tokens(v, 2 * what + half),
                                      lambda v: v[:, 0:256], True)
                else:
                    ins = product(bank[:, :], lambda v: v, lambda v: v[:, col:col + P], False)
                ins.then_inc(S["proj_mm"], 1)
            copied(NI - 4)
            copied(NI - 3)
            for pr in range(2):
                for t in range(NT):
                    ins = pe.transpose(ps[4 + pr][:, t * P:(t + 1) * P], vgT[:, pr, t * P:(t + 1) * P], ident[:, :])
                ins.then_inc(S["vg_mm"], 1)
            copied(NI - 2)
            copied(NI - 1)

            def scores(u):
                kind, j, t = UNITS[u]
                jp, lo = j // 2, HD * (j % 2)
                if u >= 2:
                    pe.wait_ge(S["sc_read"], u - 1)
                bank = 2 * (u % 2)

                def q(pair):
                    return qT[lo:lo + HD, pair, t * P:(t + 1) * P]

                if kind == "dilated":
                    mm(ps[bank][:, :], q(jp), kT[lo:lo + HD, jp, :])
                    for g in (1, 2):
                        ins = mm(ps[bank + 1][:, (g - 1) * P:g * P], q(2 * g + jp), kT[lo:lo + HD, 2 * g + jp, t * P:(t + 1) * P])
                else:
                    b = grid_tiles(t)
                    ins = mm(ps[bank][:, 0:len(b) * P], q(6 + jp), kT[lo:lo + HD, 6 + jp, b[0] * P:(b[-1] + 1) * P])
                ins.then_inc(S["scores"], 1)

            def transposes(n):
                u, b0, b1 = PARTS[n]
                if b0 == 0:
                    pe.wait_ge(S["pnorm"], u + 1)
                if n >= 2:
                    pe.wait_ge(S["pT_cp"], n - 1)
                for b in range(b0, b1):
                    ins = pe.transpose(ps[4 + n % 2][:, P * (b - b0):P * (b - b0 + 1)], probs[:, u % 4, P * b:P * (b + 1)],
                                       ident[:, :])
                ins.then_inc(S["pT"], 1)

            def values(n):
                u, b0, b1 = PARTS[n]
                kind, j, t = UNITS[u]
                e, lo = u // 2, HD * (j % 2)
                pe.wait_ge(S["pT_cp"], n + 1)
                if u % 2 == 0 and b0 == 0 and e >= 2:
                    pe.wait_ge(S["evac"], e - 1)
                for b in range(b0, b1):
                    if kind == "dilated":
                        g = max(0, b - NT + 1)
                        tile = b if g == 0 else t
                        v = vt[:, tile, 256 * g + HD * j:256 * g + HD * (j + 1)]
                        first, last = (b == 0, b == NT - 1) if g == 0 else (True, True)
                    else:
                        g = 0
                        v = vt3[:, grid_tiles(t)[b], HD * j:HD * (j + 1)]
                        first, last = b == 0, b == b1 - 1
                    ins = mm(ps[6 + e % 2][lo:lo + HD, g * P:(g + 1) * P], v, probsT[:, n % 2, P * (b - b0):P * (b - b0 + 1)],
                             first, last)
                ins.then_inc(S["pv"], 1)

            for step in range(NU + LAG):
                if step < NU:
                    scores(step)
                if step >= LAG:
                    for n in parts_of(step - LAG):
                        if n == 0:
                            pe.wait_ge(S["vg_cp"], 2)
                        transposes(n)
                        if n >= 1:
                            values(n - 1)
            values(len(PARTS) - 1)

            def mixer_out(l, src, c0, ready):
                m = L[l]

                def logits(t):
                    m.wait(pe, "xf_cp", 2 * t + 2)
                    for k in range(KD):
                        ins = mm(ps[5][:, t * NE:(t + 1) * NE], x_feat[:, k, t * P:(t + 1) * P], wr[:, k, :],
                                 k == 0, k == KD - 1)
                    ins.then_inc(m["logit_mm"], 1)

                for t in range(NT):
                    for half in range(2):
                        if t == 0:
                            filled(pe, c0 + half)
                        n = 2 * t + half
                        if n >= 4:
                            m.wait(pe, "mo_read", n - 3)
                        for k in range(KD):
                            if n == 0:
                                ready(k)
                            ins = mm(ps[n % 4][:, :], src(k, t), slot(c0 + half)[:, k, :], k == 0, k == KD - 1)
                        ins.then_inc(m["mo_mm"], 1)
                    if t >= 1:
                        m.wait(pe, "ln_done", t)
                        to_features(t - 1, m, "xf_mm", "xf_cp")
                    if t >= 2:
                        if l == 0 and t == 2:
                            pe.wait_ge(S["router_in"], 32)
                        logits(t - 2)
                logits(NT - 2)
                m.wait(pe, "ln_done", NT)
                to_features(NT - 1, m, "xf_mm", "xf_cp")
                logits(NT - 1)

            def routing(l):
                m = L[l]
                m.wait(pe, "mask", 1)
                mk = t3(msk_bf, NE)
                for t in range(NT):
                    for a in range(t):
                        mm(ps[0][:, t * NE:(t + 1) * NE], ones_bf[:, :], mk[:, a], a == 0, False)
                    mm(ps[0][:, t * NE:(t + 1) * NE], before_bf[:, :], mk[:, t], t == 0, True)
                for t in range(NT):
                    ins = mm(ps[0][:, 4 * NE:5 * NE], ones_bf[:, :], mk[:, t], t == 0, t == NT - 1)
                ins.then_inc(m["pos_mm"], 1)
                slot_tokens(m, 0)

            def slot_tokens(m, stage):
                mt = meta.rearrange("p (t e c) -> p t e c", t=NT, e=NE)
                m.wait(pe, "picks", stage + 1)
                if stage == 1:
                    m.wait(pe, "idx", 1)
                for e in range(*STAGES[stage]):
                    for t in range(NT):
                        ins = mm(ps[7][:, 4 * e:4 * e + 4], picks[:, t, e, :], mt[:, t, e, :], t == 0, t == NT - 1)
                ins.then_inc(m["idx_mm"], 1)

            def experts(l):
                m, base = L[l], MOE[l]

                def rows_T(e, i=None):
                    par = e % 2
                    m.wait(pe, f"g_full{par}", 16 * (e // 2 + 1), i, 16)
                    if e > 0:
                        m.wait(pe, "xt_cpA", e, i, 2)
                        m.wait(pe, "xt_cpV", e, i, 2)
                    for half in range(2):
                        for k in range(4):
                            ins = pe.transpose(ps[2 + half][:, k * P:(k + 1) * P], xg[:, par, 4 * half + k::8], ident[:, :])
                        ins.then_inc(m["xt_mm"], 1)

                def gate_up(e, i=None):
                    m.wait(pe, "xt_cpA", e + 1, i, 2)
                    m.wait(pe, "xt_cpV", e + 1, i, 2)
                    if e > 0:
                        m.wait(pe, "hid", e, i, 2)
                    c = base + (3 * e - 1 if e else 0)
                    for half in range(2):
                        filled(pe, c + half, i)
                        for k in range(KD):
                            ins = mm(ps[half][:, :], xgT[:, e % 2, k, :], slot(c + half)[:, k, :], k == 0, k == KD - 1)
                        ins.then_inc(m["gu_mm"], 1)

                def hidden_T(e, i=None):
                    m.wait(pe, "hid", e + 1, i, 2)
                    for k in range(KE):
                        ins = pe.transpose(ps[4][:, k * P:(k + 1) * P], hid[:, k * P:(k + 1) * P], ident[:, :])
                    ins.then_inc(m["ht_mm"], 1)

                def down(e, i=None):
                    m.wait(pe, "ht_cp", e + 1, i, 2)
                    if e > 0:
                        m.wait(pe, "y_cpA", e, i, 2)
                        m.wait(pe, "y_cpV", e, i, 2)
                    m.wait(pe, "ht_lo", e + 1, i, 2)
                    w_lo = slot_part(down_chunk(l, e), KE)
                    for k in range(KE):
                        m.wait(pe, "dn_hi", KE * e + k + 1, i, 2 * KE)
                        m.wait(pe, "dn_lo", KE * e + k + 1, i, 2 * KE)
                        for half in range(2):
                            n = slice(half * 512, (half + 1) * 512)
                            terms = [(hidT_hi, down_hi), (hidT_hi, w_lo), (hidT_lo, down_hi)]
                            for a, (x_part, w_part) in enumerate(terms):
                                ins = mm(ps[5 + half][:, :], x_part[:, k, :], w_part[:, k, n],
                                         k == 0 and a == 0, k == KE - 1 and a == 2)
                            if k == KE - 1:
                                ins.then_inc(m["dn_mm"], 1)

                rows_T(0)
                gate_up(0)
                slot_tokens(m, 1)
                slot_tokens(m, 2)
                rows_T(1)
                hidden_T(0)
                gate_up(1)
                rows_T(2)
                down(0)
                hidden_T(1)
                with pe.Fori(0, ROUNDS) as i:
                    for e in (2, 3):
                        gate_up(e, i)
                        rows_T(e + 1, i)
                        down(e - 1, i)
                        hidden_T(e, i)
                gate_up(14)
                rows_T(15)
                down(13)
                hidden_T(14)
                gate_up(15)
                down(14)
                hidden_T(15)
                down(15)

            def more_tiles(l):
                m = L[l]
                m.wait(pe, "nover", 1)
                m.wait(pe, "y_cpA", NE)
                m.wait(pe, "y_cpV", NE)
                n = pe.value_load(nover_i[0:1, 0:1], min_val=0, max_val=NOVER)
                om = ometa.rearrange("p (k t c) -> p k t c", k=2, t=NT)
                with pe.If(n > 0):
                    with pe.Fori(0, n) as j:
                        m.wait(pe, "o_pick", 1, j, 1)
                        for a in range(2):
                            for t in range(NT):
                                ins = mm(ps[7][:, 0:4], over_picks[:, a, t, :], om[:, a, t, :], a + t == 0, a + t == NT)
                        ins.then_inc(m["o_imm"], 1)
                        m.wait(pe, "o_gath", 16, j, 16)
                        for k in range(KD):
                            ins = pe.transpose(ps[2 + k // 4][:, k % 4 * P:(k % 4 + 1) * P], xg[:, 0, k::8], ident[:, :])
                        ins.then_inc(m["o_tr"], 1)
                        m.wait(pe, "o_cp", 1, j, 3)
                        for half in range(2):
                            m.wait(pe, "o_w", 16 * (half + 1), j, 48)
                            for k in range(KD):
                                ins = mm(ps[half][:, :], xgT[:, 0, k, :], over_w.rearrange("p (k n) -> p k n", k=KD)[:, k, :],
                                         k == 0, k == KD - 1)
                            ins.then_inc(m["o_mm"], 1)
                        m.wait(pe, "o_cp", 2, j, 3)
                        for k in range(KE):
                            ins = pe.transpose(ps[4][:, k * P:(k + 1) * P], hid[:, k * P:(k + 1) * P], ident[:, :])
                        ins.then_inc(m["o_tr"], 1)
                        m.wait(pe, "o_cp", 3, j, 3)
                        m.wait(pe, "o_w", 48, j, 48)
                        for half in range(2):
                            for k in range(KE):
                                ins = mm(ps[5 + half][:, :], hidT[:, k, :],
                                         over_w.rearrange("p (k n) -> p k n", k=KE)[:, k, half * 512:(half + 1) * 512],
                                         k == 0, k == KE - 1)
                        ins.then_inc(m["o_mm"], 1)

            def conv():
                for t in range(NT):
                    L[0].wait(pe, "ln2_z", t + 1)
                    for half in range(2):
                        if t == NT - 1 and half == 1:
                            pe.wait_ge(S["xf2_cpV"], 1)
                        elif t >= 1:
                            L[0].wait(pe, "xf2_cp", 2 * t - 1 + half)
                        for k in range(4):
                            ins = pe.transpose(ps[6 + half][:, k * P:(k + 1) * P], x_tok[:, t, 4 * half + k::8], ident[:, :])
                        ins.then_inc(L[0]["xf2_mm"], 1)
                pe.wait_ge(S["cvec_in"], 16 * 5)
                pe.transpose(ps[4][:, 0:40], vrow[0:40, :], ident[0:40, 0:40])
                for c in range(8):
                    ins = pe.transpose(ps[5][:, c * 32:c * 32 + NTAP], crow[0:NTAP, c * P:(c + 1) * P], ident[0:NTAP, 0:NTAP])
                ins.then_inc(S["cvec_mm"], 1)
                L[0].wait(pe, "xf2_cp", 2 * NT - 2)
                pe.wait_ge(S["xf2_cpV"], 2)

                def side_taps(c):
                    pe.wait_ge(S["u_ready"], c + 1)
                    pe.wait_ge(S["diag"], c + 1)
                    if c >= 2:
                        pe.wait_ge(S["conv_done"], c - 1)
                    for j in range(NPE[c]):
                        tap = NTAP - NPE[c] + j
                        ins = mm(ps[6 + c % 2][:, :], diag[:, c % 2, j, :], upad[:, c % 3, tap:tap + SEQ],
                                 j == 0, j == NPE[c] - 1)
                    ins.then_inc(S["side_mm"], 1)

                for c in range(8):
                    for gate in range(2):
                        ch = CONV + 2 * (c // 4) + gate
                        if c % 4 == 0:
                            filled(pe, ch)
                        if c >= 2:
                            pe.wait_ge(S["u_ready"], c - 1)
                        for k in range(KD):
                            ins = mm(ps[2 * gate + c % 2][:, :], slot(ch)[:, k, (c % 4) * P:(c % 4 + 1) * P], x_feat[:, k, :],
                                     k == 0, k == KD - 1)
                        ins.then_inc(S["pw1_mm"], 1)
                    if c >= 1:
                        side_taps(c - 1)
                side_taps(7)
                for c in range(8):
                    pe.wait_ge(S["conv_done"], c + 1)
                    ins = mm(ps[4][:, :], ones[:, :], conv_o[:, c, :], c == 0, c == 7)
                ins.then_inc(S["csum_mm"], 1)
                for c in range(8):
                    pe.wait_ge(S["c_sq"], c + 1)
                    mm(ps[5][:, :], ones[:, :], csq[:, c % 2, :], c == 0, c == 7).then_inc(S["cvar_mm"], 1)

            pe.wait_ge(S["evac"], NU // 2)
            mixer_out(0, lambda k, t: x_feat[:, k, t * P:(t + 1) * P], NP, lambda k: None)
            routing(0)
            experts(0)
            more_tiles(0)
            conv()
            mixer_out(1, lambda k, t: conv_o[:, k, t * P:(t + 1) * P], CONV + 4,
                      lambda k: pe.wait_ge(S["c_act"], k + 1))
            routing(1)
            experts(1)
            more_tiles(1)

        @block.scalar
        def _(act):
            def copy(out_, in_):
                return act.activation(out_, in_, ACT.Copy)

            act.dma_start(ident[:, :], c_mats[0]).then_inc(S["consts"], 16)
            act.wait_ge(S["preset"], 1)
            act.dma_start(rel_sb[0:32, :], rel_bias).then_inc(S["rel_in"], 16)
            act.dma_start(bucket_sb[0:33, :], c_bucket).then_inc(S["bucket_in"], 16)

            def features_copy(t, m, mm_sem, cp_sem):
                for half in range(2):
                    m.wait(act, mm_sem, 2 * t + half + 1)
                    copy(x_feat[:, 4 * half:4 * half + 4, t * P:(t + 1) * P],
                         ps[6 + half][:, :].rearrange("p (k n) -> p k n", k=4)).then_inc(m[cp_sem], 1)

            for n in range(2 * NT):
                t, half = divmod(n, 2)
                act.wait_ge(S["xf0_mm"], n + 1)
                copy(x_hi[:, 4 * half:4 * half + 4, t * P:(t + 1) * P], ps[n][:, :].rearrange("p (k n) -> p k n", k=4))\
                    .then_inc(S["xf0_cp"], 1)
            def bias_rows_out():
                for n in range(NROW):
                    act.wait_ge(S["row_mm"], n + 1)
                    c0, c1 = 512 * n, min(512 * (n + 1), (NB0 + 2) * RELW)
                    copy(rel_rows[0:12, c0:c1], ps[4 + n % 2][0:12, 0:c1 - c0]).then_inc(S["row_cp"], 1)
                act.wait_ge(S["row_cp"], NROW)
                w0 = NB0 * RELW
                act.dma_start(bias_one[0:4 * w0].rearrange("(h n) -> h n", h=4), rel_rows[0:4, 0:w0])\
                   .then_inc(S["row_out"], 16)
                both = bias_one[4 * w0:].rearrange("(h g n) -> h g n", g=2, n=RELW)
                for g in range(2):
                    act.dma_start(both[:, g, :], rel_rows[4 * (g + 1):4 * (g + 2), w0 + g * RELW:w0 + (g + 1) * RELW])\
                       .then_inc(S["row_out"], 16)

            for n in range(0, NI, 2):
                if n == 2:
                    act.dma_start(mats[:, :, :], c_mats[1:3].rearrange("m p n -> p m n")).then_inc(S["consts"], 16)
                    act.dma_start(small[:, :], c_small).then_inc(S["consts"], 16)
                    act.dma_start(window[:, :, :], c_window).then_inc(S["bias_in"], 16)
                    act.dma_start(wr[:, :, :], pk(w_router)).then_inc(S["router_in"], 16)
                    act.dma_start(rb[:, :], over_partitions(router_bias)).then_inc(S["router_in"], 16)
                if n == ROWS_AT:
                    bias_rows_out()
                if n == ROWS_AT + 2:
                    act.wait_ge(S["row_out"], 48)
                    act.dma_start(bias_rep, over_partitions(bias_one)).then_inc(S["row_rep"], 16)
                for j in pieces_at(n):
                    if j < 2:
                        act.wait_ge(S[f"first_w{j}"], 16)
                    elif j >= 4 and j % 4 == 0:
                        filled(act, 2 * (j // 4))
                    w, hi, _ = piece(j)
                    copy(hi, w).then_inc(S["w_hi"], 1)
                act.wait_ge(S["proj_mm"], n + 1)
                if ITEMS[n][0] == "vT":
                    act.wait_ge(S["bias_n"], 1)
                dst, src = item_views(n)
                act.activation(dst, src, ACT.Copy, scale=SCALE if ITEMS[n][0] == "q" else 1.0)\
                   .then_inc(S["proj_cpA"], 1)

            act.wait_ge(S["vg_mm"], 2)
            for pr in range(2):
                copy(vt3[:, :, P * pr:P * (pr + 1)], ps[4 + pr][:, :].rearrange("p (t n) -> p t n", t=NT))\
                    .then_inc(S["vg_cp"], 1)

            def part_copy(n):
                u, b0, b1 = PARTS[n]
                act.wait_ge(S["pT"], n + 1)
                if n >= 2:
                    act.wait_ge(S["pv"], n - 1)
                wid = P * (b1 - b0)
                copy(probsT[:, n % 2, 0:wid], ps[4 + n % 2][:, 0:wid]).then_inc(S["pT_cp"], 1)

            def exponentials(u):
                nk = P * key_blocks(u)
                act.wait_ge(S["nmax"], u + 1)
                act.activation(probs[:, u % 4, 0:nk], probs[:, u % 4, 0:nk], ACT.Exp, bias=nmax[:, u:u + 1],
                               accum_out=psum_e[:, u:u + 1]).then_inc(S["probs"], 1)

            def evacuate(e):
                act.wait_ge(S["pv"], PART_END[2 * e + 1])
                kind, j, t = UNITS[2 * e]
                if kind == "dilated":
                    dst = x_feat[:, j // 2:j // 2 + 5:2, t::4]
                    src = ps[6 + e % 2][:, 0:3 * P].rearrange("p (g i) -> p g i", g=3)
                else:
                    dst = in_tiles(x_feat[:, 6 + j // 2, :], 6)[:, t]
                    src = ps[6 + e % 2][:, 0:P].rearrange("p (r c) -> p r c", c=16)
                copy(dst, src).then_inc(S["evac"], 1)

            for step in range(NU + LAG + 1):
                parts = parts_of(step - LAG) if LAG <= step < NU + LAG else []
                if parts:
                    part_copy(parts[0])
                if step < NU:
                    exponentials(step)
                for n in parts[1:]:
                    part_copy(n)
                done = step - LAG - 1
                if done >= 0 and done % 2 == 1:
                    evacuate(done // 2)

            act.wait_ge(S["preset"], 3)
            link = Chain(act, S["act_chain"])

            def load_table(func):
                link(act.activation(warm[:, :], warm[:, :], func))

            def root(m, ve, std, t):
                m.wait(act, ve, t + 1)
                act.activation(mv[:, t, 3:4], mv[:, t, 2:3], ACT.Sqrt).then_inc(m[std], 1)

            def mixer(l):
                m = L[l]
                for t in range(NT):
                    if t >= 1:
                        features_copy(t - 1, m, "xf_mm", "xf_cp")
                    root(m, "ln_ve", "ln_std", t)
                features_copy(NT - 1, m, "xf_mm", "xf_cp")
                m.wait(act, "logit_mm", NT)
                act.activation(scores_s, ps[5][:, 0:NT * NE], ACT.Sigmoid).then_inc(m["score"], 1)

            def experts(l):
                m = L[l]

                def rows_copy(e, i=None):
                    m.wait(act, "xt_mm", 2 * e + 1, i, 4)
                    if e >= 2:
                        m.wait(act, "gu_mm", 2 * (e - 1), i, 4)
                    copy(xgT[:, e % 2, 0:4, :], ps[2][:, :].rearrange("p (k n) -> p k n", k=4)).then_inc(m["xt_cpA"], 1)

                def silu(e, i=None):
                    m.wait(act, "gu_mm", 2 * e + 1, i, 4)
                    if e >= 1:
                        m.wait(act, "hid", e, i, 2)
                    act.activation(sig, ps[0][:, :], ACT.Silu).then_inc(m["silu"], 1)

                def hidden_copy(e, i=None):
                    m.wait(act, "ht_mm", e + 1, i, 2)
                    if e >= 1:
                        m.wait(act, "dn_mm", 2 * e, i, 4)
                    copy(hidT_hi, ps[4][:, :].rearrange("p (k n) -> p k n", k=KE)).then_inc(m["ht_cp"], 1)
                    c = down_chunk(l, e)
                    filled(act, c, i)
                    if e == 0:
                        m.wait(act, "idx_mm", len(STAGES))
                    for k in range(KE):
                        copy(down_hi[:, k, :], slot(c, KE)[:, k, :]).then_inc(m["dn_hi"], 1)

                def rows_out(e, i=None):
                    m.wait(act, "dn_mm", 2 * e + 1, i, 4)
                    if e >= 2:
                        m.wait(act, f"s_done{e % 2}", 16 * (e // 2), i, 16)
                    copy(y_sb[:, e % 2, 0:512], ps[5][:, :]).then_inc(m["y_cpA"], 1)

                m.wait(act, "xs_st", 16 * NT)
                m.wait(act, "xf_mm", 2 * NT)
                for t in range(NT):
                    act.activation(x_tok[:, t, :], x_tok[:, t, :], ACT.Copy, scale=ALPHA).then_inc(m["x_scaled"], 1)
                rows_copy(0)
                silu(0)
                rows_copy(1)
                hidden_copy(0)
                silu(1)
                rows_copy(2)
                rows_out(0)
                hidden_copy(1)
                silu(2)
                rows_copy(3)
                rows_out(1)
                hidden_copy(2)
                with act.Fori(0, ROUNDS - 1) as i:
                    for e in (3, 4):
                        silu(e, i)
                        rows_copy(e + 1, i)
                        rows_out(e - 1, i)
                        hidden_copy(e, i)
                for e in (13, 14):
                    silu(e)
                    rows_copy(e + 1)
                    rows_out(e - 1)
                    hidden_copy(e)
                silu(15)
                rows_out(14)
                hidden_copy(15)
                rows_out(15)

            def more_tiles(l):
                m = L[l]
                m.wait(act, "nover", 1)
                n = act.value_load(nover_i[0:1, 0:1], min_val=0, max_val=NOVER)
                with act.If(n > 0):
                    with act.Fori(0, n) as j:
                        m.wait(act, "o_mm", 1, j, 3)
                        act.activation(sig, ps[0][:, :], ACT.Silu).then_inc(m["o_silu"], 1)

            def moe_norm(l):
                m = L[l]
                m.wait(act, "y_all", 1)
                for t in range(NT):
                    for k in range(2):
                        act.dma_start(yload[t][:, k, :], Y[l][k * SEQ + t * P:k * SEQ + (t + 1) * P, :])\
                           .then_inc(m[f"y_in{t}"], 16)

                load_table(ACT.Sqrt)

                def features(t):
                    for half in range(2 if t < 2 else 1):
                        m.wait(act, "xf2_mm", 2 * t + half + 1)
                        for k in range(4 * half, 4 * half + 4):
                            ins = act.activation(x_feat[:, k, t * P:(t + 1) * P], ps[6 + half][:, (k % 4) * P:(k % 4 + 1) * P],
                                                 ACT.Identity, scale=lnf[:, 0, k:k + 1], bias=lnf[:, 1, k:k + 1])
                        ins.then_inc(m["xf2_cp"], 1)

                if l == 0:
                    act.wait_ge(S["lnf_in"], 32)
                for t in range(NT):
                    root(m, "ln2_ve", "ln2_std", t)
                    m.wait(act, "ln2_rs", t + 1)
                    act.activation(x_tok[:, t, :], x_tok[:, t, :], ACT.Identity, scale=mv[:, t, 2:3], bias=mv[:, t, 4:5])\
                       .then_inc(m["ln2_z"], 1)
                    if l == 0 and t >= 1:
                        features(t - 1)
                if l == 0:
                    features(NT - 1)
                    load_table(ACT.Sigmoid)

            def conv():
                act.wait_ge(S["cvec_mm"], 1)
                link(copy(cvec[:, 0:40], ps[4][:, 0:40]))
                copy(taps[:, :, 0:NTAP], ps[5][:, 0:256].rearrange("p (c n) -> p c n", c=8)[:, :, 0:NTAP])\
                    .then_inc(S["cvec_cp"], 1)
                act.wait_ge(S["cvec_cp"], 1)

                def diagonals(c):
                    if c >= 2:
                        act.wait_ge(S["side_mm"], c - 1)
                    for j in range(NPE[c]):
                        tap = NTAP - NPE[c] + j
                        ins = act.activation(diag[:, c % 2, j, :], ident[:, :], ACT.Copy, scale=taps[:, c, tap:tap + 1])
                    ins.then_inc(S["diag"], 1)

                for c in range(8):
                    diagonals(c)
                    act.wait_ge(S["pw1_mm"], 2 * c + 2)
                    if c >= 2:
                        act.wait_ge(S["u_ready"], c - 1)
                    act.activation(gsig[:, c % 2, :], ps[2 + c % 2][:, :], ACT.Sigmoid, bias=cvec[:, 8 + c:9 + c])\
                        .then_inc(S["gate_sig"], 1)
                load_table(ACT.Sqrt)
                for c in range(8):
                    act.wait_ge(S["c_dev"], c + 1)
                    if c >= 2:
                        act.wait_ge(S["cvar_mm"], c - 1)
                    act.activation(csq[:, c % 2, :], conv_o[:, c, :], ACT.Square).then_inc(S["c_sq"], 1)
                act.wait_ge(S["c_ve"], 1)
                act.activation(crstd, crstd, ACT.Sqrt).then_inc(S["c_std"], 1)
                for c in range(8):
                    act.wait_ge(S["c_z"], c + 1)
                    act.activation(conv_o[:, c, :], conv_o[:, c, :], ACT.Silu, bias=cvec[:, 32 + c:33 + c],
                                   scale=cvec[:, 24 + c:25 + c]).then_inc(S["c_act"], 1)

            mixer(0)
            experts(0)
            more_tiles(0)
            moe_norm(0)
            conv()
            mixer(1)
            experts(1)
            more_tiles(1)
            moe_norm(1)

        @block.vector
        def _(dve):
            link = Chain(dve, S["dve_chain"])
            tt, ts, stt = dve.tensor_tensor, dve.tensor_scalar, dve.scalar_tensor_tensor

            dve.memset(rel_sb[:, :], 1.0).then_inc(S["preset"], 1)
            dve.memset(rpb_row[0:1, :], 0.0).then_inc(S["preset"], 1)
            dve.memset(ones[:, :], 1.0)
            dve.memset(warm[:, :], 1.0).then_inc(S["preset"], 1)
            for n in range(2 * NT):
                t, half = divmod(n, 2)
                dve.wait_ge(S["xf0_cp"], n + 1)
                cols = slice(t * P, (t + 1) * P)
                tt(x_lo[:, 4 * half:4 * half + 4, cols], ps[n][:, :].rearrange("p (k n) -> p k n", k=4),
                   x_hi[:, 4 * half:4 * half + 4, cols].bitcast(F32), ALU.subtract).then_inc(S["xf0_lo"], 1)

            for n in range(1, NI, 2):
                for j in pieces_at(n):
                    dve.wait_ge(S["w_hi"], j + 1)
                    w, hi, lo = piece(j)
                    tt(lo, w, hi.bitcast(F32), ALU.subtract).then_inc(S["w_lo"], 1)
                if n == 17:
                    dve.wait_ge(S["grid_bias"], 16 * 16)
                    dve.wait_ge(S["row_out"], 48)
                    for h in range(4):
                        ins = dve.tensor_copy(bias_n[:, h].rearrange("p (b r c) -> p b r c", b=3, c=16),
                                              bias_nr[h // 2][:, h % 2].rearrange("p (r b c) -> p b r c", b=3, c=16))
                    ins.then_inc(S["bias_n"], 1)
                dve.wait_ge(S["proj_mm"], n + 1)
                dst, src = item_views(n)
                if ITEMS[n][0] == "q":
                    ins = ts(dst, src, SCALE, None, ALU.mult)
                else:
                    ins = dve.tensor_copy(dst, src)
                ins.then_inc(S["proj_cpV"], 1)
            dve.wait_ge(S["consts"], 48)
            dve.tensor_copy(before_bf[:, :], mats[:, 0, :])
            dve.tensor_copy(slot_bf[:, :], mats[:, 1, :])
            dve.memset(ones_bf[:, :], 1.0)
            dve.wait_ge(S["bias_n"], 1)
            dve.wait_ge(S["biases_in"], 16)
            dve.wait_ge(S["bias_in"], 16)

            def biased(out_, raw, add, col):
                return dve.tensor_tensor_reduce(out_, raw, add, 1.0, -3e38, ALU.add, ALU.max, accum_out=mx[:, col:col + 1])

            def logits(u):
                kind, j, t = UNITS[u]
                bank = 2 * (u % 2)
                lg = probs[:, u % 4, :]
                if u >= 4:
                    dve.wait_ge(S["pT"], PART_END[u - 4])
                dve.wait_ge(S["scores"], u + 1)
                if kind == "dilated":
                    biased(lg[:, 0:512], ps[bank][:, :], bias0[:, j, (NT - 1 - t) * P:(2 * NT - 1 - t) * P], 2 * u)
                    biased(lg[:, 512:768], ps[bank + 1][:, 0:256], bias12[:, j, :], 2 * u + 1).then_inc(S["sc_read"], 1)
                    dve.wait_ge(S["sc_read"], u + 1)
                    dve.reduce_max(nmax[:, u:u + 1], mx[:, 2 * u:2 * u + 2], X_AXIS, negate=True).then_inc(S["nmax"], 1)
                else:
                    b = grid_tiles(t)
                    nk, x0 = P * len(b), b[0] - (t - 1)
                    win = window[:, t, 16 * x0:16 * (x0 + len(b))].rearrange("p (b c) -> p b c", c=16)
                    win = win.unsqueeze(2).broadcast_to([P, len(b), 8, 16])
                    tt(lg[:, 0:nk].rearrange("p (b r c) -> p b r c", r=8, c=16),
                       ps[bank][:, 0:nk].rearrange("p (b r c) -> p b r c", r=8, c=16), win, ALU.add).then_inc(S["sc_read"], 1)
                    dve.wait_ge(S["sc_read"], u + 1)
                    link(biased(lg[:, 0:nk], lg[:, 0:nk], bias_n[:, j, P * x0:P * x0 + nk], 2 * u))
                    ts(nmax[:, u:u + 1], mx[:, 2 * u:2 * u + 1], -1.0, None, ALU.mult).then_inc(S["nmax"], 1)

            def normalize(u):
                nk = P * key_blocks(u)
                dve.wait_ge(S["probs"], u + 1)
                link(dve.reciprocal(rinv[:, u:u + 1], psum_e[:, u:u + 1]))
                ts(probs[:, u % 4, 0:nk], probs[:, u % 4, 0:nk], rinv[:, u:u + 1], None, ALU.mult).then_inc(S["pnorm"], 1)

            for u in range(NU):
                logits(u)
                if u >= 1:
                    normalize(u - 1)
            normalize(NU - 1)

            def moments(t, row, m, ve):
                dve.bn_stats(stats[:, t, 0, :], row[:, 0:512])
                link(dve.bn_stats(stats[:, t, 1, :], row[:, 512:1024]))
                link(dve.bn_aggr(mv[:, t, 0:2], stats[:, t]))
                ts(mv[:, t, 2:3], mv[:, t, 1:2], LN_EPS, None, ALU.add).then_inc(m[ve], 1)

            def norm(t, m, ve, std, done, g=ln_g, b=ln_b):
                row = x_tok[:, t, :]
                moments(t, row, m, ve)
                m.wait(dve, std, t + 1)
                link(dve.reciprocal(mv[:, t, 2:3], mv[:, t, 3:4]))
                link(ts(row, row, mv[:, t, 0:1], mv[:, t, 2:3], ALU.subtract, ALU.mult))
                link(tt(row, row, g, ALU.mult))
                tt(row, row, b, ALU.add).then_inc(m[done], 1)
                m.wait(dve, done, t + 1)

            def mixer(l):
                m = L[l]
                if l == 1:
                    dve.wait_ge(S["xres"], NT)
                else:
                    dve.wait_ge(S["res_in"], 16)
                for t in range(NT):
                    for half in range(2):
                        n = 2 * t + half
                        m.wait(dve, "mo_mm", n + 1)
                        row = x_tok[:, t, 512 * half:512 * (half + 1)]
                        if l == 0:
                            stt(row, x_res[:, t, 512 * half:512 * (half + 1)], ALPHA, ps[n % 4][:, :], ALU.mult, ALU.add).then_inc(m["mo_read"], 1)
                        else:
                            tt(row, ps[n % 4][:, :], row, ALU.add).then_inc(m["mo_read"], 1)
                    m.wait(dve, "mo_read", 2 * t + 2)
                    if t == 0:
                        m.wait(dve, "lnp_in", 32)
                    norm(t, m, "ln_ve", "ln_std", "ln_done", *((ln_g0, ln_b0) if l == 0 else (ln_g, ln_b)))

            def routing(l):
                m = L[l]
                g4 = lambda v: v.rearrange("p (t g i) -> p t g i", t=NT, g=NG)
                pg = lambda v: v.rearrange("p (a i) -> p a i", i=EPG)
                mt = meta.rearrange("p (t e c) -> p t e c", t=NT, e=NE)
                parts = small[:, 36:52].rearrange("p (t c) -> p t c", t=NT)
                link(dve.tensor_copy(mt, parts.unsqueeze(2).broadcast_to([P, NT, NE, 4])))
                m.wait(dve, "score", 1)
                link(tt(t3(sel, NE), t3(scores_s, NE), rb[:, :].unsqueeze(1).broadcast_to([P, NT, NE]), ALU.add))
                a, q = pg(sel), t3(pairsum, 6)
                tt(q[:, :, 0:3], a[:, :, 0:3], a[:, :, 1:4], ALU.add)
                tt(q[:, :, 3:5], a[:, :, 0:2], a[:, :, 2:4], ALU.add)
                link(tt(q[:, :, 5:6], a[:, :, 0:1], a[:, :, 3:4], ALU.add))
                link(dve.reduce_max(gtop, q, X_AXIS))
                link(dve.reduce_max(gmax, t3(gtop, NG), X_AXIS))
                link(tt(t3(geq, NG), t3(gtop, NG), gmax.unsqueeze(2).broadcast_to([P, NT, NG]), ALU.is_equal))
                link(tt(t3(geq, NG), t3(geq, NG), on4(0, NG, NT), ALU.mult))
                link(dve.reduce_max(gmax, t3(geq, NG), X_AXIS))
                link(tt(t3(gone, NG), t3(geq, NG), gmax.unsqueeze(2).broadcast_to([P, NT, NG]), ALU.is_equal))
                by_group = t3(gone, NG).unsqueeze(3).broadcast_to([P, NT, NG, EPG])
                link(tt(g4(selw), g4(sel), by_group, ALU.mult))
                link(dve.reduce_sum(t3(v4, EPG), g4(selw).rearrange("p t g i -> p t i g"), X_AXIS))
                mine = t3(v4, EPG).unsqueeze(3).broadcast_to([P, NT, EPG, EPG])
                other = t3(v4, EPG).unsqueeze(2).broadcast_to([P, NT, EPG, EPG])
                tt(g4(beats), other, mine, ALU.is_gt)
                link(tt(g4(ties), other, mine, ALU.is_equal))
                link(tt(t3(ties, 16), t3(ties, 16), on4(4, 16, NT), ALU.mult))
                link(tt(beats, beats, ties, ALU.add))
                link(dve.reduce_sum(t3(rank, EPG), g4(beats), X_AXIS))
                ts(r0, rank, 0.0, None, ALU.is_equal)
                link(ts(r1, rank, 1.0, None, ALU.is_equal))
                for dst, r in ((m0, r0), (m1, r1)):
                    last = tt(g4(dst), by_group, t3(r, EPG).unsqueeze(2).broadcast_to([P, NT, NG, EPG]), ALU.mult)
                link(last)
                link(tt(msk, m0, m1, ALU.add))
                dve.tensor_copy(msk_bf, msk).then_inc(m["mask"], 1)
                link(ts(mt[:, :, :, 2], t3(m1, NE), float(SEQ), None, ALU.mult))
                m.wait(dve, "pos_mm", 1)
                dve.tensor_copy(cnt, ps[0][:, 64:80])
                link(stt(posm, ps[0][:, 0:64], 1.0, msk, ALU.add, ALU.mult))
                link(dve.tensor_copy(pos_bf, posm))

                slots(l, 0)
                rows_from_slots(l, 0)

            def slots(l, stage):
                e0, e1 = STAGES[stage]
                shape = [P, NT, e1 - e0, P]
                tt(picks[:, :, e0:e1, :], slot_bf[:, :].unsqueeze(1).unsqueeze(1).broadcast_to(shape),
                   t3(pos_bf, NE)[:, :, e0:e1].unsqueeze(3).broadcast_to(shape), ALU.is_equal).then_inc(L[l]["picks"], 1)

            def rows_from_slots(l, part):
                e0, e1 = STAGES[0] if part == 0 else (STAGES[0][1], NE)
                slots_to_rows(link, L[l], "idx_mm", "idx", ps[7][:, 4 * e0:4 * e1], idx_f[:, 4 * e0:4 * e1], e1 - e0,
                              idxg[:, e0:e1], idxs[:, e0:e1], idx_a[:, e0:e1], count=1 if part == 0 else len(STAGES))

            def rest_of_routing(l):
                m = L[l]
                slots(l, 1)
                slots(l, 2)
                link(tt(mtmp, m0, scores_s, ALU.mult))
                link(dve.reduce_sum(g01[:, 0:4], t3(mtmp, NE), X_AXIS))
                link(tt(mtmp, m1, scores_s, ALU.mult))
                link(dve.reduce_sum(g01[:, 4:8], t3(mtmp, NE), X_AXIS))
                link(tt(gden, g01[:, 0:4], g01[:, 4:8], ALU.add))
                link(dve.reciprocal(gden, gden))
                link(tt(g01.rearrange("p (k t) -> p k t", k=2), g01.rearrange("p (k t) -> p k t", k=2),
                        gden.unsqueeze(1).broadcast_to([P, 2, NT]), ALU.mult))
                for j in range(3):
                    last = ts(ind[:, 16 * j:16 * (j + 1)], cnt, float(P * (j + 1)), None, ALU.is_gt)
                link(last)
                link(dve.reduce_sum(nov_f, ind, X_AXIS))
                dve.tensor_copy(nover_i, nov_f).then_inc(m["nover"], 1)
                rows_from_slots(l, 1)

            def slots_to_rows(link, m, mm_sem, done, bank, f, n, rows_in, rows_out, tmp, j=None, count=1):
                m.wait(dve, mm_sem, count, j, 1)
                link(dve.tensor_copy(f, bank[:, 0:4 * n]))
                f4 = t3(f, 4)
                link(ts(tmp, f4[:, :, 3], -4096.0, 4096.0, ALU.mult, ALU.add))
                link(tt(tmp, tmp, f4[:, :, 0], ALU.add))
                link(tt(tmp, tmp, f4[:, :, 1], ALU.add))
                link(dve.tensor_copy(rows_in, tmp))
                tt(rows_out, tmp, f4[:, :, 2], ALU.add).then_inc(m[done], 1)

            def experts(l):
                m = L[l]

                def rows_copy(e, i=None):
                    m.wait(dve, "xt_mm", 2 * e + 2, i, 4)
                    if e >= 2:
                        m.wait(dve, "gu_mm", 2 * (e - 1), i, 4)
                    dve.tensor_copy(xgT[:, e % 2, 4:8, :], ps[3][:, :].rearrange("p (k n) -> p k n", k=4))\
                        .then_inc(m["xt_cpV"], 1)

                def hidden(e, i=None):
                    m.wait(dve, "silu", e + 1, i, 2)
                    m.wait(dve, "gu_mm", 2 * e + 2, i, 4)
                    if e >= 1:
                        m.wait(dve, "ht_mm", e, i, 2)
                    tt(hid, ps[1][:, :], sig, ALU.mult).then_inc(m["hid"], 1)

                def low_parts(e, i=None):
                    m.wait(dve, "ht_cp", e + 1, i, 2)
                    tt(hidT_lo, ps[4][:, :].rearrange("p (k n) -> p k n", k=KE), hidT_hi.bitcast(F32), ALU.subtract)\
                        .then_inc(m["ht_lo"], 1)
                    c = down_chunk(l, e)
                    for k in range(KE):
                        m.wait(dve, "dn_hi", KE * e + k + 1, i, 2 * KE)
                        tt(slot_part(c, KE)[:, k, :], slot(c, KE)[:, k, :], down_hi[:, k, :].bitcast(F32), ALU.subtract).then_inc(m["dn_lo"], 1)

                def rows_out(e, i=None):
                    m.wait(dve, "dn_mm", 2 * e + 2, i, 4)
                    if e >= 2:
                        m.wait(dve, f"s_done{e % 2}", 16 * (e // 2), i, 16)
                    dve.tensor_copy(y_sb[:, e % 2, 512:1024], ps[6][:, :]).then_inc(m["y_cpV"], 1)

                rows_copy(0)
                rest_of_routing(l)
                hidden(0)
                rows_copy(1)
                low_parts(0)
                hidden(1)
                rows_copy(2)
                rows_out(0)
                low_parts(1)
                hidden(2)
                rows_copy(3)
                rows_out(1)
                low_parts(2)
                with dve.Fori(0, ROUNDS - 1) as i:
                    for e in (3, 4):
                        hidden(e, i)
                        rows_copy(e + 1, i)
                        rows_out(e - 1, i)
                        low_parts(e, i)
                for e in (13, 14):
                    hidden(e)
                    rows_copy(e + 1)
                    rows_out(e - 1)
                    low_parts(e)
                hidden(15)
                rows_out(14)
                low_parts(15)
                rows_out(15)

            def more_tiles(l):
                m = L[l]
                n = dve.value_load(nover_i[0:1, 0:1], min_val=0, max_val=NOVER)
                with dve.If(n > 0):
                    m.wait(dve, "s_done0", 16 * 8)
                    m.wait(dve, "gu_mm", 32)
                    m.wait(dve, "y_cpA", NE)
                    ol = Chain(dve, m["o_chain"])
                    ol(ts(cum[:, 0:1], ind[:, 0:1], 0.0, None, ALU.mult))
                    ol(dve.tensor_copy(cum[:, 1:48], ind[:, 0:47]))
                    src, dst = cum, cum2
                    for d in (1, 2, 4, 8, 16, 32):
                        dve.tensor_copy(dst[:, 0:d], src[:, 0:d])
                        ol(tt(dst[:, d:48], src[:, d:48], src[:, 0:48 - d], ALU.add))
                        src, dst = dst, src
                    ol(ts(over, posm, 0.0, None, ALU.mult))
                    for j in range(3):
                        lo, hi = float(P * (j + 1)), float(P * (j + 2))
                        base = src[:, 16 * j:16 * (j + 1)].unsqueeze(1).broadcast_to([P, NT, NE])
                        ol(ts(t3(otmp, NE), base, float(P), -lo, ALU.mult, ALU.add))
                        ol(tt(otmp, otmp, posm, ALU.add))
                        ol(stt(otmp, posm, lo, otmp, ALU.is_gt, ALU.mult))
                        ol(stt(otmp, posm, hi, otmp, ALU.is_le, ALU.mult))
                        ol(tt(over, over, otmp, ALU.add))
                    for a, mk in ((0, m0), (1, m1)):
                        ol(tt(otmp, over, mk, ALU.mult))
                        ol(dve.reduce_sum(ovk[:, 4 * a:4 * a + 4], t3(otmp, NE), X_AXIS))
                    om = ometa.rearrange("p (k t c) -> p k t c", k=2, t=NT)
                    parts = small[:, 36:52].rearrange("p (t c) -> p t c", t=NT)
                    ol(dve.tensor_copy(om, parts.unsqueeze(1).broadcast_to([P, 2, NT, 4])))
                    ol(dve.memset(om[:, 1, :, 2], float(SEQ)))
                    ol(dve.memset(mcur, 0.0))
                    per, first = 12, ol.n
                    with dve.Fori(0, n) as j:
                        ol.n, ol.shift = first, j * per
                        for a in range(2):
                            for t in range(NT):
                                last = ts(over_picks[:, a, t, :], mats[:, 1, :], ovk[:, 4 * a + t:4 * a + t + 1], None,
                                          ALU.is_equal)
                        last.then_inc(m["o_pick"], 1)
                        m.wait(dve, "o_pick", 1, j, 1)
                        ol(ts(ovk, ovk, float(P), None, ALU.subtract))
                        here = otmp[:, 0:48]
                        ol(ts(here, src, mcur, None, ALU.is_equal))
                        ol(tt(here, here, ind, ALU.mult))
                        ol(tt(t3(here, NE), t3(here, NE), on4(20, NE, 3), ALU.mult))
                        ol(dve.reduce_sum(ocmp, here, X_AXIS))
                        ol(dve.tensor_copy(over_e_i, ocmp))
                        ol(ts(mcur, mcur, 1.0, None, ALU.add))
                        slots_to_rows(ol, m, "o_imm", "o_idx", ps[7], idx_f[:, 0:4], 1, curs[:, 4:5], curs[:, 5:6],
                                      idx_a[:, 0:1], j)
                        assert ol.n == first + per
                        m.wait(dve, "o_tr", 1, j, 2)
                        for half in range(2):
                            last = dve.tensor_copy(xgT[:, 0, 4 * half:4 * half + 4, :],
                                                   ps[2 + half][:, :].rearrange("p (k n) -> p k n", k=4))
                        last.then_inc(m["o_cp"], 1)
                        m.wait(dve, "o_silu", 1, j, 1)
                        m.wait(dve, "o_mm", 2, j, 3)
                        tt(hid, ps[1][:, :], sig, ALU.mult).then_inc(m["o_cp"], 1)
                        m.wait(dve, "o_tr", 2, j, 2)
                        dve.tensor_copy(hidT, ps[4][:, :].rearrange("p (k n) -> p k n", k=KE)).then_inc(m["o_cp"], 1)
                        m.wait(dve, "o_mm", 3, j, 3)
                        for half in range(2):
                            last = dve.tensor_copy(y_sb[:, 0, 512 * half:512 * (half + 1)], ps[5 + half][:, :])
                        last.then_inc(m["o_y"], 1)
                        m.wait(dve, "o_scat", 16, j, 16)

            def moe_norm(l):
                m = L[l]

                def scale_and_shift(t):
                    m.wait(dve, "ln2_std", t + 1)
                    link(dve.reciprocal(mv[:, t, 2:3], mv[:, t, 3:4]))
                    stt(mv[:, t, 4:5], mv[:, t, 0:1], -1.0, mv[:, t, 2:3], ALU.mult, ALU.mult).then_inc(m["ln2_rs"], 1)

                for t in range(NT):
                    row = x_tok[:, t, :]
                    m.wait(dve, "x_scaled", t + 1)
                    m.wait(dve, f"y_in{t}", 32)
                    if l == 1 and t == 0:
                        m.wait(dve, "lnp2_in", 32)
                    link(stt(row, yload[t][:, 0, :], g01[:, t:t + 1], row, ALU.mult, ALU.add))
                    if t >= 1:
                        scale_and_shift(t - 1)
                    link(stt(row, yload[t][:, 1, :], g01[:, 4 + t:5 + t], row, ALU.mult, ALU.add))
                    moments(t, row, m, "ln2_ve")
                scale_and_shift(NT - 1)
                if l == 0:
                    dve.wait_ge(S["lnf_in"], 32)
                    for t in (2, 3):
                        m.wait(dve, "xf2_mm", 2 * t + 2)
                        for k in range(4, KD):
                            ins = ts(x_feat[:, k, t * P:(t + 1) * P], ps[7][:, (k - 4) * P:(k - 3) * P], lnf[:, 0, k:k + 1],
                                     lnf[:, 1, k:k + 1], ALU.mult, ALU.add)
                        ins.then_inc(S["xf2_cpV"], 1)
                else:
                    m.wait(dve, "ln2_z", NT)
                    row = x_tok[:, NT - 1, :]
                    link(tt(row, row, ln_g, ALU.mult))
                    tt(row, row, ln_b, ALU.add).then_inc(S["out_last"], 1)

            def conv():
                link(dve.memset(upad, 0.0))
                dve.wait_ge(S["cvec_cp"], 1)

                def gated(c):
                    dve.wait_ge(S["gate_sig"], c + 1)
                    if c >= 3:
                        dve.wait_ge(S["side_mm"], c - 2)
                    stt(upad[:, c % 3, PAD:PAD + SEQ], ps[c % 2][:, :], cvec[:, c:c + 1], gsig[:, c % 2, :],
                        ALU.add, ALU.mult).then_inc(S["u_ready"], 1)

                gated(0)
                n = 0
                for c in range(8):
                    u, sums = upad[:, c % 3, :], (conv_o[:, c, :], odd_taps)
                    dve.wait_ge(S["u_ready"], c + 1)
                    for j in range(NTAP - NPE[c]):
                        if j == 14 and c + 1 < 8:
                            gated(c + 1)
                        if j >= 2:
                            dve.wait_ge(S["tap"], n - 1)
                        if j == 0:
                            ins = ts(sums[0], u[:, 0:SEQ], taps[:, c, 0:1], cvec[:, 16 + c:17 + c], ALU.mult, ALU.add)
                        elif j == 1:
                            if c >= 1:
                                dve.wait_ge(S["conv_done"], c)
                            ins = ts(sums[1], u[:, 1:1 + SEQ], taps[:, c, 1:2], None, ALU.mult)
                        else:
                            ins = stt(sums[j % 2], u[:, j:j + SEQ], taps[:, c, j:j + 1], sums[j % 2], ALU.mult, ALU.add)
                        ins.then_inc(S["tap"], 1)
                        n += 1
                    dve.wait_ge(S["side_mm"], c + 1)
                    dve.wait_ge(S["tap"], n if (NTAP - NPE[c]) % 2 else n - 1)
                    tt(sums[0], ps[6 + c % 2][:, :], sums[0], ALU.add).then_inc(S["tap"], 1)
                    n += 1
                    dve.wait_ge(S["tap"], n)
                    tt(sums[0], sums[0], odd_taps, ALU.add).then_inc(S["conv_done"], 1)
                dve.wait_ge(S["csum_mm"], 1)
                link(ts(cmean, ps[4][:, :], 1.0 / D, None, ALU.mult))
                for c in range(8):
                    tt(conv_o[:, c, :], conv_o[:, c, :], cmean, ALU.subtract).then_inc(S["c_dev"], 1)
                dve.wait_ge(S["cvar_mm"], 8)
                ts(crstd, ps[5][:, :], 1.0 / D, LN_EPS, ALU.mult, ALU.add).then_inc(S["c_ve"], 1)
                dve.wait_ge(S["c_std"], 1)
                link(dve.reciprocal(crstd, crstd))
                for c in range(8):
                    tt(conv_o[:, c, :], conv_o[:, c, :], crstd, ALU.mult).then_inc(S["c_z"], 1)

            mixer(0)
            routing(0)
            experts(0)
            more_tiles(0)
            moe_norm(0)
            conv()
            mixer(1)
            routing(1)
            experts(1)
            more_tiles(1)
            moe_norm(1)

        @block.gpsimd
        def _(pool):
            link = Chain(pool, S["pool_chain"])

            pool.wait_ge(S["preset"], 2)
            rows = rpb_row[0:1, :].rearrange("p (h r x) -> p h r x", h=4, x=RW)[:, :, 0:15, 16:47]
            for h in range(4):
                pool.dma_start(rows[:, h], rpb_2d[:, h]).then_inc(S["rpb_in"], 16)
            pool.wait_ge(S["rpb_in"], 64)
            pool.dma_start(bias_dn.rearrange("c n -> (c n)").rearrange("(o c n) -> o c n", o=1, c=16),
                           rpb_row[0:1, :].unsqueeze(1).broadcast_to([1, 16, 4 * HW])).then_inc(S["rpb_out"], 16)
            pool.wait_ge(S["rpb_out"], 16)
            for r in range(8):
                for a in range(2):
                    src = skewed(bias_dn, (7 - r) * RW + 15 + 2 * a * HW, [[4 * HW - 1, 16], [HW, 2], [1, 8 * NX]])
                    pool.dma_start(bias_nr[a][16 * r:16 * (r + 1)], src).then_inc(S["grid_bias"], 16)
            pool.wait_ge(S["row_rep"], 16)
            src = skewed(bias_rep, P - 1, [[(4 * NB0 + 8) * RELW - 1, P], [RELW, 4 * NB0 + 8], [1, P]])
            pool.dma_start(bias.rearrange("p (b n) -> p b n", n=P), src).then_inc(S["biases_in"], 16)

            def norm_params(g, b, done, to_g=ln_g, to_b=ln_b):
                pool.dma_start(to_g, over_partitions(g)).then_inc(done, 16)
                pool.dma_start(to_b, over_partitions(b)).then_inc(done, 16)

            pool.wait_ge(S["scores"], NU)
            pool.dma_start(x_res, x[0].rearrange("(t p) d -> p t d", p=P)).then_inc(S["res_in"], 16)
            for k, v in enumerate((ln_ffn_g[0], ln_ffn_b[0])):
                pool.dma_start(lnf[:, k, :], v.rearrange("(p k) -> p k", p=P)).then_inc(S["lnf_in"], 16)
            pool.wait_ge(S["sc_read"], NU)
            norm_params(ln_mix_g[0], ln_mix_b[0], L[0]["lnp_in"], ln_g0, ln_b0)

            def moe(l):
                m = L[l]
                for t in range(NT):
                    m.wait(pool, "ln_done", t + 1)
                    pool.dma_start(xs[l][t * P:(t + 1) * P, :], x_tok[:, t, :]).then_inc(m["xs_st"], 16)
                norm_params(ln_ffn_g[l], ln_ffn_b[l], m["lnp2_in"])
                chain = Chain(pool, m["p_chain"])

                def column(tab, e, dst):
                    chain(pool.tensor_copy(dst, tab[:, e:e + 1] if isinstance(e, int) else tab[:, bass.ds(e, 1)]))

                def gather(e, at_e, i=None):
                    par = e % 2
                    if e >= 2:
                        m.wait(pool, "xt_mm", 2 * (e - 1), i, 4)
                        m.wait(pool, f"g_full{par}", 16 * (e // 2), i, 16)
                    column(idxg, at_e, curs[:, par:par + 1])
                    pool.sem_inc(S["passed"], 1)
                    pool.indirect_dma_start(
                        out=xg[:, par, :], out_offset=None, in_=xs[l],
                        in_offset=bass.IndirectOffsetOnAxis(ap=curs[:, par:par + 1], axis=0),
                        bounds_check=SEQ - 1, oob_is_err=False).then_inc(m[f"g_full{par}"], 16)

                def scatter(e, at_e, i=None):
                    par = e % 2
                    if e >= 2:
                        m.wait(pool, f"s_done{par}", 16 * (e // 2), i, 16)
                    column(idxs, at_e, curs[:, 2 + par:3 + par])
                    m.wait(pool, "y_cpA", e + 1, i, 2)
                    m.wait(pool, "y_cpV", e + 1, i, 2)
                    pool.sem_inc(S["passed"], 1)
                    pool.indirect_dma_start(
                        out=Y[l], out_offset=bass.IndirectOffsetOnAxis(ap=curs[:, 2 + par:3 + par], axis=0),
                        in_=y_sb[:, par, :], in_offset=None,
                        bounds_check=2 * SEQ - 1, oob_is_err=False).then_inc(m[f"s_done{par}"], 16)

                chain(pool.memset(xg, 0.0))
                m.wait(pool, "idx", 1)
                m.wait(pool, "xs_st", 16 * NT)
                gather(0, 0)
                gather(1, 1)
                m.wait(pool, "idx", 2)
                for e in (0, 1):
                    gather(e + 2, e + 2)
                    scatter(e, e)
                per, first = 4, chain.n
                with pool.Fori(0, ROUNDS) as i:
                    chain.shift = i * per
                    for e in (2, 3):
                        gather(e + 2, i * 2 + (e + 2), i)
                        scatter(e, i * 2 + e, i)
                    assert chain.n == first + per
                chain.n, chain.shift = first + per * ROUNDS, None
                scatter(14, 14)
                scatter(15, 15)

                n = pool.value_load(nover_i[0:1, 0:1], min_val=0, max_val=NOVER)
                with pool.If(n > 0):
                    with pool.Fori(0, n) as j:
                        m.wait(pool, "o_idx", 1, j, 1)
                        pool.sem_inc(S["passed"], 1)
                        pool.indirect_dma_start(
                            out=xg[:, 0, :], out_offset=None, in_=xs[l],
                            in_offset=bass.IndirectOffsetOnAxis(ap=curs[:, 4:5], axis=0),
                            bounds_check=SEQ - 1, oob_is_err=False).then_inc(m["o_gath"], 16)
                        m.wait(pool, "o_y", 1, j, 1)
                        pool.sem_inc(S["passed"], 1)
                        pool.indirect_dma_start(
                            out=Y[l], out_offset=bass.IndirectOffsetOnAxis(ap=curs[:, 5:6], axis=0),
                            in_=y_sb[:, 0, :], in_offset=None,
                            bounds_check=2 * SEQ - 1, oob_is_err=False).then_inc(m["o_scat"], 16)
                        m.wait(pool, "o_scat", 16, j, 16)
                m.wait(pool, "s_done0", 16 * 8)
                m.wait(pool, "s_done1", 16 * 8)
                pool.sem_inc(m["y_all"], 1)
                if l == 0:
                    pool.dma_start(crow[0:NTAP, :], w_dw[0]).then_inc(S["cvec_in"], 16)
                    at_row = 0
                    for v in (b_pw1, b_dw, conv_ln_g, conv_ln_b):
                        rows = v[0].rearrange("(r n) -> r n", n=P)
                        k = rows.shape[0]
                        pool.dma_start(vrow[at_row:at_row + k, :], rows).then_inc(S["cvec_in"], 16)
                        at_row += k
                if l == 0:
                    pool.dma_start(bpw2, over_partitions(b_pw2[0])).then_inc(S["bpw2_in"], 16)

            moe(0)
            pool.wait_ge(S["bpw2_in"], 16)
            L[0].wait(pool, "lnp2_in", 32)
            link(pool.tensor_scalar(ln_b, ln_b, ALPHA, None, ALU.mult))
            link(pool.tensor_tensor(bpw2, bpw2, ln_b, ALU.add))
            link(pool.tensor_scalar(ln_g, ln_g, ALPHA, None, ALU.mult))
            for t in range(NT):
                L[0].wait(pool, "xf2_mm", 2 * t + 2)
                link(pool.tensor_tensor(x_tok[:, t, :], x_tok[:, t, :], ln_g, ALU.mult))
                pool.tensor_tensor(x_tok[:, t, :], x_tok[:, t, :], bpw2, ALU.add).then_inc(S["xres"], 1)
            pool.wait_ge(S["xres"], NT)
            norm_params(ln_mix_g[1], ln_mix_b[1], L[1]["lnp_in"])
            moe(1)
            L[1].wait(pool, "lnp2_in", 32)
            for t in range(NT - 1):
                L[1].wait(pool, "ln2_z", t + 1)
                link(pool.tensor_tensor(x_tok[:, t, :], x_tok[:, t, :], ln_g, ALU.mult))
                pool.tensor_tensor(x_tok[:, t, :], x_tok[:, t, :], ln_b, ALU.add).then_inc(S["out_ready"], 1)


_INS = ['x', 'w_in_attn', 'w_out_attn', 'rel_bias', 'rpb_2d', 'w_pw1', 'b_pw1', 'w_dw', 'b_dw', 'conv_ln_g',
        'conv_ln_b', 'w_pw2', 'b_pw2', 'ln_mix_g', 'ln_mix_b', 'ln_ffn_g', 'ln_ffn_b', 'w_router', 'router_bias',
        'w_gate', 'w_up', 'w_down']


def kernel(**inputs):
    import numpy as _np
    import concourse.bacc as _bacc
    from concourse import mybir as _mybir
    from concourse.bass_utils import run_bass_kernel_spmd as _run

    nc = _bacc.Bacc("TRN2", target_bir_lowering=False, num_devices=1)
    arrays, args = {}, []
    consts = {"c_bucket": bucket_table(), "c_window": window_mask(), "c_small": small_table(), "c_mats": matrices()}
    for name in _INS + list(consts):
        a = _np.ascontiguousarray(inputs[name] if name in inputs else consts[name])
        arrays[f"in_{name}_dram"] = a
        args.append(nc.dram_tensor(f"in_{name}_dram", a.shape, _mybir.dt.from_np(a.dtype), kind="ExternalInput").ap())
    args.append(nc.dram_tensor("out_0_dram", (1, SEQ, D), _mybir.dt.float32, kind="ExternalOutput").ap())
    trunk(nc, *args)
    r = _run(nc, [arrays], core_ids=[0])
    return r.results[0]["out_0_dram"]
```
